# Optimizing a Trainium2 kernel written in Bass

```python
import math
import jax, jax.numpy as jnp
from jax import lax
import numpy as np

D_MODEL = 2048
BATCH = 1
SEQ = 512
DEPTH = 1

CHUNK = 64
Q_BLOCK = 128
HEAD_DIM = 128
N_HEADS_TOTAL = D_MODEL // HEAD_DIM
N_MEM_HEADS = 4
N_FOX_HEADS = (N_HEADS_TOTAL - N_MEM_HEADS) // 2
N_GDN_HEADS = N_HEADS_TOTAL - N_MEM_HEADS - N_FOX_HEADS
FOX_W = N_FOX_HEADS * HEAD_DIM
GDN_W = N_GDN_HEADS * HEAD_DIM
MEM_W = N_MEM_HEADS * HEAD_DIM
MIX_W = FOX_W + GDN_W + MEM_W
MEM_LEN = 256
CONV_WIDTH = 4
FF_DIM = -(-8 * D_MODEL // (3 * 256)) * 256
NORM_EPS = 1e-6

_SIZES = (FOX_W, FOX_W, FOX_W, N_FOX_HEADS,
          3 * GDN_W, GDN_W, N_GDN_HEADS, N_GDN_HEADS,
          MEM_W)
IN_COLS = sum(_SIZES)
SPLITS = tuple(int(s) for s in np.cumsum(_SIZES)[:-1])

kernel_name = "hymba_fox_gdn_memory_layer"

def rms_norm(x, gain):
    xf = x.astype(jnp.float32)
    y = xf * lax.rsqrt(jnp.mean(xf * xf, axis=-1, keepdims=True) + NORM_EPS)
    return (y * gain.astype(jnp.float32)).astype(x.dtype)

def l2_norm(x):
    return x * lax.rsqrt(jnp.sum(x * x, axis=-1, keepdims=True) + NORM_EPS)

def causal_depthwise_conv(x, w):
    k_w, c = w.shape
    return lax.conv_general_dilated(
        x, w[:, None, :].astype(x.dtype), window_strides=(1,), padding=[(k_w - 1, 0)],
        dimension_numbers=("NWC", "WIO", "NWC"), feature_group_count=c)

def forgetting_attention(q, k, v, log_f):
    b, t, h, d = q.shape
    c = jnp.cumsum(log_f, axis=1).transpose(0, 2, 1)
    scale = d ** -0.5
    outs = []
    for i in range(t // Q_BLOCK):
        q0, q1 = i * Q_BLOCK, (i + 1) * Q_BLOCK
        s = jnp.einsum("bqhd,bkhd->bhqk", q[:, q0:q1], k[:, :q1]).astype(jnp.float32) * scale
        s = s + c[:, :, q0:q1, None] - c[:, :, None, :q1]
        mask = jnp.arange(q1)[None, :] <= (q0 + jnp.arange(Q_BLOCK))[:, None]
        p = jax.nn.softmax(jnp.where(mask, s, -jnp.inf), axis=-1)
        outs.append(jnp.einsum("bhqk,bkhd->bqhd", p.astype(v.dtype), v[:, :q1]))
    return jnp.concatenate(outs, axis=1)

def chunked_gated_delta_rule(q, k, v, g, beta):
    b, t, h, dk = q.shape
    dv = v.shape[-1]
    n = t // CHUNK

    def to_chunks(a):
        return a.reshape(b, n, CHUNK, h, -1).transpose(1, 0, 3, 2, 4)

    q, k, v = to_chunks(q), to_chunks(k), to_chunks(v)
    g = g.reshape(b, n, CHUNK, h).transpose(1, 0, 3, 2)
    beta = beta.reshape(b, n, CHUNK, h).transpose(1, 0, 3, 2)
    gc = jnp.cumsum(g, axis=-1)
    tril = jnp.tril(jnp.ones((CHUNK, CHUNK), bool))
    strict = jnp.tril(jnp.ones((CHUNK, CHUNK), bool), -1)
    decay = jnp.exp(jnp.where(tril, gc[..., :, None] - gc[..., None, :], -jnp.inf))
    kb = k * beta[..., None]
    vb = v * beta[..., None]
    lower = jnp.where(strict, jnp.einsum("nbhcd,nbhed->nbhce", kb, k) * decay, 0.0)
    a_mat = lower + jnp.eye(CHUNK, dtype=lower.dtype)
    rhs = jnp.concatenate([vb, kb * jnp.exp(gc)[..., None]], axis=-1)
    sol = lax.linalg.triangular_solve(a_mat, rhs, left_side=True, lower=True, unit_diagonal=True)
    u, w = sol[..., :dv], sol[..., dv:]
    attn_intra = jnp.where(tril, jnp.einsum("nbhcd,nbhed->nbhce", q, k) * decay, 0.0)
    qg = q * jnp.exp(gc)[..., None]
    g_last = gc[..., -1]
    kdec = k * jnp.exp(g_last[..., None] - gc)[..., None]

    def step(state, inp):
        u_i, w_i, qg_i, at_i, kd_i, gl_i = inp
        v_new = u_i - jnp.einsum("bhcd,bhde->bhce", w_i, state)
        o = jnp.einsum("bhcd,bhde->bhce", qg_i, state) + jnp.einsum("bhcs,bhse->bhce", at_i, v_new)
        state = state * jnp.exp(gl_i)[..., None, None] + jnp.einsum("bhcd,bhce->bhde", kd_i, v_new)
        return state, o

    s0 = jnp.zeros((b, h, dk, dv), jnp.float32)
    _, o = lax.scan(step, s0, (u, w, qg, attn_intra, kdec, g_last))
    return o.transpose(1, 0, 3, 2, 4).reshape(b, t, h, dv)

def gated_deltanet(qkv, z, a, bt, conv_w, a_log, dt_bias, out_gain):
    b, t, _ = qkv.shape
    qkv = jax.nn.silu(causal_depthwise_conv(qkv, conv_w))
    q, k, v = jnp.split(qkv, 3, axis=-1)
    q = l2_norm(q.reshape(b, t, N_GDN_HEADS, HEAD_DIM).astype(jnp.float32)) * (HEAD_DIM ** -0.5)
    k = l2_norm(k.reshape(b, t, N_GDN_HEADS, HEAD_DIM).astype(jnp.float32))
    v = v.reshape(b, t, N_GDN_HEADS, HEAD_DIM).astype(jnp.float32)
    beta = jax.nn.sigmoid(bt.astype(jnp.float32))
    g = -jnp.exp(a_log.astype(jnp.float32)) * jax.nn.softplus(a.astype(jnp.float32) + dt_bias.astype(jnp.float32))
    o = chunked_gated_delta_rule(q, k, v, g, beta)
    o = rms_norm(o, out_gain) * jax.nn.silu(z.reshape(b, t, N_GDN_HEADS, HEAD_DIM).astype(jnp.float32))
    return o.reshape(b, t, GDN_W).astype(qkv.dtype)

def memory_attention(q, k, v):
    s = jnp.einsum("bthd,bmhd->bhtm", q, k).astype(jnp.float32) * (q.shape[-1] ** -0.5)
    p = jax.nn.softmax(s, axis=-1)
    return jnp.einsum("bhtm,bmhd->bthd", p.astype(v.dtype), v)

def setup_inputs(seed: int = 0) -> dict:
    key = jax.random.key(seed)
    ks = jax.random.split(key, 24)
    nrm = lambda k, shape, s: jax.random.normal(k, shape, jnp.float32) * s
    gain = lambda k, shape: 1.0 + 0.02 * jax.random.normal(k, shape, jnp.float32)
    dt = jnp.exp(jax.random.uniform(ks[9], (DEPTH, N_GDN_HEADS), jnp.float32,
                                    minval=math.log(1e-3), maxval=math.log(1e-1)))
    return {
        "x": nrm(ks[0], (BATCH, SEQ, D_MODEL), 1.0),
        "mem": nrm(ks[1], (BATCH, MEM_LEN, D_MODEL), 1.0),
        "norm_mix": gain(ks[2], (DEPTH, D_MODEL)),
        "w_in": nrm(ks[3], (DEPTH, D_MODEL, IN_COLS), D_MODEL ** -0.5),
        "fox_f_bias": 2.0 + 0.1 * jax.random.normal(ks[4], (DEPTH, N_FOX_HEADS), jnp.float32),
        "fox_q_norm": gain(ks[5], (DEPTH, HEAD_DIM)),
        "fox_k_norm": gain(ks[6], (DEPTH, HEAD_DIM)),
        "gdn_conv": nrm(ks[7], (DEPTH, CONV_WIDTH, 3 * GDN_W), CONV_WIDTH ** -0.5),
        "gdn_a_log": jnp.log(jax.random.uniform(ks[8], (DEPTH, N_GDN_HEADS), jnp.float32, minval=1.0, maxval=16.0)),
        "gdn_dt_bias": dt + jnp.log(-jnp.expm1(-dt)),
        "gdn_out_norm": gain(ks[10], (DEPTH, HEAD_DIM)),
        "mem_norm": gain(ks[11], (DEPTH, D_MODEL)),
        "w_mem_kv": nrm(ks[12], (DEPTH, D_MODEL, 2 * MEM_W), D_MODEL ** -0.5),
        "mem_q_norm": gain(ks[13], (DEPTH, HEAD_DIM)),
        "mem_k_norm": gain(ks[14], (DEPTH, HEAD_DIM)),
        "w_out": nrm(ks[15], (DEPTH, MIX_W, D_MODEL), MIX_W ** -0.5),
        "norm_ffn": gain(ks[16], (DEPTH, D_MODEL)),
        "w_gate_up": nrm(ks[17], (DEPTH, D_MODEL, 2 * FF_DIM), D_MODEL ** -0.5),
        "w_down": nrm(ks[18], (DEPTH, FF_DIM, D_MODEL), FF_DIM ** -0.5),
    }

def reference(x, mem, norm_mix, w_in, fox_f_bias, fox_q_norm, fox_k_norm, gdn_conv, gdn_a_log,
              gdn_dt_bias, gdn_out_norm, mem_norm, w_mem_kv, mem_q_norm, mem_k_norm, w_out,
              norm_ffn, w_gate_up, w_down):
    b, t, _ = x.shape
    m = mem.shape[1]
    h = x
    for l in range(DEPTH):
        u = rms_norm(h, norm_mix[l])
        p = u @ w_in[l]
        fq, fk, fv, ff, gqkv, gz, ga, gb, mq = jnp.split(p, SPLITS, axis=-1)

        fq = rms_norm(fq.reshape(b, t, N_FOX_HEADS, HEAD_DIM), fox_q_norm[l])
        fk = rms_norm(fk.reshape(b, t, N_FOX_HEADS, HEAD_DIM), fox_k_norm[l])
        fv = fv.reshape(b, t, N_FOX_HEADS, HEAD_DIM)
        log_f = jax.nn.log_sigmoid(ff.astype(jnp.float32) + fox_f_bias[l].astype(jnp.float32))
        o_fox = forgetting_attention(fq, fk, fv, log_f).reshape(b, t, FOX_W)

        o_gdn = gated_deltanet(gqkv, gz, ga, gb, gdn_conv[l], gdn_a_log[l], gdn_dt_bias[l], gdn_out_norm[l])

        mkv = rms_norm(mem, mem_norm[l]) @ w_mem_kv[l]
        mk, mv = jnp.split(mkv, 2, axis=-1)
        mq = rms_norm(mq.reshape(b, t, N_MEM_HEADS, HEAD_DIM), mem_q_norm[l])
        mk = rms_norm(mk.reshape(b, m, N_MEM_HEADS, HEAD_DIM), mem_k_norm[l])
        mv = mv.reshape(b, m, N_MEM_HEADS, HEAD_DIM)
        o_mem = memory_attention(mq, mk, mv).reshape(b, t, MEM_W)

        mix = jnp.concatenate([o_fox, o_gdn.astype(o_fox.dtype), o_mem], axis=-1)
        h = h + mix @ w_out[l]

        gate, up = jnp.split(rms_norm(h, norm_ffn[l]) @ w_gate_up[l], 2, axis=-1)
        h = h + (jax.nn.silu(gate) * up) @ w_down[l]
    return h


_drawn_inputs = setup_inputs


def setup_inputs(seed=0):
    import zlib

    import numpy as np

    out = dict(_drawn_inputs(seed))
    spreads = {}
    factors = {'norm_mix': 3.78,
     'fox_f_bias': 109.816,
     'fox_q_norm': 8.0,
     'fox_k_norm': 8.0,
     'gdn_out_norm': 6.664,
     'mem_norm': 8.0,
     'mem_q_norm': 8.0,
     'mem_k_norm': 8.0,
     'norm_ffn': 11.683}
    for name, (base, spread) in spreads.items():
        noise = np.random.default_rng([zlib.crc32(name.encode()), seed]).standard_normal(out[name].shape)
        drawn = base * np.exp(spread * noise) if base else spread * noise
        out[name] = __import__('jax').numpy.asarray(drawn.astype(out[name].dtype))
    for name, factor in factors.items():
        out[name] = (out[name] * factor).astype(out[name].dtype)
    return out
```

```python
from contextlib import ExitStack

import numpy as np

import concourse.bass as bass
from concourse import mybir

F32 = mybir.dt.float32
F32R = mybir.dt.float32r
BF16 = mybir.dt.bfloat16
ALU = mybir.AluOpType
ACT = mybir.ActivationFunctionType
AX = mybir.AxisListType

P = 128
D_MODEL = 2048
SEQ = 512
MEM_LEN = 256
HD = 128
CHUNK = 64
N_MEM, N_FOX, N_GDN = 4, 6, 6
FOX_W, GDN_W, MEM_W = N_FOX * HD, N_GDN * HD, N_MEM * HD
FF = 5632
TAPS = 4
EPS = 1e-6
SCALE = HD ** -0.5
KD = D_MODEL // P
TT = SEQ // P
MT = MEM_LEN // P
NCH = SEQ // CHUNK

C_FOX = 0
C_FF = 3 * FOX_W
C_GDN = C_FF + N_FOX
C_Z = C_GDN + 3 * GDN_W
C_GA = C_Z + GDN_W
C_MQ = C_GA + 2 * N_GDN
NG = N_FOX + 2 * N_GDN

MIX_FOX, MIX_GDN, MIX_MEM = 0, N_FOX, N_FOX + N_GDN

GROUPS = [("z", 0), ("z", 1)] + [("mem", h) for h in range(N_MEM)] + \
         [("gdn", h) for h in range(N_GDN)] + [("fox", h) for h in range(N_FOX)]
HEADS = GROUPS[2:]
N_GROUPS = len(GROUPS)
UPG = KD // 2
VPG = 2 * UPG
OUT_UNIT0 = N_GROUPS * UPG
N_CG = D_MODEL // 512
FFN_UNIT0 = OUT_UNIT0 + N_CG * UPG
N_CHUNKS = FF // 512
UPC = 3 * UPG
RAW = 3
SPL = 3
AHEAD = SPL - 1
TURN_V, PV_V = 12, 13
assert UPC % RAW == 0 and UPC % SPL == 0

CONST = {}


def const_array():
    t = np.arange(P)
    half = t // CHUNK
    same = half[:, None] == half[None, :]
    le = t[:, None] <= t[None, :]
    r, c = t[:, None] % CHUNK, np.arange(CHUNK)[None, :]
    parts = {
        "ident": np.eye(P),
        "ones": np.ones((P, P)),
        "cum": same & le,
        "suffix": same & ~le,
        "sel0": np.repeat(half[:, None] == 0, P, 1),
        "sel1": np.repeat(half[:, None] == 1, P, 1),
        "negcum": np.concatenate([-(le.astype(float))] + [-np.ones((P, P))] * (TT - 1), 1),
        "causal": np.where(t[None, :] <= t[:, None], 0.0, -1e30),
        "cum64": r <= c,
        "ident64": r == c,
        "neg64": np.where(r <= c, 0.0, -1e30),
        "eps": np.full((P, 1), EPS),
    }
    for l in range(6):
        s = 1 << l
        parts[f"pair{l}"] = (r // (2 * s) == c // (2 * s)) & (r % (2 * s) < s) & (c % (2 * s) >= s)
    at = 0
    for name, a in parts.items():
        CONST[name] = (at, at + a.shape[1])
        at += a.shape[1]
    return np.concatenate([np.asarray(a, np.float32) for a in parts.values()], 1)


CONST_ARRAY = const_array()
PAR = {}
_at = 0
for _name, _n in (("norm_mix", KD), ("mem_norm", KD), ("norm_ffn", KD), ("conv", 3 * N_GDN * TAPS),
                  ("fox_q", 1), ("fox_k", 1), ("mem_q", 1), ("mem_k", 1), ("gdn_out", 1),
                  ("gate_bias", NG), ("gate_sign", NG), ("a_log", N_GDN), ("gate_w", KD * NG)):
    PAR[_name] = (_at, _at + _n)
    _at += _n
N_PAR = _at


def build(nc, x, mem, w_in, w_mem_kv, w_out, w_gate_up, w_down, const, par, out):
    ctx = ExitStack()
    with ctx:
        at = [17 * 1024]

        def place(name, cols, dt=F32, offset=None):
            if offset is None:
                offset = at[0]
                at[0] += -(-4 * cols // 32) * 32
            return nc.alloc_sbuf_tensor_at(name, [P, cols], dt, offset=offset)

        x_hi = place("x_hi", KD * SEQ, F32R)[:, :].rearrange("p (k t) -> p k t", k=KD)
        x_lo = place("x_lo", KD * SEQ, F32R)[:, :].rearrange("p (k t) -> p k t", k=KD)
        w_raw = place("w_raw", RAW * 1024)
        w_hi = place("w_hi", SPL * 1024, F32R)
        w_lo = place("w_lo", SPL * 1024, F32R)
        mix_at = at[0]
        mix = place("mix", KD * SEQ)[:, :].rearrange("p (k t) -> p k t", k=KD)
        um_hi = place("um_hi", KD * MEM_LEN, F32R, mix_at)[:, :].rearrange("p (k t) -> p k t", k=KD)
        wg_hi = place("wg_hi", KD * NG, F32R, mix_at + 8 * 2048)[:, :].rearrange("p (k c) -> p k c", k=KD)
        wg_lo = place("wg_lo", KD * NG, F32R, mix_at + 9 * 2048)[:, :].rearrange("p (k c) -> p k c", k=KD)
        act_hi = place("act_hi", 4 * SEQ, F32R, mix_at)[:, :].rearrange("p (f t) -> p f t", f=4)
        act_lo = place("act_lo", 4 * SEQ, F32R, mix_at + 8192)[:, :].rearrange("p (f t) -> p f t", f=4)
        silu_gate = place("silu_gate", 4 * SEQ, F32, mix_at + 16384)
        res_at = at[0]
        res_t = place("residual", TT * D_MODEL)
        resid = res_t[:, :].rearrange("p (t c) -> p t c", t=TT)
        um_lo = place("um_lo", KD * MEM_LEN, F32R, res_at)[:, :].rearrange("p (k t) -> p k t", k=KD)
        SCAN = 4 * SEQ + 256
        scan_b = [res_t[:, b * SCAN:(b + 1) * SCAN] for b in range(2)]
        sc_u = [s[:, 0:512].rearrange("p (t d) -> p t d", t=TT) for s in scan_b]
        sc_nw = [s[:, 512:1024] for s in scan_b]
        sc_qg = [s[:, 1024:1536] for s in scan_b]
        sc_kd = [s[:, 1536:2048].rearrange("p (t d) -> p t d", t=TT) for s in scan_b]
        sc_at = [s[:, 2048:2304].rearrange("p (t c) -> p t c", t=TT) for s in scan_b]
        zg = res_t[:, 2 * SCAN:2 * SCAN + N_GDN * SEQ].rearrange("p (h t) -> p h t", h=N_GDN)
        state = res_t[:, 7680:7808]
        v_new = res_t[:, 7808:7936]
        WORK = 1548 + 1536 + 3840 + 768
        work = place("work", WORK)
        cin = work[:, 0:1545].rearrange("p (s c) -> p s c", s=3)
        sq = work[:, 0:1024].rearrange("p (s t) -> p s t", s=2)
        qkv = work[:, 1548:3084].rearrange("p (s t) -> p s t", s=3)
        tmp = work[:, 3084:6924]
        bc = work[:, 6924:7692]
        coup = tmp[:, 0:1280].rearrange("p (l t c) -> p l t c", l=5, t=TT)
        inv = tmp[:, 1280:1792].rearrange("p (w t c) -> p w t c", w=2, t=TT)
        yb = tmp[:, 1792:2048].rearrange("p (t c) -> p t c", t=TT)
        lt = tmp[:, 2048:2304].rearrange("p (t c) -> p t c", t=TT)
        dec = tmp[:, 2304:2816].rearrange("p (w t c) -> p w t c", w=2, t=TT)
        vb = tmp[:, 2816:3328].rearrange("p (t d) -> p t d", t=TT)
        kbg = tmp[:, 3328:3840].rearrange("p (t d) -> p t d", t=TT)
        g_bc = bc[:, 0:512].rearrange("p (t c) -> p t c", t=TT)
        b_bc = bc[:, 512:768].rearrange("p (t c) -> p t c", t=TT)
        pr = tmp[:, 0:1280]
        pt = tmp[:, 1280:2560]
        vtok = tmp[:, 2560:3072].rearrange("p (t d) -> p t d", t=TT)
        ncb = tmp[:, 3072:3584]
        mem_in = work[:, 1548:1548 + 2 * D_MODEL].rearrange("p (t c) -> p t c", t=MT)
        norm_h = mix
        norm_v = norm_h.rearrange("p k t -> p (k t)").rearrange("p (t c) -> p t c", t=TT)

        NC_ = CONST_ARRAY.shape[1]
        cst = place("cst", NC_)
        K = {n: cst[:, a:b] for n, (a, b) in CONST.items()}
        prm = place("prm", N_PAR)
        A = {n: prm[:, a:b] for n, (a, b) in PAR.items()}
        conv_w = A["conv"].rearrange("p (s h j) -> p s h j", s=3, h=N_GDN)
        identb = nc.alloc_sbuf_tensor_at("identb", [P, P], BF16, offset=at[0])
        causalb = nc.alloc_sbuf_tensor_at("causalb", [P, P], BF16, offset=at[0] + 256)
        at[0] += 512
        small_t = place("small", 480)
        small_at = [0]

        def small(n):
            small_at[0] += n
            assert small_at[0] <= 480
            return small_t[:, small_at[0] - n:small_at[0]]

        gz = small(TT * NG).rearrange("p (t c) -> p t c", t=TT)
        ga = small(TT * NG).rearrange("p (t c) -> p t c", t=TT)
        coef = small(NG)
        gsum = small(4 * TT * N_GDN)
        n4 = TT * N_GDN
        ngc = small(n4).rearrange("p (t h) -> p t h", t=TT)
        kdf = small(n4).rearrange("p (t h) -> p t h", t=TT)
        beta = small(n4).rearrange("p (t h) -> p t h", t=TT)
        beg = small(n4).rearrange("p (t h) -> p t h", t=TT)
        egl = small(2 * n4).rearrange("p (j t h) -> p j t h", j=2, t=TT)
        ssx = small(4)
        rx = small(4)
        ssm = small(2)
        rm = small(2)
        mx = small(4)
        nmx = small(4)
        rsum = small(4)
        rrec = small(4)
        oss = small(4)
        orn = small(4)
        ss2 = small(TT * N_CG).rearrange("p (t g) -> p t g", t=TT)
        ss2s = small(4)
        r2 = small(4)
        comb = small(2)
        scratch = mix.rearrange("p k t -> p (k t)")[:, 10 * SEQ:10 * SEQ + D_MODEL]
        assert at[0] <= 224 * 1024
        psum = ctx.enter_context(nc.psum_tensor("psum", [P, 8 * 512], F32))
        bank = [psum[:, 512 * b:512 * b + 512] for b in range(8)]
        set_a, set_b = psum[:, 0:2048], psum[:, 2048:4096]
        S1, S2, T = bank[3], bank[7], bank[4:7]

        sems = {}

        def sem(name):
            if name not in sems:
                sems[name] = ctx.enter_context(nc.semaphore(name))
            return sems[name]

        raw_ready = [sem(f"raw_ready{i}") for i in range(RAW)]
        hi_done, lo_done, unit_done = sem("hi_done"), sem("lo_done"), sem("unit_done")
        group_sums = sem("group_sums")
        bank_taken = [sem(f"bank{s}_taken") for s in range(3)]

        w_in3 = {"gdn": w_in[:, C_GDN:C_GDN + 3 * GDN_W].rearrange("(k p) (s h c) -> p k s h c", p=P, s=3, h=N_GDN),
                 "fox": w_in[:, C_FOX:C_FOX + 3 * FOX_W].rearrange("(k p) (s h c) -> p k s h c", p=P, s=3, h=N_FOX)}
        w_in2 = w_in.rearrange("(k p) c -> p k c", p=P)
        w_kv = w_mem_kv.rearrange("(k p) (s h c) -> p k s h c", p=P, s=2, h=N_MEM)
        w_out_v = w_out.rearrange("(k p) c -> p k c", p=P)
        w_gu_v = w_gate_up.rearrange("(k p) c -> p k c", p=P)
        w_dn_v = w_down.rearrange("(f k p) c -> f p k c", p=P, k=2)
        MIX_ORDER = [6, 7, 8, 9, 10, 11, 12, 13, 14, 15, 0, 1, 2, 3, 4, 5]

        def raw_loads(u):
            s = w_raw[:, (u % RAW) * 1024:(u % RAW) * 1024 + 1024]
            if u >= OUT_UNIT0:
                cg, kk = divmod(u - OUT_UNIT0, UPG)
                k0 = MIX_ORDER[2 * kk]
                return [(s.rearrange("p (k c) -> p k c", k=2), w_out_v[:, k0:k0 + 2, 512 * cg:512 * cg + 512])]
            g, kk = divmod(u, UPG)
            kind, h = GROUPS[g]
            ks = slice(2 * kk, 2 * kk + 2)
            s = s[:, 0:768].rearrange("p (k s c) -> p k s c", k=2, s=3)
            if kind == "z":
                return [(s.rearrange("p k s c -> p k (s c)"), w_in2[:, ks, C_Z + 384 * h:C_Z + 384 * h + 384])]
            if kind == "mem":
                return [(s[:, :, 0, :], w_in2[:, ks, C_MQ + HD * h:C_MQ + HD * h + HD])] + \
                       [(s[:, k, 1:3, :], w_kv[:, 2 * kk + k, :, h, :]) for k in range(2)]
            return [(s[:, k, :, :], w_in3[kind][:, 2 * kk + k, :, h, :]) for k in range(2)]

        resid_added = sem("resid_added")
        LOOP_J = 2 * UPG

        def ffn_slot(jj, n):
            return (FFN_UNIT0 + jj) % n

        raw_count = [0] * RAW
        raw_at = []
        for u in range(FFN_UNIT0):
            raw_count[u % RAW] += 16 * len(raw_loads(u))
            raw_at.append(raw_count[u % RAW])

        def ffn_raw_at(jj):
            s = ffn_slot(jj, RAW)
            return raw_count[s] + 16 * sum(ffn_slot(i, RAW) == s for i in range(jj + 1))

        def unit_cols(u):
            return 768 if u < OUT_UNIT0 else 1024

        def head_visit(t):
            out_ = []
            for n, (kind, h) in enumerate(HEADS):
                v = t - VPG * (n + 3)
                last = {"mem": 16, "fox": 16, "gdn": 53}[kind]
                if 0 <= v < last:
                    out_.append((n, kind, h, v))
            return out_

        LAST_VISIT = VPG * N_GROUPS + 16

        def banks_taken(eng, groups):
            for s in range(3):
                eng.wait_ge(bank_taken[s], groups)

        def qkv_free(eng, n):
            if n == 0:
                return
            kind, h = HEADS[n - 1]
            if kind == "gdn":
                eng.wait_ge(sem("tok_ready"), n)
                eng.wait_ge(sem("qg_ready"), h + 1)
            else:
                eng.wait_ge(sem(kind + "_scores"), (2 if kind == "mem" else 3) * (h + 1))

        def bcl(ap, n):
            return ap.unsqueeze(2).to_broadcast([ap.shape[0], ap.shape[1], n])

        block = ctx.enter_context(nc.Block())

        @block.sync
        def _(sp):
            x_v = x.rearrange("(t p) c -> p t c", p=P)
            for t in range(TT):
                sp.dma_start(resid[:, t, :], x_v[:, t, :]).then_inc(sem(f"x_in{t}"), 16)
            for u in range(FFN_UNIT0):
                if u >= RAW:
                    sp.wait_ge(lo_done, u - RAW + 1)
                for dst, src in raw_loads(u):
                    sp.dma_start(dst, src).then_inc(raw_ready[u % RAW], 16)

            def load(base, jj, src):
                slot = ffn_slot(jj, RAW)
                sp.wait_ge(lo_done, base - RAW + 1)
                s = w_raw[:, slot * 1024:slot * 1024 + 1024].rearrange("p (k c) -> p k c", k=2)
                sp.dma_start(s, src).then_inc(raw_ready[slot], 16)

            def gate_up(u0, jj, c, up):
                for kk in range(UPG):
                    load(u0 + kk, jj + kk, w_gu_v[:, 2 * kk:2 * kk + 2, bass.ds(c * 512 + (FF if up else 0), 512)])

            def down(u0, jj, c):
                for j in range(2 * N_CG):
                    cg, kk = divmod(j, 2)
                    load(u0 + j, jj + j, w_dn_v[bass.ds(c * 2 + kk, 1), :, :, 512 * cg:512 * cg + 512]
                         .rearrange("f p k c -> (f p) k c"))

            gate_up(FFN_UNIT0, 0, 0, False)
            gate_up(FFN_UNIT0 + UPG, UPG, 0, True)
            with sp.Fori(1, N_CHUNKS) as c:
                u0 = FFN_UNIT0 + c * UPC - UPG
                gate_up(u0, LOOP_J, c, False)
                down(u0 + UPG, LOOP_J + UPG, c - 1)
                gate_up(u0 + 2 * UPG, LOOP_J + 2 * UPG, c, True)
            down(FFN_UNIT0 + N_CHUNKS * UPC - UPG, LOOP_J, N_CHUNKS - 1)
            out_v = out.rearrange("(t p) c -> p t c", p=P)
            for cg in range(N_CG):
                sp.wait_ge(resid_added, N_CG * N_CHUNKS + cg + 1)
                sp.dma_start(out_v[:, :, 512 * cg:512 * cg + 512],
                             resid[:, :, 512 * cg:512 * cg + 512]).then_inc(sem("out_done"), 16)
            sp.wait_ge(sem("out_done"), 16 * N_CG)

        @block.tensor
        def _(pe):
            mm = nc.tensor.matmul

            def mm3(dst, ahi, alo, bhi, blo, first, last):
                mm(dst, ahi, bhi, start=first, stop=False)
                mm(dst, ahi, blo, start=False, stop=False)
                return mm(dst, alo, bhi, start=False, stop=last)

            def w_tiles(slot, a, b):
                return w_hi[:, slot * 1024 + a:slot * 1024 + b], w_lo[:, slot * 1024 + a:slot * 1024 + b]

            def x_transpose(k):
                if k >= 5:
                    pe.wait_ge(sem("x_split"), k - 4)
                for t in range(TT):
                    last = nc.tensor.transpose(bank[3 + k % 5][:, t * P:t * P + P],
                                               resid[:, t, k * P:k * P + P], K["ident"])
                last.then_inc(sem("x_turned"), 1)

            def mem_transpose(j):
                if j < 5:
                    pe.wait_ge(sem("x_split"), KD)
                else:
                    pe.wait_ge(sem("mem_split"), 2 * (j - 4))
                for i in range(2):
                    for t in range(MT):
                        k = 2 * j + i
                        last = nc.tensor.transpose(bank[3 + j % 5][:, i * 256 + t * P:i * 256 + t * P + P],
                                                   mem_in[:, t, k * P:k * P + P], K["ident"])
                last.then_inc(sem("mem_turned"), 1)

            def gates():
                pe.wait_ge(sem("gate_w_split"), 1)
                pe.wait_ge(sem("mem_split"), KD)
                for t in range(TT):
                    for k in range(KD):
                        last = mm3(bank[3][:, t * NG:t * NG + NG], x_hi[:, k, t * P:t * P + P],
                                   x_lo[:, k, t * P:t * P + P], wg_hi[:, k, :], wg_lo[:, k, :], k == 0, k == KD - 1)
                last.then_inc(sem("gates_ready"), 1)

            def gate_sums():
                pe.wait_ge(sem("gate_logs"), 1)
                g = ga[:, :, N_FOX:N_FOX + N_GDN]
                for i, name in enumerate(("cum", "suffix", "sel0", "sel1")):
                    last = mm(bank[4][:, i * n4:i * n4 + n4].rearrange("p (t h) -> p t h", t=TT), K[name], g,
                              start=True, stop=True)
                last.then_inc(sem("gate_sums"), 1)

            def unit_half(u, half):
                g, kk = divmod(u, UPG)
                slot = u % SPL
                k = 2 * kk + half
                if half == 0:
                    pe.wait_ge(lo_done, u + 1)
                if u >= OUT_UNIT0:
                    cg, kk = divmod(u - OUT_UNIT0, UPG)
                    k = MIX_ORDER[2 * kk + half]
                    pe.wait_ge(sem("mix_split"), 2 * kk + half + 1)
                    if kk == 0 and half == 0:
                        if cg == 0:
                            banks_taken(pe, N_GROUPS)
                            pe.wait_ge(sem("gdn_mixed"), N_GDN)
                        elif cg == 1:
                            pe.wait_ge(sem("fox_mixed"), N_FOX)
                        else:
                            pe.wait_ge(resid_added, cg - 1)
                    hi, lo = w_tiles(slot, half * 512, half * 512 + 512)
                    for t in range(TT):
                        last = mm3(bank[4 * (cg % 2) + t], x_hi[:, k, t * P:t * P + P], x_lo[:, k, t * P:t * P + P],
                                   hi, lo, kk == 0 and half == 0, kk == UPG - 1 and half == 1)
                    if half == 1:
                        last.then_inc(unit_done, 1)
                    return
                kind, h = GROUPS[g]
                for s, i in ((0, 0), (0, 1), (1, 0)) if half == 0 else ((1, 1), (2, 0), (2, 1)):
                    k = 2 * kk + i
                    if kk == 0 and i == 0 and g > 0:
                        pe.wait_ge(bank_taken[s], g)
                    if g == 0 and s == 0:
                        pe.wait_ge(sem("x_split"), k + 1)
                    hi, lo = w_tiles(slot, i * 384 + s * P, i * 384 + s * P + P)
                    bhi, blo, dst = x_hi[:, k, :], x_lo[:, k, :], bank[s]
                    if kind == "mem" and s > 0:
                        bhi, blo, dst = um_hi[:, k, :], um_lo[:, k, :], bank[s][:, 0:MEM_LEN]
                    last = mm3(dst, hi, lo, bhi, blo, k == 0, k == KD - 1)
                    if k == KD - 1 and s < 2:
                        last.then_inc(group_sums, 1)
                if half == 1:
                    last.then_inc(unit_done, 1)

            def halves():
                for i in range(TT):
                    for a in range(2):
                        yield i, slice(64 * a, 64 * a + 64)

            def banks_free(n):
                if n == 0:
                    pe.wait_ge(sem("gate_sums_read"), 1)
                elif HEADS[n - 1][0] == "gdn":
                    pe.wait_ge(sem("uw_taken"), 2 * (HEADS[n - 1][1] + 1))
                else:
                    pe.wait_ge(sem(HEADS[n - 1][0] + "_mixed"), HEADS[n - 1][1] + 1)

            def norms(n, kind):
                pe.wait_ge(sem("sq_ready"), n + 1)
                mm(T[0], K["ones"], sq[:, 0, :], start=True, stop=True)
                nk = MEM_LEN if kind == "mem" else SEQ
                mm(T[1][:, 0:nk], K["ones"], sq[:, 1, 0:nk], start=True, stop=True).then_inc(sem("ssq_ready"), 1)

            def mem_side(n, h, v):
                if v == 5:
                    banks_free(n)
                    norms(n, "mem")
                if v == 7:
                    for t in range(MT):
                        last = nc.tensor.transpose(T[2][:, t * P:t * P + P], qkv[:, 2, t * P:t * P + P], K["ident"])
                    last.then_inc(sem("tok_ready"), 1)
                if v in (8, 9):
                    if v == 8:
                        pe.wait_ge(sem("qn_ready"), n + 1)
                        pe.wait_ge(sem("kn_ready"), n + 1)
                    j0 = 2 * (v - 8)
                    for j in (j0, j0 + 1):
                        last = mm(T[v - 8][:, (j - j0) * 256:(j - j0) * 256 + 256], qkv[:, 0, j * P:j * P + P],
                                  qkv[:, 1, 0:MEM_LEN], start=True, stop=True)
                    last.then_inc(sem("mem_scores"), 1)
                if v == TURN_V:
                    pe.wait_ge(sem("mem_probs"), h + 1)
                    for i in range(MT):
                        for j in range(TT):
                            last = nc.tensor.transpose(T[i][:, j * P:j * P + P], pr[:, j * 256 + i * P:j * 256 + i * P + P],
                                                       K["ident"])
                        last.then_inc(sem("mem_turned_p"), 1)
                if v == PV_V:
                    pe.wait_ge(sem("mem_pt0"), h + 1)
                    pe.wait_ge(sem("mem_pt1"), h + 1)
                    pe.wait_ge(sem("vtok_ready"), h + 1)
                    for i in range(MT):
                        last = mm(T[2], vtok[:, i, :], pt[:, i * 512:i * 512 + 512], start=(i == 0), stop=(i == MT - 1))
                    last.then_inc(sem("mem_pv"), 1)

            def fox_side(n, h, v):
                if v == 5:
                    banks_free(n)
                    if h <= 2:
                        pe.wait_ge(sem("gdn_mixed"), h + 4)
                    pe.wait_ge(sem("bc_ready"), 2 * N_GDN + h + 1)
                    for i in range(TT):
                        last = mm(T[2][:, i * P:], g_bc[:, i, :], K["negcum"][:, 0:SEQ - i * P], start=(i == 0),
                                  stop=(i == TT - 1))
                    last.then_inc(sem("negc_ready"), 1)
                    norms(n, "fox")
                if v == 7:
                    pe.wait_ge(sem("ncb_ready"), h + 1)
                    for t in range(TT):
                        last = nc.tensor.transpose(T[2][:, t * P:t * P + P], qkv[:, 2, t * P:t * P + P], K["ident"])
                    last.then_inc(sem("tok_ready"), 1)
                if v in (8, 9, 10):
                    if v == 8:
                        pe.wait_ge(sem("qn_ready"), n + 1)
                        pe.wait_ge(sem("kn_ready"), n + 1)
                        pe.wait_ge(sem("bf_consts"), 2)
                    if v == 10:
                        pe.wait_ge(sem("vtok_ready"), N_MEM + h + 1)
                    for j, b, c0 in {8: ((0, 0, 0), (1, 0, 128)), 9: ((2, 1, 0),), 10: ((3, 2, 0),)}[v]:
                        w = (j + 1) * P
                        mm(T[b][:, c0:c0 + w], qkv[:, 0, j * P:j * P + P], qkv[:, 1, 0:w], start=True, stop=False)
                        last = mm(T[b][:, c0 + j * P:c0 + w], identb[:, :], causalb[:, :], start=False, stop=True)
                    last.then_inc(sem("fox_scores"), 1)
                if v == TURN_V:
                    pe.wait_ge(sem("fox_probs"), h + 1)
                    off = [0, 128, 384, 768]
                    for b, blocks in ((0, ((0, 0),)), (1, ((1, 0),)), (2, ((2, 0), (3, 256)))):
                        for i, c0 in blocks:
                            for j in range(i, TT):
                                last = nc.tensor.transpose(T[b][:, c0 + (j - i) * P:c0 + (j - i + 1) * P],
                                                           pr[:, off[j] + i * P:off[j] + i * P + P], K["ident"])
                        last.then_inc(sem(f"fox_turned{b}"), 1)
                if v == PV_V:
                    pe.wait_ge(sem("fox_pt0"), h + 1)
                    pe.wait_ge(sem("fox_pt1"), h + 1)
                    pe.wait_ge(sem("fox_pt2"), h + 1)
                    offp = [0, 512, 896, 1152]
                    for i in range(TT):
                        last = mm(T[2][:, i * P:], vtok[:, i, :], pt[:, offp[i]:offp[i] + SEQ - i * P],
                                  start=(i == 0), stop=(i == TT - 1))
                    last.then_inc(sem("fox_pv"), 1)

            def gdn_side(n, h, v):
                b = h % 2
                if v == 5:
                    banks_free(n)
                    if h >= 3:
                        pe.wait_ge(sem("gdn_mixed"), h - 2)
                    pe.wait_ge(sem("bc_ready"), 2 * h + 2)
                    for i, s in halves():
                        mm(T[2][s, i * 64:i * 64 + 64], g_bc[s, i, 0:64], K["cum64"][s, :], start=True, stop=True)
                        c = 256 + i * 64
                        mm(T[2][s, c:c + 64], g_bc[s, i, 0:64], K["cum64"][s, :], start=True, stop=False)
                        last = mm(T[2][s, c:c + 64], b_bc[s, i, :], K["ident64"][s, :], start=False, stop=True)
                    last.then_inc(sem("decay_rows"), 1)
                    norms(n, "gdn")
                if v == 6:
                    pe.wait_ge(sem("dec_arg"), h + 1)
                    for i in range(TT):
                        last = mm(T[2][:, i * P:i * P + P], g_bc[:, i, :], K["cum"], start=True, stop=True)
                    last.then_inc(sem("gc_rows"), 1)
                if v == 7:
                    pe.wait_ge(sem("qn_ready"), n + 1)
                    pe.wait_ge(sem("kn_ready"), n + 1)
                    for i, s in halves():
                        c = i * P + s.start
                        mm(T[0][s, i * 64:i * 64 + 64], qkv[:, 1, c:c + 64], qkv[:, 1, c:c + 64], start=True, stop=True)
                        last = mm(T[0][s, 256 + i * 64:320 + i * 64], qkv[:, 1, c:c + 64], qkv[:, 0, c:c + 64],
                                  start=True, stop=True)
                    last.then_inc(sem("gram_ready"), 1)
                    for i in range(TT):
                        last = nc.tensor.transpose(T[1][:, i * P:i * P + P], qkv[:, 1, i * P:i * P + P], K["ident"])
                    last.then_inc(sem("ktok_ready"), 1)
                    pe.wait_ge(sem("qg_exp"), h + 1)
                    for i in range(TT):
                        last = nc.tensor.transpose(T[2][:, i * P:i * P + P], qkv[:, 2, i * P:i * P + P], K["ident"])
                    last.then_inc(sem("tok_ready"), 1)
                if v == 8:
                    pe.wait_ge(sem("inv0_ready"), h + 1)
                    for i, s in halves():
                        last = mm(T[0][s, i * 64:i * 64 + 64], inv[s, 1, i, :], K["ident64"][s, :], start=True, stop=True)
                    last.then_inc(sem("inv0_turned"), 1)
                for l in range(1, 6):
                    if v == 7 + 2 * l:
                        pe.wait_ge(sem("coup_ready"), 5 * h + l)
                        if l == 1:
                            pe.wait_ge(sem("inv0_copied"), h + 1)
                            pe.wait_ge(sem("k_scaled"), h + 1)
                        else:
                            pe.wait_ge(sem("inv_updated"), 5 * h + l - 1)
                        for i, s in halves():
                            last = mm(T[1][s, i * 64:i * 64 + 64], coup[s, l - 1, i, :], inv[s, 0, i, :],
                                      start=True, stop=True)
                        last.then_inc(sem("y_ready"), 1)
                    if v == 8 + 2 * l:
                        pe.wait_ge(sem("y_copied"), 5 * h + l)
                        for i, s in halves():
                            if l < 5:
                                mm(T[0][s, i * 64:i * 64 + 64], inv[s, 1, i, :], yb[s, i, :], start=True, stop=True)
                            last = mm(T[0][s, 256 + i * 64:320 + i * 64], yb[s, i, :], inv[s, 1, i, :],
                                      start=True, stop=True)
                        last.then_inc(sem("xy_ready"), 1)
                if v == 19:
                    pe.wait_ge(sem("inv_updated"), 5 * h + 5)
                    pe.wait_ge(sem("v_scaled"), h + 1)
                    for i, s in halves():
                        last = mm(T[1][s, i * P:i * P + P], inv[s, 1, i, :], vb[s, i, :], start=True, stop=True)
                    last.then_inc(sem("u_ready"), 1)
                    for i, s in halves():
                        last = mm(T[2 - s.start // 32][:, i * 64:i * 64 + 64], kbg[s, i, :], inv[s, 1, i, :],
                                  start=True, stop=True)
                    last.then_inc(sem("w_ready"), 1)
                if 21 <= v < 21 + 2 * NCH:
                    c, second = divmod(v - 21, 2)
                    i, s = c // 2, slice(64 * (c % 2), 64 * (c % 2) + 64)
                    cols = slice(64 * c, 64 * c + 64)
                    if not second:
                        if c == 0:
                            pe.wait_ge(sem("uw_taken"), 2 * h + 2)
                            pe.wait_ge(sem("state_clear"), h + 1)
                        else:
                            pe.wait_ge(sem("state_new"), (NCH - 1) * h + c)
                        mm(S1[s, 0:P], sc_nw[b][:, cols], state, start=True, stop=True).then_inc(sem("ws_ready"), 1)
                    else:
                        pe.wait_ge(sem("v_new"), NCH * h + c + 1)
                        if c == 0:
                            pe.wait_ge(sem("qg_ready"), h + 1)
                            if h > 0:
                                pe.wait_ge(sem("o_scaled"), h)
                        mm(S2[s, i * P:i * P + P], sc_qg[b][:, cols], state, start=True, stop=False)
                        mm(S2[s, i * P:i * P + P], sc_at[b][s, i, :], v_new[s, :], start=False, stop=True)
                        mm(S1[:, P:2 * P], sc_kd[b][s, i, :], v_new[s, :], start=True, stop=True) \
                            .then_inc(sem("ds_ready"), 1)
                if v == 52:
                    pe.wait_ge(sem("o_scaled"), h + 1)
                    if h + 2 < N_GDN:
                        pe.wait_ge(sem("uw_taken"), 2 * (h + 3))
                    k = MIX_GDN + h
                    for i in range(TT):
                        last = nc.tensor.transpose(T[0][:, i * P:i * P + P], mix[:, k, i * P:i * P + P], K["ident"])
                    last.then_inc(sem("o_turned"), 1)

            pe.wait_ge(sem("const_in"), 16)
            pe.wait_ge(sem("x_normed"), TT)
            for k in range(4):
                x_transpose(k)
            for t in range(LAST_VISIT):
                u, half = divmod(t, 2)
                if u < UPG and half == 0:
                    for k in (2 * u + 4, 2 * u + 5):
                        if k < KD:
                            x_transpose(k)
                unit_half(u, half)
                if t == VPG:
                    pe.wait_ge(sem("mem_normed"), MT)
                if VPG <= t < VPG + KD // 2:
                    mem_transpose(t - VPG)
                if t == VPG + 10:
                    gates()
                if t == VPG + 15:
                    gate_sums()
                for n, kind, h, v in head_visit(t):
                    {"mem": mem_side, "gdn": gdn_side, "fox": fox_side}[kind](n, h, v)
            for t in range(LAST_VISIT, 2 * FFN_UNIT0):
                unit_half(t // 2, t % 2)

            pe.wait_ge(sem("h_normed"), TT)
            pe.wait_ge(resid_added, N_CG)

            def h_transpose(k):
                if k >= 4:
                    pe.wait_ge(sem("h_split"), k - 3)
                for t in range(TT):
                    last = nc.tensor.transpose(bank[4 + k % 4][:, t * P:t * P + P], norm_v[:, t, k * P:k * P + P],
                                               K["ident"])
                last.then_inc(sem("h_turned"), 1)

            def gate_up(u0, jj, side, peeled=False):
                for kk in range(UPG):
                    if peeled:
                        for k in (2 * kk + 4, 2 * kk + 5):
                            if k < KD:
                                h_transpose(k)
                    pe.wait_ge(lo_done, u0 + kk + 1)
                    for half in range(2):
                        k = 2 * kk + half
                        if peeled:
                            pe.wait_ge(sem("h_split"), k + 1)
                        for s in range(4):
                            hi, lo = w_tiles(ffn_slot(jj + kk, SPL), half * 512 + s * P, half * 512 + s * P + P)
                            last = mm3(bank[4 * side + s], hi, lo, x_hi[:, k, :], x_lo[:, k, :], k == 0, k == KD - 1)
                    last.then_inc(unit_done, 1)

            def down(u0, jj, side):
                for kk in range(2):
                    pe.wait_ge(lo_done, u0 + kk + 1)
                    slot = ffn_slot(jj + kk, SPL)
                    for half in range(2):
                        f = 2 * kk + half
                        hi, lo = w_tiles(slot, half * 512, half * 512 + 512)
                        for t in range(TT):
                            last = mm3(bank[4 * side + t], act_hi[:, f, t * P:t * P + P], act_lo[:, f, t * P:t * P + P],
                                       hi, lo, f == 0, f == 3)
                    last.then_inc(unit_done, 1)

            for k in range(4):
                h_transpose(k)
            gate_up(FFN_UNIT0, 0, 0, peeled=True)
            gate_up(FFN_UNIT0 + UPG, UPG, 1)
            with pe.Fori(1, N_CHUNKS) as c:
                u0 = FFN_UNIT0 + c * UPC - UPG
                added = c * N_CG
                pe.wait_ge(resid_added, added)
                pe.wait_ge(sem("gate_taken"), c)
                gate_up(u0, LOOP_J, 0)
                pe.wait_ge(sem("act_ready"), c)
                down(u0 + UPG, LOOP_J + UPG, 1)
                pe.wait_ge(sem("gate_taken"), c + 1)
                down(u0 + UPG + 2, LOOP_J + UPG + 2, 0)
                pe.wait_ge(resid_added, added + 1)
                down(u0 + UPG + 4, LOOP_J + UPG + 4, 1)
                pe.wait_ge(resid_added, added + 2)
                down(u0 + UPG + 6, LOOP_J + UPG + 6, 0)
                pe.wait_ge(resid_added, added + 3)
                gate_up(u0 + 2 * UPG, LOOP_J + 2 * UPG, 1)
            u0 = FFN_UNIT0 + N_CHUNKS * UPC - UPG
            added = N_CHUNKS * N_CG
            pe.wait_ge(resid_added, added)
            pe.wait_ge(sem("act_ready"), N_CHUNKS)
            down(u0, LOOP_J, 0)
            down(u0 + 2, LOOP_J + 2, 1)
            pe.wait_ge(resid_added, added + 1)
            down(u0 + 4, LOOP_J + 4, 0)
            pe.wait_ge(resid_added, added + 2)
            down(u0 + 6, LOOP_J + 6, 1)

        @block.scalar
        def _(act):
            fn = nc.scalar.activation

            act.dma_start(cst[:, :], const).then_inc(sem("const_in"), 16)
            act.dma_start(prm[:, :], par).then_inc(sem("par_in"), 16)
            mem_v = mem.rearrange("(t p) c -> p t c", p=P)
            act.dma_start(mem_in, mem_v).then_inc(sem("mem_in"), 16)

            def hi_half(u):
                if u >= SPL:
                    act.wait_ge(unit_done, u - SPL + 1)
                act.wait_ge(raw_ready[u % RAW], raw_at[u] if u < FFN_UNIT0 else ffn_raw_at(u - FFN_UNIT0))
                n = unit_cols(u)
                fn(w_hi[:, (u % SPL) * 1024:(u % SPL) * 1024 + n], w_raw[:, (u % RAW) * 1024:(u % RAW) * 1024 + n],
                   ACT.Copy).then_inc(hi_done, 1)

            def link(ins):
                chain[0] += 1
                ins.then_inc(sem("act_chain"), 1)
                act.wait_ge(sem("act_chain"), chain[0])

            def inv_root(dst, src, scale):
                link(fn(dst, src, ACT.Ln, scale=scale, bias=eps))
                return fn(dst, dst, ACT.Exp, scale=-0.5)

            chain = [0]
            eps = K["eps"]

            act.wait_ge(sem("const_in"), 16)
            act.wait_ge(sem("par_in"), 16)
            for t in range(TT):
                act.wait_ge(sem(f"x_in{t}"), 16)
                link(fn(scratch, resid[:, t, :], ACT.Square, accum_out=ssx[:, t:t + 1]))
            inv_root(rx, ssx, 1.0 / D_MODEL).then_inc(sem("rx_ready"), 1)
            hi_half(0)
            hi_half(1)

            def x_split(k):
                act.wait_ge(sem("x_turned"), k + 1)
                fn(x_hi[:, k, :], bank[3 + k % 5], ACT.Copy, scale=A["norm_mix"][:, k:k + 1]).then_inc(sem("x_hi_done"), 1)

            def mem_split(j):
                act.wait_ge(sem("mem_turned"), j + 1)
                for k in (2 * j, 2 * j + 1):
                    fn(um_hi[:, k, :], bank[3 + j % 5][:, (k % 2) * 256:(k % 2) * 256 + 256], ACT.Copy,
                       scale=A["mem_norm"][:, k:k + 1]).then_inc(sem("mem_hi_done"), 1)

            def main_copies(n, kind, h, g):
                if kind == "gdn":
                    act.wait_ge(sem("pads_zero"), h + 1)
                else:
                    qkv_free(act, n)
                for s in range(2):
                    act.wait_ge(group_sums, 2 * g + s + 1)
                    w = MEM_LEN if kind == "mem" and s == 1 else SEQ
                    dst = cin[:, s, 3:] if kind == "gdn" else qkv[:, s, 0:w]
                    fn(dst, bank[s][:, 0:w], ACT.Copy).then_inc(bank_taken[s], 1)

            def squares(n, kind, g):
                for s in range(2):
                    act.wait_ge(bank_taken[s], g + 1)
                if n > 0:
                    act.wait_ge(sem("qn_ready"), n)
                    act.wait_ge(sem("kn_ready"), n)
                if kind == "mem":
                    fn(sq[:, 0, :], qkv[:, 0, :], ACT.Square)
                    fn(sq[:, 1, 0:MEM_LEN], qkv[:, 1, 0:MEM_LEN], ACT.Square).then_inc(sem("sq_ready"), 1)
                else:
                    fn(sq, qkv[:, 0:2, :], ACT.Square).then_inc(sem("sq_ready"), 1)

            def factors(n, kind):
                act.wait_ge(sem("ssq_ready"), n + 1)
                width = SEQ + (MEM_LEN if kind == "mem" else SEQ)
                flat = sq.rearrange("p s t -> p (s t)")[:, 0:width]
                src = psum[:, 2048:2048 + width]
                inv_root(flat, src, 1.0 if kind == "gdn" else 1.0 / HD).then_inc(sem("rn_ready"), 1)

            def mem_side(n, h, v):
                if v == 1:
                    squares(n, "mem", n + 2)
                if v == 5:
                    factors(n, "mem")
                if v == 10:
                    act.wait_ge(sem("mem_max"), h + 1)
                    for j in range(TT):
                        last = fn(pr[:, j * 256:j * 256 + 256], T[j // 2][:, (j % 2) * 256:(j % 2) * 256 + 256], ACT.Exp,
                                  bias=nmx[:, j:j + 1], accum_out=rsum[:, j:j + 1])
                    last.then_inc(sem("mem_exp"), 1)
                if v == TURN_V:
                    act.wait_ge(sem("mem_turned_p"), 2 * h + 1)
                    fn(pt[:, 0:512], T[0], ACT.Copy).then_inc(sem("mem_pt0"), 1)

            def fox_side(n, h, v):
                if v == 1:
                    squares(n, "fox", n + 2)
                if v == 5:
                    act.wait_ge(sem("negc_ready"), h + 1)
                    fn(ncb, T[2], ACT.Copy).then_inc(sem("ncb_ready"), 1)
                    factors(n, "fox")
                if v == 10:
                    act.wait_ge(sem("fox_max"), h + 1)
                    off = [0, 128, 384, 768, 1280]
                    for j in range(TT):
                        last = fn(pr[:, off[j]:off[j + 1]], pr[:, off[j]:off[j + 1]], ACT.Exp,
                                  bias=nmx[:, j:j + 1], accum_out=rsum[:, j:j + 1])
                    last.then_inc(sem("fox_exp"), 1)
                if v == TURN_V:
                    act.wait_ge(sem("fox_turned0"), h + 1)
                    fn(pt[:, 0:512], T[0], ACT.Copy).then_inc(sem("fox_pt0"), 1)
                    act.wait_ge(sem("fox_turned2"), h + 1)
                    fn(pt[:, 896:1280], T[2][:, 0:384], ACT.Copy).then_inc(sem("fox_pt2"), 1)

            def gdn_side(n, h, v):
                b = h % 2
                if v == 2:
                    act.wait_ge(sem("conv_step"), 12 * h + 12)
                    fn(qkv, qkv, ACT.Silu).then_inc(sem("silu_done"), 1)
                    act.wait_ge(sem("silu_done"), h + 1)
                    squares(n, "gdn", n + 2)
                if v == 5:
                    factors(n, "gdn")
                    act.wait_ge(sem("dec_arg"), h + 1)
                    fn(dec, dec, ACT.Exp).then_inc(sem("decay"), 1)
                if v == 6:
                    act.wait_ge(sem("gc_rows"), h + 1)
                    if h >= 2:
                        act.wait_ge(sem("ds_ready"), NCH * (h - 1))
                    fn(sc_qg[b], T[2], ACT.Exp).then_inc(sem("qg_exp"), 1)
                if v == 8:
                    act.wait_ge(sem("inv0_turned"), h + 1)
                    fn(inv[:, 0, :, :].rearrange("p t c -> p (t c)"), T[0][:, 0:256], ACT.Copy) \
                        .then_inc(sem("inv0_copied"), 1)
                for l in range(1, 6):
                    if v == 7 + 2 * l:
                        act.wait_ge(sem("y_ready"), 5 * h + l)
                        fn(yb.rearrange("p t c -> p (t c)"), T[1][:, 0:256], ACT.Copy).then_inc(sem("y_copied"), 1)
                if v == 19:
                    act.wait_ge(sem("u_ready"), h + 1)
                    fn(sc_u[b].rearrange("p t d -> p (t d)"), T[1], ACT.Copy).then_inc(sem("uw_taken"), 1)
                    act.wait_ge(sem("w_ready"), h + 1)
                    for a in range(2):
                        last = fn(sc_nw[b].rearrange("p (t a c) -> p a t c", t=TT, a=2)[:, a],
                                  T[2 - 2 * a][:, 0:256].rearrange("p (t c) -> p t c", t=TT), ACT.Copy, scale=-1.0)
                    last.then_inc(sem("uw_taken"), 1)
                if v == 36:
                    act.wait_ge(sem("ds_ready"), NCH * (h + 1))
                    for i in range(TT):
                        last = fn(mix[:, MIX_GDN + h, i * P:i * P + P], S2[:, i * P:i * P + P], ACT.Square,
                                  accum_out=oss[:, i:i + 1])
                    link(last)
                    inv_root(orn, oss, 1.0 / HD).then_inc(sem("or_ready"), 1)

            def z_side(i):
                for s in range(3):
                    if s < 2:
                        act.wait_ge(group_sums, 2 * i + s + 1)
                    else:
                        act.wait_ge(unit_done, UPG * (i + 1))
                    fn(zg[:, 3 * i + s, :], bank[s], ACT.Silu).then_inc(bank_taken[s], 1)

            def mix_split(j):
                k = MIX_ORDER[j]
                if j == 0:
                    act.wait_ge(unit_done, OUT_UNIT0)
                if k >= MIX_MEM:
                    act.wait_ge(sem("mem_mixed"), N_MEM)
                elif k >= MIX_GDN:
                    act.wait_ge(sem("gdn_mixed"), N_GDN)
                else:
                    act.wait_ge(sem("fox_mixed"), k + 1)
                fn(x_hi[:, k, :], mix[:, k, :], ACT.Copy).then_inc(sem("mix_hi_done"), 1)

            for k in range(4):
                x_split(k)
            for t in range(LAST_VISIT):
                u, half = divmod(t, 2)
                if half == 0 and u < UPG:
                    for k in (2 * u + 4, 2 * u + 5):
                        if k < KD:
                            x_split(k)
                if half == 0:
                    hi_half(u + AHEAD)
                if t == 4:
                    fn(wg_hi.rearrange("p k c -> p (k c)"), A["gate_w"], ACT.Copy).then_inc(sem("gate_w_hi"), 1)
                    act.wait_ge(sem("mem_in"), 16)
                    for m in range(MT):
                        link(fn(scratch, mem_in[:, m, :], ACT.Square, accum_out=ssm[:, m:m + 1]))
                    inv_root(rm, ssm, 1.0 / D_MODEL).then_inc(sem("rm_ready"), 1)
                if t in (VPG - 1, 2 * VPG - 1):
                    z_side(t // VPG)
                g = (t + 1) // VPG - 1
                if (t + 1) % VPG == 0 and 2 <= g < N_GROUPS:
                    main_copies(g - 2, *GROUPS[g], g)
                if VPG <= t < VPG + KD // 2:
                    mem_split(t - VPG)
                if t == VPG + 11:
                    fn(coef[:, N_FOX:N_FOX + N_GDN], A["a_log"], ACT.Exp).then_inc(sem("rates"), 1)
                    act.wait_ge(sem("gate_abs"), 1)
                    link(fn(ga, ga, ACT.Exp, scale=-1.0))
                    fn(ga, ga, ACT.Ln, bias=K["ones"][:, 0:1]).then_inc(sem("gate_ln"), 1)
                if t == VPG + 15:
                    act.wait_ge(sem("gate_sums_read"), 1)
                    gs = gsum.rearrange("p (i t h) -> p i t h", i=4, t=TT)
                    fn(kdf, gs[:, 1], ACT.Exp)
                    fn(egl, gs[:, 2:4], ACT.Exp)
                    fn(beta, ga[:, :, N_FOX + N_GDN:], ACT.Exp)
                    act.wait_ge(sem("beg_arg"), 1)
                    fn(beg, beg, ACT.Exp).then_inc(sem("gate_exps"), 1)
                if t >= VPG * N_GROUPS and t % 2 == 0:
                    kk = (t - VPG * N_GROUPS) // 2
                    for j in range(2 * kk + 2 if kk else 0, min(2 * kk + 4, KD - 1)):
                        mix_split(j)
                for n, kind, h, v in head_visit(t):
                    {"mem": mem_side, "gdn": gdn_side, "fox": fox_side}[kind](n, h, v)
                if t == VPG * (N_GROUPS - 1):
                    act.wait_ge(sem("gdn_mixed"), N_GDN)
                    act.dma_start(resid, x.rearrange("(t p) c -> p t c", p=P)).then_inc(sem("resid_in"), 16)
            mix_split(KD - 1)

            def part_squares(cg):
                act.wait_ge(resid_added, cg + 1)
                act.wait_ge(sem("mix_split"), KD)
                if cg > 0:
                    act.wait_ge(sem("part_sq"), cg)
                for t in range(TT):
                    last = fn(scratch[:, 512 * t:512 * t + 512], resid[:, t, 512 * cg:512 * cg + 512], ACT.Square,
                              accum_out=ss2[:, t, cg:cg + 1])
                last.then_inc(sem("part_sq"), 1)

            for u in range(LAST_VISIT // 2, FFN_UNIT0):
                hi_half(u + AHEAD)
                cg, kk = divmod(u - OUT_UNIT0, UPG)
                if kk == 3 and cg > 0:
                    part_squares(cg - 1)
            part_squares(N_CG - 1)
            act.wait_ge(sem("ss2_sum"), 1)
            inv_root(r2, ss2s, 1.0 / D_MODEL).then_inc(sem("r2_ready"), 1)
            act.wait_ge(sem("r2_ready"), 1)
            fn(norm_v[:, TT - 1, :], resid[:, TT - 1, :], ACT.Copy, scale=r2[:, TT - 1:TT]).then_inc(sem("h_normed"), 1)

            def h_split(k):
                act.wait_ge(sem("h_turned"), k + 1)
                fn(x_hi[:, k, :], bank[4 + k % 4], ACT.Copy, scale=A["norm_ffn"][:, k:k + 1]).then_inc(sem("h_hi_done"), 1)

            def ffn_hi(u, jj, landed):
                act.wait_ge(unit_done, u - SPL + 1)
                act.wait_ge(raw_ready[ffn_slot(jj, RAW)], landed)
                sr, ss = 1024 * ffn_slot(jj, RAW), 1024 * ffn_slot(jj, SPL)
                fn(w_hi[:, ss:ss + 1024], w_raw[:, sr:sr + 1024], ACT.Copy).then_inc(hi_done, 1)

            def take_gate(done, taken):
                act.wait_ge(unit_done, done)
                if taken is not None:
                    act.wait_ge(sem("act_ready"), taken)
                fn(silu_gate[:, :], set_a, ACT.Silu).then_inc(sem("gate_taken"), 1)

            def act_hi_half(chunks):
                act.wait_ge(sem("up_taken"), chunks)
                fn(act_hi.rearrange("p f t -> p (f t)"), silu_gate[:, :], ACT.Copy).then_inc(sem("act_hi_done"), 1)

            for k in range(4):
                h_split(k)
            for j in range(2 * UPG):
                for k in (2 * j + 4, 2 * j + 5):
                    if k < KD:
                        h_split(k)
                ffn_hi(FFN_UNIT0 + j + AHEAD, j + AHEAD, ffn_raw_at(j + AHEAD))
                if j == UPG:
                    take_gate(FFN_UNIT0 + UPG, None)
            with act.Fori(1, N_CHUNKS) as c:
                u0 = FFN_UNIT0 + c * UPC - UPG
                for j in range(UPC):
                    jj = LOOP_J + j + AHEAD
                    ffn_hi(u0 + j + AHEAD, jj, c * (16 * UPC // RAW) + (ffn_raw_at(jj) - 16 * UPC // RAW))
                    if j == 0:
                        act_hi_half(c)
                    if j == UPG:
                        take_gate(u0 + UPG, c)
            u0 = FFN_UNIT0 + N_CHUNKS * UPC - UPG
            for j in range(UPG):
                if j + AHEAD < UPG:
                    jj = UPC * (N_CHUNKS - 1) + LOOP_J + j + AHEAD
                    ffn_hi(u0 + j + AHEAD, jj, ffn_raw_at(jj))
                if j == 0:
                    act_hi_half(N_CHUNKS)

        @block.vector
        def _(dve):
            tt, ts, stt, copy = (nc.vector.tensor_tensor, nc.vector.tensor_scalar, nc.vector.scalar_tensor_tensor,
                                 nc.vector.tensor_copy)
            chain = [0]

            def link(ins):
                chain[0] += 1
                ins.then_inc(sem("dve_chain"), 1)
                dve.wait_ge(sem("dve_chain"), chain[0])

            def lo_half(u):
                dve.wait_ge(hi_done, u + 1)
                n, sr, ss = unit_cols(u), (u % RAW) * 1024, (u % SPL) * 1024
                tt(w_lo[:, ss:ss + n], w_raw[:, sr:sr + n], w_hi[:, ss:ss + n].bitcast(F32), ALU.subtract) \
                    .then_inc(lo_done, 1)

            def x_split(k):
                dve.wait_ge(sem("x_hi_done"), k + 1)
                stt(x_lo[:, k, :], bank[3 + k % 5], A["norm_mix"][:, k:k + 1], x_hi[:, k, :].bitcast(F32),
                    ALU.mult, ALU.subtract).then_inc(sem("x_split"), 1)

            def mem_split(j):
                for k in (2 * j, 2 * j + 1):
                    dve.wait_ge(sem("mem_hi_done"), 2 * j + 2)
                    stt(um_lo[:, k, :], bank[3 + j % 5][:, (k % 2) * 256:(k % 2) * 256 + 256],
                        A["mem_norm"][:, k:k + 1], um_hi[:, k, :].bitcast(F32), ALU.mult, ALU.subtract) \
                        .then_inc(sem("mem_split"), 1)

            def take_v(n, kind, h):
                dve.wait_ge(unit_done, UPG * (n + 3))
                if kind == "gdn":
                    dve.wait_ge(sem("pads_zero"), h + 1)
                    copy(cin[:, 2, 3:], bank[2]).then_inc(bank_taken[2], 1)
                    return
                qkv_free(dve, n)
                w = MEM_LEN if kind == "mem" else SEQ
                copy(qkv[:, 2, 0:w], bank[2][:, 0:w]).then_inc(bank_taken[2], 1)

            def norm_q(n, kind):
                dve.wait_ge(sem("rn_ready"), n + 1)
                gain = {"mem": comb[:, 0:1], "fox": comb[:, 1:2], "gdn": SCALE}[kind]
                stt(qkv[:, 0, :], qkv[:, 0, :], gain, sq[:, 0, :], ALU.mult, ALU.mult).then_inc(sem("qn_ready"), 1)

            def scale_probs(kind, h, cuts):
                dve.wait_ge(sem(kind + "_exp"), h + 1)
                link(nc.vector.reciprocal(rrec, rsum))
                for j in range(TT):
                    last = ts(pr[:, cuts[j]:cuts[j + 1]], pr[:, cuts[j]:cuts[j + 1]], rrec[:, j:j + 1], None, ALU.mult)
                last.then_inc(sem(kind + "_probs"), 1)

            def mem_side(n, h, v):
                if v == 5:
                    norm_q(n, "mem")
                if v == 7:
                    dve.wait_ge(sem("tok_ready"), n + 1)
                    copy(vtok[:, 0:MT, :].rearrange("p t d -> p (t d)"), T[2][:, 0:MEM_LEN]).then_inc(sem("vtok_ready"), 1)
                if v in (8, 9):
                    i = v - 8
                    dve.wait_ge(sem("mem_scores"), 2 * h + i + 1)
                    last = nc.vector.tensor_reduce(mx[:, 2 * i:2 * i + 2], T[i].rearrange("p (j c) -> p j c", j=2),
                                                   AX.X, ALU.max)
                    if v == 9:
                        link(last)
                        ts(nmx, mx, -1.0, None, ALU.mult).then_inc(sem("mem_max"), 1)
                if v == 10:
                    scale_probs("mem", h, [256 * j for j in range(TT + 1)])
                if v == TURN_V:
                    dve.wait_ge(sem("mem_turned_p"), 2 * h + 2)
                    copy(pt[:, 512:1024], T[1]).then_inc(sem("mem_pt1"), 1)
                if v == PV_V:
                    dve.wait_ge(sem("mem_pv"), h + 1)
                    copy(mix[:, MIX_MEM + h, :], T[2]).then_inc(sem("mem_mixed"), 1)

            def fox_side(n, h, v):
                if v == 5:
                    norm_q(n, "fox")
                if v == 7:
                    dve.wait_ge(sem("tok_ready"), n + 1)
                    copy(vtok.rearrange("p t d -> p (t d)"), T[2]).then_inc(sem("vtok_ready"), 1)
                off = [0, 128, 384, 768, 1280]
                if v in (8, 9, 10):
                    if v == 8:
                        dve.wait_ge(sem("ncb_ready"), h + 1)
                    dve.wait_ge(sem("fox_scores"), 3 * h + v - 7)
                    for j, b, c0 in {8: ((0, 0, 0), (1, 0, 128)), 9: ((2, 1, 0),), 10: ((3, 2, 0),)}[v]:
                        w = (j + 1) * P
                        last = nc.vector.tensor_tensor_reduce(pr[:, off[j]:off[j + 1]], T[b][:, c0:c0 + w], ncb[:, 0:w],
                                                              1.0, -3e38, ALU.add, ALU.max, mx[:, j:j + 1])
                    if v == 10:
                        link(last)
                        ts(nmx, mx, -1.0, None, ALU.mult).then_inc(sem("fox_max"), 1)
                        scale_probs("fox", h, off)
                if v == TURN_V:
                    dve.wait_ge(sem("fox_turned1"), h + 1)
                    copy(pt[:, 512:896], T[1][:, 0:384]).then_inc(sem("fox_pt1"), 1)
                if v == PV_V:
                    dve.wait_ge(sem("fox_pv"), h + 1)
                    copy(mix[:, MIX_FOX + h, :], T[2]).then_inc(sem("fox_mixed"), 1)

            def conv(n, h):
                banks_taken(dve, n + 3)
                qkv_free(dve, n)
                for j in range(TAPS):
                    for s in range(3):
                        w, src = conv_w[:, s, h, j:j + 1], cin[:, s, j:j + SEQ]
                        if j == 0:
                            ins = ts(qkv[:, s, :], src, w, None, ALU.mult)
                        else:
                            dve.wait_ge(sem("conv_step"), 12 * h + 3 * (j - 1) + s + 1)
                            ins = stt(qkv[:, s, :], src, w, qkv[:, s, :], ALU.mult, ALU.add)
                        ins.then_inc(sem("conv_step"), 1)

            def gdn_side(n, h, v):
                b = h % 2
                hc = slice(h, h + 1)
                if v == 0:
                    conv(n, h)
                if v == 5:
                    dve.wait_ge(sem("decay_rows"), h + 1)
                    if h == 0:
                        dve.wait_ge(sem("gate_exps"), 1)
                    for w in range(2):
                        last = tt(dec[:, w], T[2][:, 256 * w:256 * w + 256].rearrange("p (t c) -> p t c", t=TT),
                                  bcl(ngc[:, :, h], CHUNK), ALU.add)
                    link(last)
                    d8 = dec.rearrange("p w t c -> p (w t) c")
                    tt(d8, d8, K["neg64"].unsqueeze(1).to_broadcast([P, 2 * TT, CHUNK]), ALU.add) \
                        .then_inc(sem("dec_arg"), 1)
                    norm_q(n, "gdn")
                if v == 7:
                    i64 = K["ident64"].unsqueeze(1).to_broadcast([P, TT, CHUNK])
                    pair0 = K["pair0"].unsqueeze(1).to_broadcast([P, TT, CHUNK])
                    dve.wait_ge(sem("gram_ready"), h + 1)
                    dve.wait_ge(sem("decay"), h + 1)
                    if h > 0:
                        dve.wait_ge(sem("coup_ready"), 5 * h)
                    if h >= 2:
                        dve.wait_ge(sem("ds_ready"), NCH * (h - 1))
                    t0 = T[0].rearrange("p (w t c) -> p w t c", w=2, t=TT)
                    tt(lt, t0[:, 0], dec[:, 1], ALU.mult).then_inc(sem("lt_ready"), 1)
                    tt(sc_at[b], t0[:, 1], dec[:, 0], ALU.mult)
                    dve.wait_ge(sem("lt_ready"), h + 1)
                    link(tt(inv[:, 1], lt, pair0, ALU.mult))
                    tt(inv[:, 1], i64, inv[:, 1], ALU.subtract).then_inc(sem("inv0_ready"), 1)
                    dve.wait_ge(sem("ktok_ready"), h + 1)
                    k3 = T[1].rearrange("p (t d) -> p t d", t=TT)
                    tt(kbg, k3, bcl(beg[:, :, h], HD), ALU.mult)
                    tt(sc_kd[b], k3, bcl(kdf[:, :, h], HD), ALU.mult).then_inc(sem("k_scaled"), 1)
                    dve.wait_ge(sem("tok_ready"), n + 1)
                    tt(vb, T[2].rearrange("p (t d) -> p t d", t=TT), bcl(beta[:, :, h], HD), ALU.mult) \
                        .then_inc(sem("v_scaled"), 1)
                for l in range(1, 6):
                    if v == 8 + 2 * l:
                        dve.wait_ge(sem("xy_ready"), 5 * h + l)
                        t0 = T[0].rearrange("p (w t c) -> p w t c", w=2, t=TT)
                        if l == 1:
                            dve.wait_ge(sem("inv0_copied"), h + 1)
                        w = slice(0, 2) if l < 5 else slice(1, 2)
                        i8, p8 = (a[:, w].rearrange("p w t c -> p (w t c)") for a in (inv, t0))
                        tt(i8, i8, p8, ALU.subtract).then_inc(sem("inv_updated"), 1)
                if 21 <= v < 21 + 2 * NCH:
                    c, second = divmod(v - 21, 2)
                    i, s = c // 2, slice(64 * (c % 2), 64 * (c % 2) + 64)
                    if not second:
                        dve.wait_ge(sem("ws_ready"), NCH * h + c + 1)
                        tt(v_new[s, :], sc_u[b][s, i, :], S1[s, 0:P], ALU.add).then_inc(sem("v_new"), 1)
                    else:
                        dve.wait_ge(sem("ds_ready"), NCH * h + c + 1)
                        if c < NCH - 1:
                            stt(state, state, egl[:, c % 2, i, hc], S1[:, P:2 * P], ALU.mult, ALU.add) \
                                .then_inc(sem("state_new"), 1)
                        else:
                            nc.vector.memset(state, 0.0).then_inc(sem("state_clear"), 1)
                if v == 37:
                    dve.wait_ge(sem("or_ready"), h + 1)
                    tt(mix[:, MIX_GDN + h, :].rearrange("p (t d) -> p t d", t=TT),
                       S2.rearrange("p (t d) -> p t d", t=TT), bcl(orn, HD), ALU.mult).then_inc(sem("o_scaled"), 1)
                if v == 52:
                    dve.wait_ge(sem("o_turned"), h + 1)
                    dve.wait_ge(sem("zg_ready"), 2)
                    tt(mix[:, MIX_GDN + h, :], T[0], zg[:, h, :], ALU.mult).then_inc(sem("gdn_mixed"), 1)

            def mix_split(j):
                k = MIX_ORDER[j]
                dve.wait_ge(sem("mix_hi_done"), j + 1)
                tt(x_lo[:, k, :], mix[:, k, :], x_hi[:, k, :].bitcast(F32), ALU.subtract).then_inc(sem("mix_split"), 1)

            def out_add(cg):
                dve.wait_ge(unit_done, OUT_UNIT0 + UPG * (cg + 1))
                dve.wait_ge(sem("resid_in"), 16)
                r = resid[:, :, 512 * cg:512 * cg + 512]
                tt(r, (set_a, set_b)[cg % 2].rearrange("p (t c) -> p t c", t=TT), r, ALU.add).then_inc(resid_added, 1)

            dve.wait_ge(sem("const_in"), 16)
            dve.wait_ge(sem("par_in"), 16)
            copy(identb[:, :], K["ident"]).then_inc(sem("bf_consts"), 1)
            copy(causalb[:, :], K["causal"]).then_inc(sem("bf_consts"), 1)
            stt(comb[:, 0:1], A["mem_q"], SCALE, A["mem_k"], ALU.mult, ALU.mult)
            stt(comb[:, 1:2], A["fox_q"], SCALE, A["fox_k"], ALU.mult, ALU.mult).then_inc(sem("comb_ready"), 1)
            nc.vector.memset(coef, -1.0).then_inc(sem("coef_set"), 1)
            dve.wait_ge(sem("comb_ready"), 1)
            dve.wait_ge(sem("rx_ready"), 1)
            for t in range(TT):
                ts(resid[:, t, :], resid[:, t, :], rx[:, t:t + 1], None, ALU.mult).then_inc(sem("x_normed"), 1)
            lo_half(0)
            lo_half(1)
            for k in range(4):
                x_split(k)
            for t in range(LAST_VISIT):
                u, half = divmod(t, 2)
                if half == 0 and u < UPG:
                    for k in (2 * u + 4, 2 * u + 5):
                        if k < KD:
                            x_split(k)
                for n, kind, h, v in head_visit(t):
                    if v == 0:
                        take_v(n, kind, h)
                if half == 0:
                    lo_half(u + AHEAD)
                if t == 5:
                    dve.wait_ge(sem("gate_w_hi"), 1)
                    tt(wg_lo.rearrange("p k c -> p (k c)"), A["gate_w"],
                       wg_hi.rearrange("p k c -> p (k c)").bitcast(F32), ALU.subtract).then_inc(sem("gate_w_split"), 1)
                    dve.wait_ge(sem("rm_ready"), 1)
                    for m in range(MT):
                        ts(mem_in[:, m, :], mem_in[:, m, :], rm[:, m:m + 1], None, ALU.mult).then_inc(sem("mem_normed"), 1)
                if VPG <= t < VPG + KD // 2:
                    mem_split(t - VPG)
                if t == VPG + 11:
                    dve.wait_ge(sem("gates_ready"), 1)
                    row = lambda a, n: a.unsqueeze(1).to_broadcast([P, TT, n])
                    link(tt(gz, bank[3][:, 0:TT * NG].rearrange("p (t c) -> p t c", t=TT), row(A["gate_bias"], NG), ALU.add))
                    link(tt(gz, gz, row(A["gate_sign"], NG), ALU.mult))
                    stt(ga, gz, -1.0, gz, ALU.mult, ALU.max).then_inc(sem("gate_abs"), 1)
                    dve.wait_ge(sem("rates"), 1)
                    rates = coef[:, N_FOX:N_FOX + N_GDN]
                    link(ts(rates, rates, -1.0, None, ALU.mult))
                    dve.wait_ge(sem("gate_ln"), 1)
                    link(stt(ga, gz, 0.0, ga, ALU.max, ALU.add))
                    tt(ga, ga, row(coef, NG), ALU.mult).then_inc(sem("gate_logs"), 1)
                if t == VPG + 15:
                    dve.wait_ge(sem("gate_sums"), 1)
                    copy(gsum, bank[4][:, 0:4 * n4]).then_inc(sem("gate_sums_read"), 1)
                    dve.wait_ge(sem("gate_sums_read"), 1)
                    gc = gsum[:, 0:n4].rearrange("p (t h) -> p t h", t=TT)
                    tt(beg, gc, ga[:, :, N_FOX + N_GDN:], ALU.add).then_inc(sem("beg_arg"), 1)
                    ts(ngc, gc, -1.0, None, ALU.mult).then_inc(sem("ngc_ready"), 1)
                    nc.vector.memset(state, 0.0).then_inc(sem("state_clear"), 1)
                    dve.wait_ge(sem("ngc_ready"), 1)
                if t >= VPG * N_GROUPS and t % 2 == 0:
                    kk = (t - VPG * N_GROUPS) // 2
                    for j in range(2 * kk + 2 if kk else 0, min(2 * kk + 4, KD - 1)):
                        mix_split(j)
                for n, kind, h, v in head_visit(t):
                    {"mem": mem_side, "gdn": gdn_side, "fox": fox_side}[kind](n, h, v)
            mix_split(KD - 1)
            for u in range(LAST_VISIT // 2, FFN_UNIT0):
                lo_half(u + AHEAD)
                cg, kk = divmod(u - OUT_UNIT0, UPG)
                if kk == 0:
                    out_add(cg - 1)
            out_add(N_CG - 1)
            dve.wait_ge(sem("part_sq"), N_CG)
            nc.vector.tensor_reduce(ss2s, ss2, AX.X, ALU.add).then_inc(sem("ss2_sum"), 1)
            dve.wait_ge(sem("r2_ready"), 1)
            for t in range(TT - 1):
                ts(norm_v[:, t, :], resid[:, t, :], r2[:, t:t + 1], None, ALU.mult).then_inc(sem("h_normed"), 1)

            def h_split(k):
                dve.wait_ge(sem("h_hi_done"), k + 1)
                stt(x_lo[:, k, :], bank[4 + k % 4], A["norm_ffn"][:, k:k + 1], x_hi[:, k, :].bitcast(F32),
                    ALU.mult, ALU.subtract).then_inc(sem("h_split"), 1)

            def ffn_lo(u, jj):
                dve.wait_ge(hi_done, u + 1)
                sr, ss = 1024 * ffn_slot(jj, RAW), 1024 * ffn_slot(jj, SPL)
                tt(w_lo[:, ss:ss + 1024], w_raw[:, sr:sr + 1024], w_hi[:, ss:ss + 1024].bitcast(F32), ALU.subtract) \
                    .then_inc(lo_done, 1)

            def take_up(done, chunks):
                dve.wait_ge(unit_done, done)
                dve.wait_ge(sem("gate_taken"), chunks)
                tt(silu_gate[:, :], set_b, silu_gate[:, :], ALU.mult).then_inc(sem("up_taken"), 1)

            def act_lo_half(chunks):
                dve.wait_ge(sem("act_hi_done"), chunks)
                tt(act_lo.rearrange("p f t -> p (f t)"), silu_gate[:, :],
                   act_hi.rearrange("p f t -> p (f t)").bitcast(F32), ALU.subtract).then_inc(sem("act_ready"), 1)

            def down_add(done, before, cg, side):
                dve.wait_ge(unit_done, done)
                dve.wait_ge(resid_added, before)
                r = resid[:, :, 512 * cg:512 * cg + 512]
                tt(r, (set_a, set_b)[side].rearrange("p (t c) -> p t c", t=TT), r, ALU.add).then_inc(resid_added, 1)

            for k in range(4):
                h_split(k)
            for j in range(2 * UPG):
                for k in (2 * j + 4, 2 * j + 5):
                    if k < KD:
                        h_split(k)
                ffn_lo(FFN_UNIT0 + j + AHEAD, j + AHEAD)
            with dve.Fori(1, N_CHUNKS) as c:
                u0 = FFN_UNIT0 + c * UPC - UPG
                for j in range(UPC):
                    ffn_lo(u0 + j + AHEAD, LOOP_J + j + AHEAD)
                    if j == 0:
                        take_up(u0, c)
                    if j == 1:
                        act_lo_half(c)
                    if j in (10, 12, 14, 16):
                        cg = (j - 10) // 2
                        down_add(u0 + j, c * N_CG + cg, cg, 1 - cg % 2)
            u0 = FFN_UNIT0 + N_CHUNKS * UPC - UPG
            for j in range(UPG + 1):
                if j + AHEAD < UPG:
                    ffn_lo(u0 + j + AHEAD, LOOP_J + j + AHEAD)
                if j == 0:
                    take_up(u0, N_CHUNKS)
                    act_lo_half(N_CHUNKS)
                if j >= 2 and j % 2 == 0:
                    cg = j // 2 - 1
                    down_add(u0 + j, N_CHUNKS * N_CG + cg, cg, cg % 2)

        @block.gpsimd
        def _(pool):
            tt, copy = nc.gpsimd.tensor_tensor, nc.gpsimd.tensor_copy

            def norm_k(n, kind):
                pool.wait_ge(sem("rn_ready"), n + 1)
                w = MEM_LEN if kind == "mem" else SEQ
                tt(qkv[:, 1, 0:w], qkv[:, 1, 0:w], sq[:, 1, 0:w], ALU.mult).then_inc(sem("kn_ready"), 1)

            def mem_side(n, h, v):
                if v == 5:
                    norm_k(n, "mem")

            def fox_side(n, h, v):
                if v == 0:
                    pool.wait_ge(sem("gc_rows"), N_GDN)
                    if h > 0:
                        pool.wait_ge(sem("negc_ready"), h)
                    copy(g_bc, bcl(ga[:, :, h], P)).then_inc(sem("bc_ready"), 1)
                if v == 5:
                    norm_k(n, "fox")

            def gdn_side(n, h, v):
                b = h % 2
                if v == 0:
                    pool.wait_ge(sem("qn_ready"), n)
                    pool.wait_ge(sem("kn_ready"), n)
                    nc.gpsimd.memset(cin[:, :, 0:TAPS - 1], 0.0).then_inc(sem("pads_zero"), 1)
                    if h > 0:
                        pool.wait_ge(sem("gc_rows"), h)
                    else:
                        pool.wait_ge(sem("gate_exps"), 1)
                    copy(g_bc, bcl(ga[:, :, N_FOX + h], P)).then_inc(sem("bc_ready"), 1)
                    copy(b_bc, bcl(ga[:, :, N_FOX + N_GDN + h], CHUNK)).then_inc(sem("bc_ready"), 1)
                if v == 5:
                    norm_k(n, "gdn")
                if v == 6:
                    pool.wait_ge(sem("qn_ready"), n + 1)
                    pool.wait_ge(sem("qg_exp"), h + 1)
                    tt(sc_qg[b], sc_qg[b], qkv[:, 0, :], ALU.mult).then_inc(sem("qg_ready"), 1)
                if v == 7:
                    pool.wait_ge(sem("lt_ready"), h + 1)
                    if h > 0:
                        pool.wait_ge(sem("y_ready"), 5 * h)
                    for l in range(1, 6):
                        tt(coup[:, l - 1], lt, K[f"pair{l}"].unsqueeze(1).to_broadcast([P, TT, CHUNK]), ALU.mult) \
                            .then_inc(sem("coup_ready"), 1)

            pool.wait_ge(sem("par_in"), 16)
            for t in range(LAST_VISIT):
                if t in (VPG, 2 * VPG):
                    i = t // VPG - 1
                    banks_taken(pool, i + 1)
                    z = zg[:, 3 * i:3 * i + 3, :]
                    nc.gpsimd.tensor_scalar(z, z, A["gdn_out"], 1.0, ALU.mult, ALU.mult).then_inc(sem("zg_ready"), 1)
                for n, kind, h, v in head_visit(t):
                    {"mem": mem_side, "gdn": gdn_side, "fox": fox_side}[kind](n, h, v)


_INS = ["x", "mem", "w_in", "w_mem_kv", "w_out", "w_gate_up", "w_down"]


def kernel(x, mem, norm_mix, w_in, fox_f_bias, fox_q_norm, fox_k_norm, gdn_conv, gdn_a_log, gdn_dt_bias,
           gdn_out_norm, mem_norm, w_mem_kv, mem_q_norm, mem_k_norm, w_out, norm_ffn, w_gate_up, w_down):
    import concourse.bacc as bacc
    from concourse.bass_utils import run_bass_kernel_spmd

    a = {n: np.ascontiguousarray(np.asarray(v)[0]) for n, v in
         dict(x=x, mem=mem, w_in=w_in, w_mem_kv=w_mem_kv, w_out=w_out, w_gate_up=w_gate_up, w_down=w_down).items()}
    tiles = lambda v: np.asarray(v)[0].reshape(-1, P).T
    rows = lambda v: np.repeat(np.asarray(v, np.float32).reshape(1, -1), P, 0)
    zeros, ones = np.zeros(N_GDN, np.float32), np.ones(N_GDN, np.float32)
    gate_cols = np.concatenate([a["w_in"][:, C_FF:C_FF + N_FOX], a["w_in"][:, C_GA:C_GA + 2 * N_GDN]], 1)
    parts = dict(
        norm_mix=tiles(norm_mix), mem_norm=tiles(mem_norm), norm_ffn=tiles(norm_ffn),
        conv=np.asarray(gdn_conv)[0].reshape(TAPS, 3 * N_GDN, P).transpose(2, 1, 0).reshape(P, -1),
        fox_q=tiles(fox_q_norm), fox_k=tiles(fox_k_norm), mem_q=tiles(mem_q_norm), mem_k=tiles(mem_k_norm),
        gdn_out=tiles(gdn_out_norm),
        gate_bias=rows(np.concatenate([np.asarray(fox_f_bias)[0], np.asarray(gdn_dt_bias)[0], zeros])),
        gate_sign=rows(np.concatenate([-ones, ones, -ones])),
        a_log=rows(np.asarray(gdn_a_log)[0]),
        gate_w=gate_cols.reshape(KD, P, NG).transpose(1, 0, 2).reshape(P, -1))
    a["const"] = CONST_ARRAY
    a["par"] = np.ascontiguousarray(np.concatenate([parts[n] for n in PAR], 1))
    nc = bacc.Bacc("TRN2", target_bir_lowering=False, num_devices=1)
    args = [nc.dram_tensor(f"in_{n}", v.shape, mybir.dt.from_np(v.dtype), kind="ExternalInput").ap()
            for n, v in a.items()]
    out = nc.dram_tensor("out", (SEQ, D_MODEL), F32, kind="ExternalOutput").ap()
    build(nc, *args, out)
    r = run_bass_kernel_spmd(nc, [{f"in_{n}": v for n, v in a.items()}], core_ids=[0])
    return r.results[0]["out"].reshape(1, SEQ, D_MODEL)
```

```python
from contextlib import ExitStack

import numpy as np

import concourse.bass as bass
from concourse import mybir

F32 = mybir.dt.float32
F32R = mybir.dt.float32r
BF16 = mybir.dt.bfloat16
ALU = mybir.AluOpType
ACT = mybir.ActivationFunctionType
AX = mybir.AxisListType

P = 128
D_MODEL = 2048
SEQ = 512
MEM_LEN = 256
HD = 128
CHUNK = 64
N_MEM, N_FOX, N_GDN = 4, 6, 6
FOX_W, GDN_W, MEM_W = N_FOX * HD, N_GDN * HD, N_MEM * HD
FF = 5632
TAPS = 4
EPS = 1e-6
SCALE = HD ** -0.5
KD = D_MODEL // P
TT = SEQ // P
MT = MEM_LEN // P
NCH = SEQ // CHUNK

C_FOX = 0
C_FF = 3 * FOX_W
C_GDN = C_FF + N_FOX
C_Z = C_GDN + 3 * GDN_W
C_GA = C_Z + GDN_W
C_MQ = C_GA + 2 * N_GDN
NG = N_FOX + 2 * N_GDN

MIX_FOX, MIX_GDN, MIX_MEM = 0, N_FOX, N_FOX + N_GDN

GROUPS = [("z", 0), ("z", 1)] + [("mem", h) for h in range(N_MEM)] + \
         [("gdn", h) for h in range(N_GDN)] + [("fox", h) for h in range(N_FOX)]
HEADS = GROUPS[2:]
N_GROUPS = len(GROUPS)
UPG = KD // 2
VPG = 2 * UPG
OUT_UNIT0 = N_GROUPS * UPG
N_CG = D_MODEL // 512
FFN_UNIT0 = OUT_UNIT0 + N_CG * UPG
N_CHUNKS = FF // 512
UPC = 3 * UPG
RAW = 3
SPL = 3
AHEAD = SPL - 1
TURN_V, PV_V = 12, 13
assert UPC % RAW == 0 and UPC % SPL == 0

CONST = {}


def const_array():
    t = np.arange(P)
    half = t // CHUNK
    same = half[:, None] == half[None, :]
    le = t[:, None] <= t[None, :]
    r, c = t[:, None] % CHUNK, np.arange(CHUNK)[None, :]
    parts = {
        "eps": np.full((P, 1), EPS),
        "ident": np.eye(P),
        "ones": np.ones((P, P)),
        "cum": same & le,
        "suffix": same & ~le,
        "sel0": np.repeat(half[:, None] == 0, P, 1),
        "sel1": np.repeat(half[:, None] == 1, P, 1),
        "negcum": -(le.astype(float)),
        "negall": -np.ones((P, P)),
        "causal": np.where(t[None, :] <= t[:, None], 0.0, -1e30),
        "ident64": r == c,
        "neg64": np.where(r <= c, 0.0, -1e30),
    }
    for l in range(6):
        s = 1 << l
        parts[f"pair{l}"] = (r // (2 * s) == c // (2 * s)) & (r % (2 * s) < s) & (c % (2 * s) >= s)
    at = 0
    for name, a in parts.items():
        CONST[name] = (at, at + a.shape[1])
        at += a.shape[1]
    return np.concatenate([np.asarray(a, np.float32) for a in parts.values()], 1)


CONST_ARRAY = const_array()
PAR = {}
_at = 0
for _name, _n in (("norm_mix", KD), ("mem_norm", KD), ("norm_ffn", KD), ("conv", 3 * N_GDN * TAPS),
                  ("fox_q", 1), ("fox_k", 1), ("mem_q", 1), ("mem_k", 1), ("gdn_out", 1),
                  ("gate_bias", 1), ("gate_sign", 1), ("a_log", 1), ("gate_w", KD * NG)):
    PAR[_name] = (_at, _at + _n)
    _at += _n
N_PAR = _at


def build(nc, x, mem, w_in, w_mem_kv, w_out, w_gate_up, w_down, const, par, out):
    ctx = ExitStack()
    with ctx:
        at = [17 * 1024]

        def place(name, cols, dt=F32, offset=None):
            if offset is None:
                offset = at[0]
                at[0] += -(-4 * cols // 32) * 32
            return nc.alloc_sbuf_tensor_at(name, [P, cols], dt, offset=offset)

        x_hi = place("x_hi", KD * SEQ, F32R)[:, :].rearrange("p (k t) -> p k t", k=KD)
        x_lo = place("x_lo", KD * SEQ, F32R)[:, :].rearrange("p (k t) -> p k t", k=KD)
        w_raw = place("w_raw", RAW * 1024)
        w_hi = place("w_hi", SPL * 1024, F32R)
        w_lo = place("w_lo", SPL * 1024, F32R)
        mix_at = at[0]
        mix = place("mix", KD * SEQ)[:, :].rearrange("p (k t) -> p k t", k=KD)
        um_hi = place("um_hi", KD * MEM_LEN, F32R, mix_at)[:, :].rearrange("p (k t) -> p k t", k=KD)
        wg_hi = place("wg_hi", KD * NG, F32R, mix_at + 8 * 2048)[:, :].rearrange("p (k c) -> p k c", k=KD)
        wg_lo = place("wg_lo", KD * NG, F32R, mix_at + 9 * 2048)[:, :].rearrange("p (k c) -> p k c", k=KD)
        act_hi = place("act_hi", 4 * SEQ, F32R, mix_at)[:, :].rearrange("p (f t) -> p f t", f=4)
        act_lo = place("act_lo", 4 * SEQ, F32R, mix_at + 8192)[:, :].rearrange("p (f t) -> p f t", f=4)
        silu_gate = place("silu_gate", 4 * SEQ, F32, mix_at + 16384)
        res_at = at[0]
        res_t = place("residual", TT * D_MODEL)
        resid = res_t[:, :].rearrange("p (t c) -> p t c", t=TT)
        um_lo = place("um_lo", KD * MEM_LEN, F32R, res_at)[:, :].rearrange("p (k t) -> p k t", k=KD)
        SCAN = 4 * SEQ + 256
        scan_b = [res_t[:, b * SCAN:(b + 1) * SCAN] for b in range(2)]
        sc_u = [s[:, 0:512].rearrange("p (t d) -> p t d", t=TT) for s in scan_b]
        sc_nw = [s[:, 512:1024] for s in scan_b]
        sc_qg = [s[:, 1024:1536] for s in scan_b]
        sc_kd = [s[:, 1536:2048].rearrange("p (t d) -> p t d", t=TT) for s in scan_b]
        sc_at = [s[:, 2048:2304].rearrange("p (t c) -> p t c", t=TT) for s in scan_b]
        zg = res_t[:, 2 * SCAN:2 * SCAN + N_GDN * SEQ].rearrange("p (h t) -> p h t", h=N_GDN)
        state = res_t[:, 7680:7808]
        v_new = res_t[:, 7808:7936]
        WORK = 1548 + 1536 + 3840
        work = place("work", WORK)
        cin = work[:, 0:1545].rearrange("p (s c) -> p s c", s=3)
        sq = work[:, 0:1024].rearrange("p (s t) -> p s t", s=2)
        qkv = work[:, 1548:3084].rearrange("p (s t) -> p s t", s=3)
        tmp = work[:, 3084:6924]
        coup = tmp[:, 0:1280].rearrange("p (l t c) -> p l t c", l=5, t=TT)
        inv = tmp[:, 1280:1792].rearrange("p (w t c) -> p w t c", w=2, t=TT)
        yb = tmp[:, 1792:2048].rearrange("p (t c) -> p t c", t=TT)
        lt = tmp[:, 2048:2304].rearrange("p (t c) -> p t c", t=TT)
        dec = tmp[:, 2304:2816].rearrange("p (w t c) -> p w t c", w=2, t=TT)
        vb = tmp[:, 2816:3328].rearrange("p (t d) -> p t d", t=TT)
        kbg = tmp[:, 3328:3840].rearrange("p (t d) -> p t d", t=TT)
        pr = tmp[:, 0:1280]
        pt = tmp[:, 1280:2560]
        vtok = tmp[:, 2560:3072].rearrange("p (t d) -> p t d", t=TT)
        ncb = tmp[:, 3072:3584]
        mem_in = work[:, 1548:1548 + 2 * D_MODEL].rearrange("p (t c) -> p t c", t=MT)
        diag = work[:, 0:TT * P].rearrange("p (t c) -> p t c", t=TT)
        gz = tmp[0:NG, 0:SEQ]
        gl = tmp[0:NG, SEQ:2 * SEQ]
        GL, GC, NC = 0, 32, 64
        N_ROWS = NC + NG
        rows_hi = place("rows_hi", SEQ, F32R)
        rows_lo = place("rows_lo", SEQ, F32R)
        pick = place("pick", 2 * P, F32R)[:, :].rearrange("p (w c) -> p w c", w=2)

        NC_ = CONST_ARRAY.shape[1]
        cst = place("cst", NC_)
        K = {n: cst[:, a:b] for n, (a, b) in CONST.items()}
        prm = place("prm", N_PAR)
        A = {n: prm[:, a:b] for n, (a, b) in PAR.items()}
        conv_w = A["conv"].rearrange("p (s h j) -> p s h j", s=3, h=N_GDN)
        identb = nc.alloc_sbuf_tensor_at("identb", [P, P], BF16, offset=at[0])
        causalb = nc.alloc_sbuf_tensor_at("causalb", [P, P], BF16, offset=at[0] + 256)
        at[0] += 512
        small_t = place("small", 400)
        small_at = [0]

        def small(n):
            small_at[0] += n
            assert small_at[0] <= 400
            return small_t[:, small_at[0] - n:small_at[0]]

        ga = small(TT * NG).rearrange("p (t c) -> p t c", t=TT)
        coef = small(1)
        gsum = small(4 * TT * N_GDN)
        n4 = TT * N_GDN
        ngc = small(n4).rearrange("p (t h) -> p t h", t=TT)
        kdf = small(n4).rearrange("p (t h) -> p t h", t=TT)
        beta = small(n4).rearrange("p (t h) -> p t h", t=TT)
        beg = small(n4).rearrange("p (t h) -> p t h", t=TT)
        egl = small(2 * n4).rearrange("p (j t h) -> p j t h", j=2, t=TT)
        ssx = small(4)
        rx = small(4)
        ssm = small(2)
        rm = small(2)
        mx = small(4)
        nmx = small(4)
        rsum = small(4)
        rrec = small(4)
        oss = small(4)
        orn = small(4)
        ss2 = small(TT * N_CG).rearrange("p (t g) -> p t g", t=TT)
        ss2s = small(4)
        r2 = small(4)
        comb = small(2)
        scratch = mix.rearrange("p k t -> p (k t)")[:, 10 * SEQ:10 * SEQ + D_MODEL]
        assert at[0] <= 224 * 1024
        psum = ctx.enter_context(nc.psum_tensor("psum", [P, 8 * 512], F32))
        bank = [psum[:, 512 * b:512 * b + 512] for b in range(8)]
        set_a, set_b = psum[:, 0:2048], psum[:, 2048:4096]
        S1, S2, T = bank[3], bank[7], bank[4:7]

        sems = {}

        def sem(name):
            if name not in sems:
                sems[name] = ctx.enter_context(nc.semaphore(name))
            return sems[name]

        raw_ready = [sem(f"raw_ready{i}") for i in range(RAW)]
        hi_done, lo_done, unit_done = sem("hi_done"), sem("lo_done"), sem("unit_done")
        group_sums = sem("group_sums")
        bank_taken = [sem(f"bank{s}_taken") for s in range(3)]

        w_in3 = {"gdn": w_in[:, C_GDN:C_GDN + 3 * GDN_W].rearrange("(k p) (s h c) -> p k s h c", p=P, s=3, h=N_GDN),
                 "fox": w_in[:, C_FOX:C_FOX + 3 * FOX_W].rearrange("(k p) (s h c) -> p k s h c", p=P, s=3, h=N_FOX)}
        w_in2 = w_in.rearrange("(k p) c -> p k c", p=P)
        w_kv = w_mem_kv.rearrange("(k p) (s h c) -> p k s h c", p=P, s=2, h=N_MEM)
        w_out_v = w_out.rearrange("(k p) c -> p k c", p=P)
        w_gu_v = w_gate_up.rearrange("(k p) c -> p k c", p=P)
        w_dn_v = w_down.rearrange("(f k p) c -> f p k c", p=P, k=2)
        MIX_ORDER = [6, 7, 8, 9, 10, 11, 12, 13, 14, 15, 0, 1, 2, 3, 4, 5]

        def raw_loads(u):
            s = w_raw[:, (u % RAW) * 1024:(u % RAW) * 1024 + 1024]
            if u >= OUT_UNIT0:
                cg, kk = divmod(u - OUT_UNIT0, UPG)
                k0 = MIX_ORDER[2 * kk]
                return [(s.rearrange("p (k c) -> p k c", k=2), w_out_v[:, k0:k0 + 2, 512 * cg:512 * cg + 512])]
            g, kk = divmod(u, UPG)
            kind, h = GROUPS[g]
            ks = slice(2 * kk, 2 * kk + 2)
            s = s[:, 0:768].rearrange("p (k s c) -> p k s c", k=2, s=3)
            if kind == "z":
                return [(s.rearrange("p k s c -> p k (s c)"), w_in2[:, ks, C_Z + 384 * h:C_Z + 384 * h + 384])]
            if kind == "mem":
                return [(s[:, :, 0, :], w_in2[:, ks, C_MQ + HD * h:C_MQ + HD * h + HD])] + \
                       [(s[:, k, 1:3, :], w_kv[:, 2 * kk + k, :, h, :]) for k in range(2)]
            return [(s[:, k, :, :], w_in3[kind][:, 2 * kk + k, :, h, :]) for k in range(2)]

        resid_added = sem("resid_added")
        LOOP_J = 2 * UPG

        def ffn_slot(jj, n):
            return (FFN_UNIT0 + jj) % n

        raw_count = [0] * RAW
        raw_at = []
        for u in range(FFN_UNIT0):
            raw_count[u % RAW] += 16 * len(raw_loads(u))
            raw_at.append(raw_count[u % RAW])

        def ffn_raw_at(jj):
            s = ffn_slot(jj, RAW)
            return raw_count[s] + 16 * sum(ffn_slot(i, RAW) == s for i in range(jj + 1))

        def unit_cols(u):
            return 768 if u < OUT_UNIT0 else 1024

        def head_visit(t):
            out_ = []
            for n, (kind, h) in enumerate(HEADS):
                v = t - VPG * (n + 3)
                last = {"mem": 16, "fox": 16, "gdn": 53}[kind]
                if 0 <= v < last:
                    out_.append((n, kind, h, v))
            return out_

        LAST_VISIT = VPG * N_GROUPS + 16

        def banks_taken(eng, groups):
            for s in range(3):
                eng.wait_ge(bank_taken[s], groups)

        def qkv_free(eng, n):
            if n == 0:
                return
            kind, h = HEADS[n - 1]
            if kind == "gdn":
                eng.wait_ge(sem("tok_ready"), n)
                eng.wait_ge(sem("qg_ready"), h + 1)
            else:
                eng.wait_ge(sem(kind + "_scores"), (2 if kind == "mem" else 3) * (h + 1))

        def bcl(ap, n):
            return ap.unsqueeze(2).to_broadcast([ap.shape[0], ap.shape[1], n])

        block = ctx.enter_context(nc.Block())

        @block.sync
        def _(sp):
            x_v = x.rearrange("(t p) c -> p t c", p=P)
            for t in range(TT):
                sp.dma_start(resid[:, t, :], x_v[:, t, :]).then_inc(sem(f"x_in{t}"), 16)
            for u in range(FFN_UNIT0):
                if u >= RAW:
                    sp.wait_ge(lo_done, u - RAW + 1)
                for dst, src in raw_loads(u):
                    sp.dma_start(dst, src).then_inc(raw_ready[u % RAW], 16)

            def load(base, jj, src):
                slot = ffn_slot(jj, RAW)
                sp.wait_ge(lo_done, base - RAW + 1)
                s = w_raw[:, slot * 1024:slot * 1024 + 1024].rearrange("p (k c) -> p k c", k=2)
                sp.dma_start(s, src).then_inc(raw_ready[slot], 16)

            def gate_up(u0, jj, c, up):
                for kk in range(UPG):
                    load(u0 + kk, jj + kk, w_gu_v[:, 2 * kk:2 * kk + 2, bass.ds(c * 512 + (FF if up else 0), 512)])

            def down(u0, jj, c):
                for j in range(2 * N_CG):
                    cg, kk = divmod(j, 2)
                    load(u0 + j, jj + j, w_dn_v[bass.ds(c * 2 + kk, 1), :, :, 512 * cg:512 * cg + 512]
                         .rearrange("f p k c -> (f p) k c"))

            gate_up(FFN_UNIT0, 0, 0, False)
            gate_up(FFN_UNIT0 + UPG, UPG, 0, True)
            with sp.Fori(1, N_CHUNKS) as c:
                u0 = FFN_UNIT0 + c * UPC - UPG
                gate_up(u0, LOOP_J, c, False)
                down(u0 + UPG, LOOP_J + UPG, c - 1)
                gate_up(u0 + 2 * UPG, LOOP_J + 2 * UPG, c, True)
            down(FFN_UNIT0 + N_CHUNKS * UPC - UPG, LOOP_J, N_CHUNKS - 1)
            out_v = out.rearrange("(t p) c -> p t c", p=P)
            for cg in range(N_CG - 1):
                sp.wait_ge(resid_added, N_CG * N_CHUNKS + cg + 1)
                sp.dma_start(out_v[:, :, 512 * cg:512 * cg + 512],
                             resid[:, :, 512 * cg:512 * cg + 512]).then_inc(sem("out_done"), 16)
            for t in range(TT):
                sp.wait_ge(sem("tail_added"), t + 1)
                sp.dma_start(out_v[:, t, 512 * (N_CG - 1):], resid[:, t, 512 * (N_CG - 1):]) \
                    .then_inc(sem("out_done"), 16)
            sp.wait_ge(sem("out_done"), 16 * (N_CG - 1 + TT))

        @block.tensor
        def _(pe):
            mm = nc.tensor.matmul

            def mm3(dst, ahi, alo, bhi, blo, first, last):
                mm(dst, ahi, bhi, start=first, stop=False)
                mm(dst, ahi, blo, start=False, stop=False)
                return mm(dst, alo, bhi, start=False, stop=last)

            def w_tiles(slot, a, b):
                return w_hi[:, slot * 1024 + a:slot * 1024 + b], w_lo[:, slot * 1024 + a:slot * 1024 + b]

            def turn_scaled(dst, k, t):
                return mm(dst[:, t * P:t * P + P], resid[:, t, k * P:k * P + P], diag[:, t, :], start=True, stop=True)

            def x_transpose(k):
                pe.wait_ge(sem("x_split"), k - 4)
                for t in range(TT):
                    last = turn_scaled(bank[3 + k % 5], k, t)
                last.then_inc(sem("x_turned"), 1)

            def mem_transpose(j):
                if j < 5:
                    pe.wait_ge(sem("x_split"), KD)
                else:
                    pe.wait_ge(sem("mem_split"), 2 * (j - 4))
                for i in range(2):
                    for t in range(MT):
                        k = 2 * j + i
                        last = nc.tensor.transpose(bank[3 + j % 5][:, i * 256 + t * P:i * 256 + t * P + P],
                                                   mem_in[:, t, k * P:k * P + P], K["ident"])
                last.then_inc(sem("mem_turned"), 1)

            def gates():
                pe.wait_ge(sem("gate_w_split"), 1)
                pe.wait_ge(sem("mem_split"), KD)
                for k in range(KD):
                    last = mm3(bank[3][0:NG, :], wg_hi[:, k, :], wg_lo[:, k, :], x_hi[:, k, :], x_lo[:, k, :],
                               k == 0, k == KD - 1)
                last.then_inc(sem("gates_ready"), 1)

            def gates_turn():
                pe.wait_ge(sem("gate_logs"), 1)
                for t in range(TT):
                    last = nc.tensor.transpose(bank[4][:, t * NG:t * NG + NG], gl[:, t * P:t * P + P],
                                               K["ident"][0:NG, 0:NG])
                last.then_inc(sem("gates_turned"), 1)

            def gate_sums():
                pe.wait_ge(sem("gates_by_token"), 1)
                pe.wait_ge(sem("const_in"), 16)
                g = ga[:, :, N_FOX:N_FOX + N_GDN]
                for i, name in enumerate(("cum", "suffix", "sel0", "sel1")):
                    last = mm(bank[5][:, i * n4:i * n4 + n4].rearrange("p (t h) -> p t h", t=TT), K[name], g,
                              start=True, stop=True)
                last.then_inc(sem("gate_sums"), 1)
                for t in range(TT):
                    last = mm(bank[6][GC:GC + NG, t * P:t * P + P], ga[:, t, :], K["cum"], start=True, stop=True)
                for j in range(TT):
                    for t in range(j + 1):
                        last = mm(bank[7][NC:NC + NG, j * P:j * P + P], ga[:, t, :], K["negall" if t < j else "negcum"],
                                  start=(t == 0), stop=(t == j))
                last.then_inc(sem("gate_sum_rows"), 1)

            def spread(dst, w):
                mm(dst, pick[0:N_ROWS, w, :], rows_hi[0:N_ROWS, :], start=True, stop=False)
                return mm(dst, pick[0:N_ROWS, w, :], rows_lo[0:N_ROWS, :], start=False, stop=True)

            def unit_half(u, half):
                g, kk = divmod(u, UPG)
                slot = u % SPL
                k = 2 * kk + half
                if half == 0:
                    pe.wait_ge(lo_done, u + 1)
                if u >= OUT_UNIT0:
                    cg, kk = divmod(u - OUT_UNIT0, UPG)
                    k = MIX_ORDER[2 * kk + half]
                    pe.wait_ge(sem("mix_split"), 2 * kk + half + 1)
                    if kk == 0 and half == 0:
                        if cg == 0:
                            banks_taken(pe, N_GROUPS)
                            pe.wait_ge(sem("gdn_mixed"), N_GDN)
                        elif cg == 1:
                            pe.wait_ge(sem("fox_mixed"), N_FOX)
                        else:
                            pe.wait_ge(resid_added, cg - 1)
                    hi, lo = w_tiles(slot, half * 512, half * 512 + 512)
                    for t in range(TT):
                        last = mm3(bank[4 * (cg % 2) + t], x_hi[:, k, t * P:t * P + P], x_lo[:, k, t * P:t * P + P],
                                   hi, lo, kk == 0 and half == 0, kk == UPG - 1 and half == 1)
                        if u == FFN_UNIT0 - 1 and half == 1 and t < TT - 1:
                            last.then_inc(sem("last_out_sums"), 1)
                    if half == 1:
                        last.then_inc(unit_done, 1)
                    return
                kind, h = GROUPS[g]
                for s, i in ((0, 0), (0, 1), (1, 0)) if half == 0 else ((1, 1), (2, 0), (2, 1)):
                    k = 2 * kk + i
                    if kk == 0 and i == 0 and g > 0:
                        pe.wait_ge(bank_taken[s], g)
                    if g == 0 and s == 0:
                        pe.wait_ge(sem("x_split"), k + 1)
                    hi, lo = w_tiles(slot, i * 384 + s * P, i * 384 + s * P + P)
                    bhi, blo, dst = x_hi[:, k, :], x_lo[:, k, :], bank[s]
                    if kind == "mem" and s > 0:
                        bhi, blo, dst = um_hi[:, k, :], um_lo[:, k, :], bank[s][:, 0:MEM_LEN]
                    last = mm3(dst, hi, lo, bhi, blo, k == 0, k == KD - 1)
                    if k == KD - 1 and s < 2:
                        last.then_inc(group_sums, 1)
                if half == 1:
                    last.then_inc(unit_done, 1)

            def halves():
                for i in range(TT):
                    for a in range(2):
                        yield i, slice(64 * a, 64 * a + 64)

            def banks_free(n):
                if n == 0:
                    pe.wait_ge(sem("gate_sums_read"), 1)
                    pe.wait_ge(sem("rows_lo_done"), 3)
                elif HEADS[n - 1][0] == "gdn":
                    pe.wait_ge(sem("uw_taken"), 2 * (HEADS[n - 1][1] + 1))
                else:
                    pe.wait_ge(sem(HEADS[n - 1][0] + "_mixed"), HEADS[n - 1][1] + 1)

            def norms(n, kind):
                pe.wait_ge(sem("sq_ready"), n + 1)
                mm(T[0], K["ones"], sq[:, 0, :], start=True, stop=True)
                nk = MEM_LEN if kind == "mem" else SEQ
                mm(T[1][:, 0:nk], K["ones"], sq[:, 1, 0:nk], start=True, stop=True).then_inc(sem("ssq_ready"), 1)

            def mem_side(n, h, v):
                if v == 5:
                    banks_free(n)
                    norms(n, "mem")
                if v == 7:
                    for t in range(MT):
                        last = nc.tensor.transpose(T[2][:, t * P:t * P + P], qkv[:, 2, t * P:t * P + P], K["ident"])
                    last.then_inc(sem("tok_ready"), 1)
                if v in (8, 9):
                    if v == 8:
                        pe.wait_ge(sem("qn_ready"), n + 1)
                        pe.wait_ge(sem("kn_ready"), n + 1)
                    j0 = 2 * (v - 8)
                    for j in (j0, j0 + 1):
                        last = mm(T[v - 8][:, (j - j0) * 256:(j - j0) * 256 + 256], qkv[:, 0, j * P:j * P + P],
                                  qkv[:, 1, 0:MEM_LEN], start=True, stop=True)
                    last.then_inc(sem("mem_scores"), 1)
                if v == TURN_V:
                    pe.wait_ge(sem("mem_probs"), h + 1)
                    for i in range(MT):
                        for j in range(TT):
                            last = nc.tensor.transpose(T[i][:, j * P:j * P + P], pr[:, j * 256 + i * P:j * 256 + i * P + P],
                                                       K["ident"])
                        last.then_inc(sem("mem_turned_p"), 1)
                if v == PV_V:
                    pe.wait_ge(sem("mem_pt0"), h + 1)
                    pe.wait_ge(sem("mem_pt1"), h + 1)
                    pe.wait_ge(sem("vtok_ready"), h + 1)
                    for i in range(MT):
                        last = mm(T[2], vtok[:, i, :], pt[:, i * 512:i * 512 + 512], start=(i == 0), stop=(i == MT - 1))
                    last.then_inc(sem("mem_pv"), 1)

            def fox_side(n, h, v):
                if v == 5:
                    banks_free(n)
                    if h <= 2:
                        pe.wait_ge(sem("gdn_mixed"), h + 4)
                    pe.wait_ge(sem("picks_ready"), 2 * N_GDN + h + 1)
                    spread(T[2], 0).then_inc(sem("negc_ready"), 1)
                    norms(n, "fox")
                if v == 7:
                    pe.wait_ge(sem("ncb_ready"), h + 1)
                    for t in range(TT):
                        last = nc.tensor.transpose(T[2][:, t * P:t * P + P], qkv[:, 2, t * P:t * P + P], K["ident"])
                    last.then_inc(sem("tok_ready"), 1)
                if v in (8, 9, 10):
                    if v == 8:
                        pe.wait_ge(sem("qn_ready"), n + 1)
                        pe.wait_ge(sem("kn_ready"), n + 1)
                        pe.wait_ge(sem("bf_consts"), 2)
                    if v == 10:
                        pe.wait_ge(sem("vtok_ready"), N_MEM + h + 1)
                    for j, b, c0 in {8: ((0, 0, 0), (1, 0, 128)), 9: ((2, 1, 0),), 10: ((3, 2, 0),)}[v]:
                        w = (j + 1) * P
                        mm(T[b][:, c0:c0 + w], qkv[:, 0, j * P:j * P + P], qkv[:, 1, 0:w], start=True, stop=False)
                        last = mm(T[b][:, c0 + j * P:c0 + w], identb[:, :], causalb[:, :], start=False, stop=True)
                    last.then_inc(sem("fox_scores"), 1)
                if v == TURN_V:
                    pe.wait_ge(sem("fox_probs"), h + 1)
                    off = [0, 128, 384, 768]
                    for b, blocks in ((0, ((0, 0),)), (1, ((1, 0),)), (2, ((2, 0), (3, 256)))):
                        for i, c0 in blocks:
                            for j in range(i, TT):
                                last = nc.tensor.transpose(T[b][:, c0 + (j - i) * P:c0 + (j - i + 1) * P],
                                                           pr[:, off[j] + i * P:off[j] + i * P + P], K["ident"])
                        last.then_inc(sem(f"fox_turned{b}"), 1)
                if v == PV_V:
                    pe.wait_ge(sem("fox_pt0"), h + 1)
                    pe.wait_ge(sem("fox_pt1"), h + 1)
                    pe.wait_ge(sem("fox_pt2"), h + 1)
                    offp = [0, 512, 896, 1152]
                    for i in range(TT):
                        last = mm(T[2][:, i * P:], vtok[:, i, :], pt[:, offp[i]:offp[i] + SEQ - i * P],
                                  start=(i == 0), stop=(i == TT - 1))
                    last.then_inc(sem("fox_pv"), 1)

            def gdn_side(n, h, v):
                b = h % 2
                if v == 5:
                    banks_free(n)
                    if h >= 3:
                        pe.wait_ge(sem("gdn_mixed"), h - 2)
                    pe.wait_ge(sem("picks_ready"), 2 * h + 2)
                    spread(T[2], 0).then_inc(sem("gc_rows"), 1)
                    norms(n, "gdn")
                if v == 6:
                    pe.wait_ge(sem("gc_taken"), h + 1)
                    spread(T[2], 1).then_inc(sem("gcb_rows"), 1)
                if v == 7:
                    pe.wait_ge(sem("qn_ready"), n + 1)
                    pe.wait_ge(sem("kn_ready"), n + 1)
                    for i, s in halves():
                        c = i * P + s.start
                        mm(T[0][s, i * 64:i * 64 + 64], qkv[:, 1, c:c + 64], qkv[:, 1, c:c + 64], start=True, stop=True)
                        last = mm(T[0][s, 256 + i * 64:320 + i * 64], qkv[:, 1, c:c + 64], qkv[:, 0, c:c + 64],
                                  start=True, stop=True)
                    last.then_inc(sem("gram_ready"), 1)
                    for i in range(TT):
                        last = nc.tensor.transpose(T[1][:, i * P:i * P + P], qkv[:, 1, i * P:i * P + P], K["ident"])
                    last.then_inc(sem("ktok_ready"), 1)
                    pe.wait_ge(sem("dec_arg"), h + 1)
                    for i in range(TT):
                        last = nc.tensor.transpose(T[2][:, i * P:i * P + P], qkv[:, 2, i * P:i * P + P], K["ident"])
                    last.then_inc(sem("tok_ready"), 1)
                if v == 8:
                    pe.wait_ge(sem("inv0_ready"), h + 1)
                    for i, s in halves():
                        last = mm(T[0][s, i * 64:i * 64 + 64], inv[s, 1, i, :], K["ident64"][s, :], start=True, stop=True)
                    last.then_inc(sem("inv0_turned"), 1)
                for l in range(1, 6):
                    if v == 7 + 2 * l:
                        pe.wait_ge(sem("coup_ready"), 5 * h + l)
                        if l == 1:
                            pe.wait_ge(sem("inv0_copied"), h + 1)
                            pe.wait_ge(sem("k_scaled"), h + 1)
                        else:
                            pe.wait_ge(sem("inv_updated"), 5 * h + l - 1)
                        for i, s in halves():
                            last = mm(T[1][s, i * 64:i * 64 + 64], coup[s, l - 1, i, :], inv[s, 0, i, :],
                                      start=True, stop=True)
                        last.then_inc(sem("y_ready"), 1)
                    if v == 8 + 2 * l:
                        pe.wait_ge(sem("y_copied"), 5 * h + l)
                        for i, s in halves():
                            if l < 5:
                                mm(T[0][s, i * 64:i * 64 + 64], inv[s, 1, i, :], yb[s, i, :], start=True, stop=True)
                            last = mm(T[0][s, 256 + i * 64:320 + i * 64], yb[s, i, :], inv[s, 1, i, :],
                                      start=True, stop=True)
                        last.then_inc(sem("xy_ready"), 1)
                if v == 19:
                    pe.wait_ge(sem("inv_updated"), 5 * h + 5)
                    pe.wait_ge(sem("v_scaled"), h + 1)
                    for i, s in halves():
                        last = mm(T[1][s, i * P:i * P + P], inv[s, 1, i, :], vb[s, i, :], start=True, stop=True)
                    last.then_inc(sem("u_ready"), 1)
                    for i, s in halves():
                        last = mm(T[2 - s.start // 32][:, i * 64:i * 64 + 64], kbg[s, i, :], inv[s, 1, i, :],
                                  start=True, stop=True)
                    last.then_inc(sem("w_ready"), 1)
                if 21 <= v < 21 + 2 * NCH:
                    c, second = divmod(v - 21, 2)
                    i, s = c // 2, slice(64 * (c % 2), 64 * (c % 2) + 64)
                    cols = slice(64 * c, 64 * c + 64)
                    if not second:
                        if c == 0:
                            pe.wait_ge(sem("uw_taken"), 2 * h + 2)
                            pe.wait_ge(sem("state_clear"), h + 1)
                        else:
                            pe.wait_ge(sem("state_new"), (NCH - 1) * h + c)
                        mm(S1[s, 0:P], sc_nw[b][:, cols], state, start=True, stop=True).then_inc(sem("ws_ready"), 1)
                    else:
                        pe.wait_ge(sem("v_new"), NCH * h + c + 1)
                        if c == 0:
                            pe.wait_ge(sem("qg_ready"), h + 1)
                            if h > 0:
                                pe.wait_ge(sem("o_scaled"), h)
                        mm(S2[s, i * P:i * P + P], sc_qg[b][:, cols], state, start=True, stop=False)
                        mm(S2[s, i * P:i * P + P], sc_at[b][s, i, :], v_new[s, :], start=False, stop=True)
                        mm(S1[:, P:2 * P], sc_kd[b][s, i, :], v_new[s, :], start=True, stop=True) \
                            .then_inc(sem("ds_ready"), 1)
                if v == 52:
                    pe.wait_ge(sem("o_scaled"), h + 1)
                    if h + 2 < N_GDN:
                        pe.wait_ge(sem("uw_taken"), 2 * (h + 3))
                    k = MIX_GDN + h
                    for i in range(TT):
                        last = nc.tensor.transpose(T[0][:, i * P:i * P + P], mix[:, k, i * P:i * P + P], K["ident"])
                    last.then_inc(sem("o_turned"), 1)

            for t in range(TT):
                pe.wait_ge(sem("diag_ready"), t + 1)
                for k in range(5):
                    last = turn_scaled(bank[3 + k], k, t)
                    if t == TT - 1:
                        last.then_inc(sem("x_turned"), 1)
            for t in range(LAST_VISIT):
                u, half = divmod(t, 2)
                if u < UPG and half == 0:
                    for k in (2 * u + 4, 2 * u + 5):
                        if 5 <= k < KD:
                            x_transpose(k)
                unit_half(u, half)
                if t == VPG:
                    pe.wait_ge(sem("mem_normed"), MT)
                if VPG <= t < VPG + KD // 2:
                    mem_transpose(t - VPG)
                if t == VPG + 10:
                    gates()
                if t == VPG + 12:
                    gates_turn()
                if t == VPG + 15:
                    gate_sums()
                for n, kind, h, v in head_visit(t):
                    {"mem": mem_side, "gdn": gdn_side, "fox": fox_side}[kind](n, h, v)
            for t in range(LAST_VISIT, 2 * FFN_UNIT0):
                unit_half(t // 2, t % 2)

            for t in range(TT):
                pe.wait_ge(sem("diag_ready"), TT + t + 1)
                for k in range(4):
                    last = turn_scaled(bank[k], k, t)
                    if t == TT - 1:
                        last.then_inc(sem("h_turned"), 1)

            def h_transpose(k):
                if k >= 8:
                    pe.wait_ge(sem("h_split"), k - 3)
                else:
                    pe.wait_ge(resid_added, N_CG)
                for t in range(TT):
                    last = turn_scaled(bank[4 + k % 4], k, t)
                last.then_inc(sem("h_turned"), 1)

            def gate_up(u0, jj, side, peeled=False):
                for kk in range(UPG):
                    if peeled:
                        for k in (2 * kk + 4, 2 * kk + 5):
                            if k < KD:
                                h_transpose(k)
                        if kk == 0:
                            pe.wait_ge(sem("h_split"), 4)
                    pe.wait_ge(lo_done, u0 + kk + 1)
                    for half in range(2):
                        k = 2 * kk + half
                        if peeled:
                            pe.wait_ge(sem("h_split"), k + 1)
                        for s in range(4):
                            hi, lo = w_tiles(ffn_slot(jj + kk, SPL), half * 512 + s * P, half * 512 + s * P + P)
                            last = mm3(bank[4 * side + s], hi, lo, x_hi[:, k, :], x_lo[:, k, :], k == 0, k == KD - 1)
                    last.then_inc(unit_done, 1)

            def down(u0, jj, side, turned=False, tail=False):
                for kk in range(2):
                    pe.wait_ge(lo_done, u0 + kk + 1)
                    slot = ffn_slot(jj + kk, SPL)
                    steps = [(f, t) for f in (2 * kk, 2 * kk + 1) for t in range(TT)]
                    for f, t in sorted(steps, key=lambda ft: ft[1]) if tail and kk == 1 else steps:
                        if turned and t == 0:
                            pe.wait_ge(sem("act_ready"), N_CHUNKS + f)
                        hi, lo = w_tiles(slot, (f % 2) * 512, (f % 2) * 512 + 512)
                        last = mm3(bank[4 * side + t], act_hi[:, f, t * P:t * P + P], act_lo[:, f, t * P:t * P + P],
                                   hi, lo, f == 0, f == 3)
                        if tail and f == 3 and t < TT - 1:
                            last.then_inc(sem("tail_sums"), 1)
                    last.then_inc(unit_done, 1)

            gate_up(FFN_UNIT0, 0, 0, peeled=True)
            gate_up(FFN_UNIT0 + UPG, UPG, 1)
            with pe.Fori(1, N_CHUNKS) as c:
                u0 = FFN_UNIT0 + c * UPC - UPG
                added = c * N_CG
                pe.wait_ge(resid_added, added)
                pe.wait_ge(sem("gate_taken"), c)
                gate_up(u0, LOOP_J, 0)
                pe.wait_ge(sem("act_ready"), c)
                down(u0 + UPG, LOOP_J + UPG, 1)
                pe.wait_ge(sem("gate_taken"), c + 1)
                down(u0 + UPG + 2, LOOP_J + UPG + 2, 0)
                pe.wait_ge(resid_added, added + 1)
                down(u0 + UPG + 4, LOOP_J + UPG + 4, 1)
                pe.wait_ge(resid_added, added + 2)
                down(u0 + UPG + 6, LOOP_J + UPG + 6, 0)
                pe.wait_ge(resid_added, added + 3)
                gate_up(u0 + 2 * UPG, LOOP_J + 2 * UPG, 1)
            u0 = FFN_UNIT0 + N_CHUNKS * UPC - UPG
            added = N_CHUNKS * N_CG
            pe.wait_ge(resid_added, added)
            down(u0, LOOP_J, 0, turned=True)
            down(u0 + 2, LOOP_J + 2, 1)
            pe.wait_ge(resid_added, added + 1)
            down(u0 + 4, LOOP_J + 4, 0)
            pe.wait_ge(resid_added, added + 2)
            down(u0 + 6, LOOP_J + 6, 1, tail=True)

        @block.scalar
        def _(act):
            fn = nc.scalar.activation

            first = CONST["ident"][1]
            act.dma_start(cst[:, 0:first], const[:, 0:first]).then_inc(sem("ident_in"), 16)
            act.dma_start(prm[:, :], par).then_inc(sem("par_in"), 16)

            def hi_half(u):
                if u >= SPL:
                    act.wait_ge(unit_done, u - SPL + 1)
                act.wait_ge(raw_ready[u % RAW], raw_at[u] if u < FFN_UNIT0 else ffn_raw_at(u - FFN_UNIT0))
                n = unit_cols(u)
                fn(w_hi[:, (u % SPL) * 1024:(u % SPL) * 1024 + n], w_raw[:, (u % RAW) * 1024:(u % RAW) * 1024 + n],
                   ACT.Copy).then_inc(hi_done, 1)

            def link(ins):
                chain[0] += 1
                ins.then_inc(sem("act_chain"), 1)
                act.wait_ge(sem("act_chain"), chain[0])

            def inv_root(dst, src, scale):
                link(fn(dst, src, ACT.Ln, scale=scale, bias=eps))
                return fn(dst, dst, ACT.Exp, scale=-0.5)

            chain = [0]
            eps = K["eps"]

            act.wait_ge(sem("ident_in"), 16)
            act.wait_ge(sem("par_in"), 16)
            for t in range(TT):
                act.wait_ge(sem(f"x_in{t}"), 16)
                link(fn(scratch, resid[:, t, :], ACT.Square, accum_out=ssx[:, t:t + 1]))
                inv_root(rx[:, t:t + 1], ssx[:, t:t + 1], 1.0 / D_MODEL).then_inc(sem("rx_ready"), 1)
            act.dma_start(cst[:, first:], const[:, first:]).then_inc(sem("const_in"), 16)
            act.dma_start(mem_in, mem.rearrange("(t p) c -> p t c", p=P)).then_inc(sem("mem_in"), 16)
            hi_half(0)
            hi_half(1)

            def x_split(k):
                act.wait_ge(sem("x_turned"), k + 1)
                fn(x_hi[:, k, :], bank[3 + k % 5], ACT.Copy, scale=A["norm_mix"][:, k:k + 1]).then_inc(sem("x_hi_done"), 1)

            def mem_split(j):
                act.wait_ge(sem("mem_turned"), j + 1)
                for k in (2 * j, 2 * j + 1):
                    fn(um_hi[:, k, :], bank[3 + j % 5][:, (k % 2) * 256:(k % 2) * 256 + 256], ACT.Copy,
                       scale=A["mem_norm"][:, k:k + 1]).then_inc(sem("mem_hi_done"), 1)

            def main_copies(n, kind, h, g):
                if kind == "gdn":
                    act.wait_ge(sem("pads_zero"), h + 1)
                else:
                    qkv_free(act, n)
                for s in range(2):
                    act.wait_ge(group_sums, 2 * g + s + 1)
                    w = MEM_LEN if kind == "mem" and s == 1 else SEQ
                    dst = cin[:, s, 3:] if kind == "gdn" else qkv[:, s, 0:w]
                    fn(dst, bank[s][:, 0:w], ACT.Copy).then_inc(bank_taken[s], 1)

            def squares(n, kind, g):
                for s in range(2):
                    act.wait_ge(bank_taken[s], g + 1)
                if n > 0:
                    act.wait_ge(sem("qn_ready"), n)
                    act.wait_ge(sem("kn_ready"), n)
                if kind == "mem":
                    fn(sq[:, 0, :], qkv[:, 0, :], ACT.Square)
                    fn(sq[:, 1, 0:MEM_LEN], qkv[:, 1, 0:MEM_LEN], ACT.Square).then_inc(sem("sq_ready"), 1)
                else:
                    fn(sq, qkv[:, 0:2, :], ACT.Square).then_inc(sem("sq_ready"), 1)

            def factors(n, kind):
                act.wait_ge(sem("ssq_ready"), n + 1)
                width = SEQ + (MEM_LEN if kind == "mem" else SEQ)
                flat = sq.rearrange("p s t -> p (s t)")[:, 0:width]
                src = psum[:, 2048:2048 + width]
                inv_root(flat, src, 1.0 if kind == "gdn" else 1.0 / HD).then_inc(sem("rn_ready"), 1)

            def mem_side(n, h, v):
                if v == 1:
                    squares(n, "mem", n + 2)
                if v == 5:
                    factors(n, "mem")
                if v == 10:
                    act.wait_ge(sem("mem_max"), h + 1)
                    for j in range(TT):
                        last = fn(pr[:, j * 256:j * 256 + 256], T[j // 2][:, (j % 2) * 256:(j % 2) * 256 + 256], ACT.Exp,
                                  bias=nmx[:, j:j + 1], accum_out=rsum[:, j:j + 1])
                    last.then_inc(sem("mem_exp"), 1)
                if v == TURN_V:
                    act.wait_ge(sem("mem_turned_p"), 2 * h + 1)
                    fn(pt[:, 0:512], T[0], ACT.Copy).then_inc(sem("mem_pt0"), 1)

            def fox_side(n, h, v):
                if v == 1:
                    squares(n, "fox", n + 2)
                if v == 5:
                    act.wait_ge(sem("negc_ready"), h + 1)
                    fn(ncb, T[2], ACT.Copy).then_inc(sem("ncb_ready"), 1)
                    factors(n, "fox")
                if v == 10:
                    act.wait_ge(sem("fox_max"), h + 1)
                    off = [0, 128, 384, 768, 1280]
                    for j in range(TT):
                        last = fn(pr[:, off[j]:off[j + 1]], pr[:, off[j]:off[j + 1]], ACT.Exp,
                                  bias=nmx[:, j:j + 1], accum_out=rsum[:, j:j + 1])
                    last.then_inc(sem("fox_exp"), 1)
                if v == TURN_V:
                    act.wait_ge(sem("fox_turned0"), h + 1)
                    fn(pt[:, 0:512], T[0], ACT.Copy).then_inc(sem("fox_pt0"), 1)
                    act.wait_ge(sem("fox_turned2"), h + 1)
                    fn(pt[:, 896:1280], T[2][:, 0:384], ACT.Copy).then_inc(sem("fox_pt2"), 1)

            def gdn_side(n, h, v):
                b = h % 2
                if v == 2:
                    act.wait_ge(sem("conv_step"), 12 * h + 12)
                    fn(qkv, qkv, ACT.Silu).then_inc(sem("silu_done"), 1)
                    act.wait_ge(sem("silu_done"), h + 1)
                    squares(n, "gdn", n + 2)
                if v == 6:
                    act.wait_ge(sem("dec_arg"), h + 1)
                    fn(dec, dec, ACT.Exp).then_inc(sem("decay"), 1)
                if v == 5:
                    act.wait_ge(sem("gc_rows"), h + 1)
                    if h >= 2:
                        act.wait_ge(sem("ds_ready"), NCH * (h - 1))
                    fn(sc_qg[b], T[2], ACT.Exp).then_inc(sem("qg_exp"), 1)
                    factors(n, "gdn")
                if v == 8:
                    act.wait_ge(sem("inv0_turned"), h + 1)
                    fn(inv[:, 0, :, :].rearrange("p t c -> p (t c)"), T[0][:, 0:256], ACT.Copy) \
                        .then_inc(sem("inv0_copied"), 1)
                for l in range(1, 6):
                    if v == 7 + 2 * l:
                        act.wait_ge(sem("y_ready"), 5 * h + l)
                        fn(yb.rearrange("p t c -> p (t c)"), T[1][:, 0:256], ACT.Copy).then_inc(sem("y_copied"), 1)
                if v == 19:
                    act.wait_ge(sem("u_ready"), h + 1)
                    fn(sc_u[b].rearrange("p t d -> p (t d)"), T[1], ACT.Copy).then_inc(sem("uw_taken"), 1)
                    act.wait_ge(sem("w_ready"), h + 1)
                    for a in range(2):
                        last = fn(sc_nw[b].rearrange("p (t a c) -> p a t c", t=TT, a=2)[:, a],
                                  T[2 - 2 * a][:, 0:256].rearrange("p (t c) -> p t c", t=TT), ACT.Copy, scale=-1.0)
                    last.then_inc(sem("uw_taken"), 1)
                if v == 36:
                    act.wait_ge(sem("ds_ready"), NCH * (h + 1))
                    for i in range(TT):
                        last = fn(mix[:, MIX_GDN + h, i * P:i * P + P], S2[:, i * P:i * P + P], ACT.Square,
                                  accum_out=oss[:, i:i + 1])
                    link(last)
                    inv_root(orn, oss, 1.0 / HD).then_inc(sem("or_ready"), 1)

            def z_side(i):
                for s in range(3):
                    if s < 2:
                        act.wait_ge(group_sums, 2 * i + s + 1)
                    else:
                        act.wait_ge(unit_done, UPG * (i + 1))
                    fn(zg[:, 3 * i + s, :], bank[s], ACT.Silu).then_inc(bank_taken[s], 1)

            def mix_split(j):
                k = MIX_ORDER[j]
                if j == 0:
                    act.wait_ge(unit_done, OUT_UNIT0)
                if k >= MIX_MEM:
                    act.wait_ge(sem("mem_mixed"), N_MEM)
                elif k >= MIX_GDN:
                    act.wait_ge(sem("gdn_mixed"), N_GDN)
                else:
                    act.wait_ge(sem("fox_mixed"), k + 1)
                fn(x_hi[:, k, :], mix[:, k, :], ACT.Copy).then_inc(sem("mix_hi_done"), 1)

            for k in range(4):
                x_split(k)
            for t in range(LAST_VISIT):
                u, half = divmod(t, 2)
                if half == 0 and u < UPG:
                    for k in (2 * u + 4, 2 * u + 5):
                        if k < KD:
                            x_split(k)
                if half == 0:
                    hi_half(u + AHEAD)
                if t == 4:
                    fn(wg_hi.rearrange("p k c -> p (k c)"), A["gate_w"], ACT.Copy).then_inc(sem("gate_w_hi"), 1)
                    act.wait_ge(sem("mem_in"), 16)
                    for m in range(MT):
                        link(fn(scratch, mem_in[:, m, :], ACT.Square, accum_out=ssm[:, m:m + 1]))
                    inv_root(rm, ssm, 1.0 / D_MODEL).then_inc(sem("rm_ready"), 1)
                if t in (VPG - 1, 2 * VPG - 1):
                    z_side(t // VPG)
                g = (t + 1) // VPG - 1
                if (t + 1) % VPG == 0 and 2 <= g < N_GROUPS:
                    main_copies(g - 2, *GROUPS[g], g)
                if VPG <= t < VPG + KD // 2:
                    mem_split(t - VPG)
                if t == VPG + 11:
                    fn(coef, A["a_log"], ACT.Exp).then_inc(sem("rates"), 1)
                    act.wait_ge(sem("gate_abs"), 1)
                    link(fn(gl, gl, ACT.Exp, scale=-1.0))
                    act.wait_ge(sem("const_in"), 16)
                    fn(gl, gl, ACT.Ln, bias=K["ones"][0:NG, 0:1]).then_inc(sem("gate_ln"), 1)
                if t == VPG + 15:
                    act.wait_ge(sem("rows_zero"), 2)
                    act.wait_ge(sem("gate_sum_rows"), 1)
                    for r, src in ((GL, gl), (GC, bank[6][GC:GC + NG, :]), (NC, bank[7][NC:NC + NG, :])):
                        fn(rows_hi[r:r + NG, :], src, ACT.Copy).then_inc(sem("rows_hi_done"), 1)
                    act.wait_ge(sem("gate_sums_read"), 1)
                    gs = gsum.rearrange("p (i t h) -> p i t h", i=4, t=TT)
                    fn(kdf, gs[:, 1], ACT.Exp)
                    fn(egl, gs[:, 2:4], ACT.Exp)
                    fn(beta, ga[:, :, N_FOX + N_GDN:], ACT.Exp)
                    act.wait_ge(sem("beg_arg"), 1)
                    fn(beg, beg, ACT.Exp).then_inc(sem("gate_exps"), 1)
                if t >= VPG * N_GROUPS and t % 2 == 0:
                    kk = (t - VPG * N_GROUPS) // 2
                    for j in range(2 * kk + 2 if kk else 0, min(2 * kk + 4, KD - 1)):
                        mix_split(j)
                for n, kind, h, v in head_visit(t):
                    {"mem": mem_side, "gdn": gdn_side, "fox": fox_side}[kind](n, h, v)
                if t == VPG * (N_GROUPS - 1):
                    act.wait_ge(sem("gdn_mixed"), N_GDN)
                    act.dma_start(resid, x.rearrange("(t p) c -> p t c", p=P)).then_inc(sem("resid_in"), 16)
            mix_split(KD - 1)

            def part_squares(cg):
                act.wait_ge(sem("mix_split"), KD)
                if cg > 0:
                    act.wait_ge(sem("part_sq"), TT * cg)
                for t in range(TT):
                    if cg == N_CG - 1 and t < TT - 1:
                        act.wait_ge(sem("last_out_added"), t + 1)
                    elif t == 0 or cg == N_CG - 1:
                        act.wait_ge(resid_added, cg + 1)
                    fn(scratch[:, 512 * t:512 * t + 512], resid[:, t, 512 * cg:512 * cg + 512], ACT.Square,
                       accum_out=ss2[:, t, cg:cg + 1]).then_inc(sem("part_sq"), 1)

            for u in range(LAST_VISIT // 2, FFN_UNIT0):
                hi_half(u + AHEAD)
                cg, kk = divmod(u - OUT_UNIT0, UPG)
                if kk == 3 and cg > 0:
                    part_squares(cg - 1)
            part_squares(N_CG - 1)
            for t in range(TT):
                act.wait_ge(sem("ss2_sum"), t + 1)
                inv_root(r2[:, t:t + 1], ss2s[:, t:t + 1], 1.0 / D_MODEL).then_inc(sem("r2_ready"), 1)

            def h_split(k):
                act.wait_ge(sem("h_turned"), k + 1)
                fn(x_hi[:, k, :], bank[k if k < 4 else 4 + k % 4], ACT.Copy, scale=A["norm_ffn"][:, k:k + 1]) \
                    .then_inc(sem("h_hi_done"), 1)

            def ffn_hi(u, jj, landed):
                act.wait_ge(unit_done, u - SPL + 1)
                act.wait_ge(raw_ready[ffn_slot(jj, RAW)], landed)
                sr, ss = 1024 * ffn_slot(jj, RAW), 1024 * ffn_slot(jj, SPL)
                fn(w_hi[:, ss:ss + 1024], w_raw[:, sr:sr + 1024], ACT.Copy).then_inc(hi_done, 1)

            def take_gate(done, taken):
                act.wait_ge(unit_done, done)
                if taken is not None:
                    act.wait_ge(sem("act_ready"), taken)
                fn(silu_gate[:, :], set_a, ACT.Silu).then_inc(sem("gate_taken"), 1)

            def act_hi_half(chunks):
                act.wait_ge(sem("up_taken"), chunks)
                fn(act_hi.rearrange("p f t -> p (f t)"), silu_gate[:, :], ACT.Copy).then_inc(sem("act_hi_done"), 1)

            for k in range(4):
                h_split(k)
            for j in range(2 * UPG):
                for k in (2 * j + 4, 2 * j + 5):
                    if k < KD:
                        h_split(k)
                ffn_hi(FFN_UNIT0 + j + AHEAD, j + AHEAD, ffn_raw_at(j + AHEAD))
                if j == UPG:
                    take_gate(FFN_UNIT0 + UPG, None)
            with act.Fori(1, N_CHUNKS) as c:
                u0 = FFN_UNIT0 + c * UPC - UPG
                for j in range(UPC):
                    jj = LOOP_J + j + AHEAD
                    ffn_hi(u0 + j + AHEAD, jj, c * (16 * UPC // RAW) + (ffn_raw_at(jj) - 16 * UPC // RAW))
                    if j == 0:
                        act_hi_half(c)
                    if j == UPG:
                        take_gate(u0 + UPG, c)
            u0 = FFN_UNIT0 + N_CHUNKS * UPC - UPG
            for j in range(UPG):
                if j + AHEAD < UPG:
                    jj = UPC * (N_CHUNKS - 1) + LOOP_J + j + AHEAD
                    ffn_hi(u0 + j + AHEAD, jj, ffn_raw_at(jj))
                if j == 0:
                    for f in range(4):
                        act.wait_ge(sem("up_taken"), N_CHUNKS + f)
                        fn(act_hi[:, f, :], silu_gate[:, f * SEQ:f * SEQ + SEQ], ACT.Copy).then_inc(sem("act_hi_done"), 1)

        @block.vector
        def _(dve):
            tt, ts, stt, copy = (nc.vector.tensor_tensor, nc.vector.tensor_scalar, nc.vector.scalar_tensor_tensor,
                                 nc.vector.tensor_copy)
            chain = [0]

            def link(ins):
                chain[0] += 1
                ins.then_inc(sem("dve_chain"), 1)
                dve.wait_ge(sem("dve_chain"), chain[0])

            def lo_half(u):
                dve.wait_ge(hi_done, u + 1)
                n, sr, ss = unit_cols(u), (u % RAW) * 1024, (u % SPL) * 1024
                tt(w_lo[:, ss:ss + n], w_raw[:, sr:sr + n], w_hi[:, ss:ss + n].bitcast(F32), ALU.subtract) \
                    .then_inc(lo_done, 1)

            def x_split(k):
                dve.wait_ge(sem("x_hi_done"), k + 1)
                stt(x_lo[:, k, :], bank[3 + k % 5], A["norm_mix"][:, k:k + 1], x_hi[:, k, :].bitcast(F32),
                    ALU.mult, ALU.subtract).then_inc(sem("x_split"), 1)

            def mem_split(j):
                for k in (2 * j, 2 * j + 1):
                    dve.wait_ge(sem("mem_hi_done"), 2 * j + 2)
                    stt(um_lo[:, k, :], bank[3 + j % 5][:, (k % 2) * 256:(k % 2) * 256 + 256],
                        A["mem_norm"][:, k:k + 1], um_hi[:, k, :].bitcast(F32), ALU.mult, ALU.subtract) \
                        .then_inc(sem("mem_split"), 1)

            def take_v(n, kind, h):
                dve.wait_ge(unit_done, UPG * (n + 3))
                if kind == "gdn":
                    dve.wait_ge(sem("pads_zero"), h + 1)
                    copy(cin[:, 2, 3:], bank[2]).then_inc(bank_taken[2], 1)
                    return
                qkv_free(dve, n)
                w = MEM_LEN if kind == "mem" else SEQ
                copy(qkv[:, 2, 0:w], bank[2][:, 0:w]).then_inc(bank_taken[2], 1)

            def norm_q(n, kind):
                dve.wait_ge(sem("rn_ready"), n + 1)
                gain = {"mem": comb[:, 0:1], "fox": comb[:, 1:2], "gdn": SCALE}[kind]
                stt(qkv[:, 0, :], qkv[:, 0, :], gain, sq[:, 0, :], ALU.mult, ALU.mult).then_inc(sem("qn_ready"), 1)

            def scale_probs(kind, h, cuts):
                dve.wait_ge(sem(kind + "_exp"), h + 1)
                link(nc.vector.reciprocal(rrec, rsum))
                for j in range(TT):
                    last = ts(pr[:, cuts[j]:cuts[j + 1]], pr[:, cuts[j]:cuts[j + 1]], rrec[:, j:j + 1], None, ALU.mult)
                last.then_inc(sem(kind + "_probs"), 1)

            def mem_side(n, h, v):
                if v == 5:
                    norm_q(n, "mem")
                if v == 7:
                    dve.wait_ge(sem("tok_ready"), n + 1)
                    copy(vtok[:, 0:MT, :].rearrange("p t d -> p (t d)"), T[2][:, 0:MEM_LEN]).then_inc(sem("vtok_ready"), 1)
                if v in (8, 9):
                    i = v - 8
                    dve.wait_ge(sem("mem_scores"), 2 * h + i + 1)
                    last = nc.vector.tensor_reduce(mx[:, 2 * i:2 * i + 2], T[i].rearrange("p (j c) -> p j c", j=2),
                                                   AX.X, ALU.max)
                    if v == 9:
                        link(last)
                        ts(nmx, mx, -1.0, None, ALU.mult).then_inc(sem("mem_max"), 1)
                if v == 10:
                    scale_probs("mem", h, [256 * j for j in range(TT + 1)])
                if v == TURN_V:
                    dve.wait_ge(sem("mem_turned_p"), 2 * h + 2)
                    copy(pt[:, 512:1024], T[1]).then_inc(sem("mem_pt1"), 1)
                if v == PV_V:
                    dve.wait_ge(sem("mem_pv"), h + 1)
                    copy(mix[:, MIX_MEM + h, :], T[2]).then_inc(sem("mem_mixed"), 1)

            def fox_side(n, h, v):
                if v == 5:
                    norm_q(n, "fox")
                if v == 7:
                    dve.wait_ge(sem("tok_ready"), n + 1)
                    copy(vtok.rearrange("p t d -> p (t d)"), T[2]).then_inc(sem("vtok_ready"), 1)
                off = [0, 128, 384, 768, 1280]
                if v in (8, 9, 10):
                    if v == 8:
                        dve.wait_ge(sem("ncb_ready"), h + 1)
                    dve.wait_ge(sem("fox_scores"), 3 * h + v - 7)
                    for j, b, c0 in {8: ((0, 0, 0), (1, 0, 128)), 9: ((2, 1, 0),), 10: ((3, 2, 0),)}[v]:
                        w = (j + 1) * P
                        last = nc.vector.tensor_tensor_reduce(pr[:, off[j]:off[j + 1]], T[b][:, c0:c0 + w], ncb[:, 0:w],
                                                              1.0, -3e38, ALU.add, ALU.max, mx[:, j:j + 1])
                    if v == 10:
                        link(last)
                        ts(nmx, mx, -1.0, None, ALU.mult).then_inc(sem("fox_max"), 1)
                        scale_probs("fox", h, off)
                if v == TURN_V:
                    dve.wait_ge(sem("fox_turned1"), h + 1)
                    copy(pt[:, 512:896], T[1][:, 0:384]).then_inc(sem("fox_pt1"), 1)
                if v == PV_V:
                    dve.wait_ge(sem("fox_pv"), h + 1)
                    copy(mix[:, MIX_FOX + h, :], T[2]).then_inc(sem("fox_mixed"), 1)

            def conv(n, h):
                banks_taken(dve, n + 3)
                qkv_free(dve, n)
                for j in range(TAPS):
                    for s in range(3):
                        w, src = conv_w[:, s, h, j:j + 1], cin[:, s, j:j + SEQ]
                        if j == 0:
                            ins = ts(qkv[:, s, :], src, w, None, ALU.mult)
                        else:
                            dve.wait_ge(sem("conv_step"), 12 * h + 3 * (j - 1) + s + 1)
                            ins = stt(qkv[:, s, :], src, w, qkv[:, s, :], ALU.mult, ALU.add)
                        ins.then_inc(sem("conv_step"), 1)

            def decay_arg(w, h):
                rows_ = T[2].rearrange("p (t a c) -> p t a c", t=TT, a=2)
                for a in range(2):
                    s = slice(64 * a, 64 * a + 64)
                    last = tt(dec[s, w], rows_[s, :, a], bcl(ngc[s, :, h], CHUNK), ALU.add)
                return last

            def gdn_side(n, h, v):
                b = h % 2
                hc = slice(h, h + 1)
                if v == 0:
                    conv(n, h)
                if v == 5:
                    dve.wait_ge(sem("qg_exp"), h + 1)
                    if h == 0:
                        dve.wait_ge(sem("gate_exps"), 1)
                    decay_arg(0, h).then_inc(sem("gc_taken"), 1)
                    norm_q(n, "gdn")
                if v == 6:
                    dve.wait_ge(sem("gcb_rows"), h + 1)
                    link(decay_arg(1, h))
                    dve.wait_ge(sem("gc_taken"), h + 1)
                    d8 = dec.rearrange("p w t c -> p (w t) c")
                    tt(d8, d8, K["neg64"].unsqueeze(1).to_broadcast([P, 2 * TT, CHUNK]), ALU.add) \
                        .then_inc(sem("dec_arg"), 1)
                if v == 7:
                    i64 = K["ident64"].unsqueeze(1).to_broadcast([P, TT, CHUNK])
                    pair0 = K["pair0"].unsqueeze(1).to_broadcast([P, TT, CHUNK])
                    dve.wait_ge(sem("gram_ready"), h + 1)
                    dve.wait_ge(sem("decay"), h + 1)
                    if h > 0:
                        dve.wait_ge(sem("coup_ready"), 5 * h)
                    if h >= 2:
                        dve.wait_ge(sem("ds_ready"), NCH * (h - 1))
                    t0 = T[0].rearrange("p (w t c) -> p w t c", w=2, t=TT)
                    tt(lt, t0[:, 0], dec[:, 1], ALU.mult).then_inc(sem("lt_ready"), 1)
                    tt(sc_at[b], t0[:, 1], dec[:, 0], ALU.mult)
                    dve.wait_ge(sem("lt_ready"), h + 1)
                    link(tt(inv[:, 1], lt, pair0, ALU.mult))
                    tt(inv[:, 1], i64, inv[:, 1], ALU.subtract).then_inc(sem("inv0_ready"), 1)
                    dve.wait_ge(sem("ktok_ready"), h + 1)
                    k3 = T[1].rearrange("p (t d) -> p t d", t=TT)
                    tt(kbg, k3, bcl(beg[:, :, h], HD), ALU.mult)
                    tt(sc_kd[b], k3, bcl(kdf[:, :, h], HD), ALU.mult).then_inc(sem("k_scaled"), 1)
                    dve.wait_ge(sem("tok_ready"), n + 1)
                    tt(vb, T[2].rearrange("p (t d) -> p t d", t=TT), bcl(beta[:, :, h], HD), ALU.mult) \
                        .then_inc(sem("v_scaled"), 1)
                for l in range(1, 6):
                    if v == 8 + 2 * l:
                        dve.wait_ge(sem("xy_ready"), 5 * h + l)
                        t0 = T[0].rearrange("p (w t c) -> p w t c", w=2, t=TT)
                        if l == 1:
                            dve.wait_ge(sem("inv0_copied"), h + 1)
                        w = slice(0, 2) if l < 5 else slice(1, 2)
                        i8, p8 = (a[:, w].rearrange("p w t c -> p (w t c)") for a in (inv, t0))
                        tt(i8, i8, p8, ALU.subtract).then_inc(sem("inv_updated"), 1)
                if 21 <= v < 21 + 2 * NCH:
                    c, second = divmod(v - 21, 2)
                    i, s = c // 2, slice(64 * (c % 2), 64 * (c % 2) + 64)
                    if not second:
                        dve.wait_ge(sem("ws_ready"), NCH * h + c + 1)
                        tt(v_new[s, :], sc_u[b][s, i, :], S1[s, 0:P], ALU.add).then_inc(sem("v_new"), 1)
                    else:
                        dve.wait_ge(sem("ds_ready"), NCH * h + c + 1)
                        if c < NCH - 1:
                            stt(state, state, egl[:, c % 2, i, hc], S1[:, P:2 * P], ALU.mult, ALU.add) \
                                .then_inc(sem("state_new"), 1)
                        else:
                            nc.vector.memset(state, 0.0).then_inc(sem("state_clear"), 1)
                if v == 37:
                    dve.wait_ge(sem("or_ready"), h + 1)
                    tt(mix[:, MIX_GDN + h, :].rearrange("p (t d) -> p t d", t=TT),
                       S2.rearrange("p (t d) -> p t d", t=TT), bcl(orn, HD), ALU.mult).then_inc(sem("o_scaled"), 1)
                if v == 52:
                    dve.wait_ge(sem("o_turned"), h + 1)
                    dve.wait_ge(sem("zg_ready"), 2)
                    tt(mix[:, MIX_GDN + h, :], T[0], zg[:, h, :], ALU.mult).then_inc(sem("gdn_mixed"), 1)

            def mix_split(j):
                k = MIX_ORDER[j]
                dve.wait_ge(sem("mix_hi_done"), j + 1)
                tt(x_lo[:, k, :], mix[:, k, :], x_hi[:, k, :].bitcast(F32), ALU.subtract).then_inc(sem("mix_split"), 1)

            def out_add(cg):
                dve.wait_ge(unit_done, OUT_UNIT0 + UPG * (cg + 1))
                dve.wait_ge(sem("resid_in"), 16)
                r = resid[:, :, 512 * cg:512 * cg + 512]
                tt(r, (set_a, set_b)[cg % 2].rearrange("p (t c) -> p t c", t=TT), r, ALU.add).then_inc(resid_added, 1)

            def out_add_last():
                for t in range(TT):
                    if t < TT - 1:
                        dve.wait_ge(sem("last_out_sums"), t + 1)
                    else:
                        dve.wait_ge(unit_done, FFN_UNIT0)
                    r = resid[:, t, 512 * (N_CG - 1):]
                    tt(r, bank[4 * ((N_CG - 1) % 2) + t], r, ALU.add) \
                        .then_inc(sem("last_out_added") if t < TT - 1 else resid_added, 1)

            def diagonals(r, count):
                for t in range(TT):
                    dve.wait_ge(sem(count), t + 1)
                    ts(diag[:, t, :], K["ident"], r[:, t:t + 1], None, ALU.mult).then_inc(sem("diag_ready"), 1)

            dve.wait_ge(sem("ident_in"), 16)
            dve.wait_ge(sem("par_in"), 16)
            stt(comb[:, 0:1], A["mem_q"], SCALE, A["mem_k"], ALU.mult, ALU.mult)
            stt(comb[:, 1:2], A["fox_q"], SCALE, A["fox_k"], ALU.mult, ALU.mult).then_inc(sem("comb_ready"), 1)
            dve.wait_ge(sem("comb_ready"), 1)
            diagonals(rx, "rx_ready")
            lo_half(0)
            lo_half(1)
            for k in range(4):
                x_split(k)
            for t in range(LAST_VISIT):
                u, half = divmod(t, 2)
                if half == 0 and u < UPG:
                    for k in (2 * u + 4, 2 * u + 5):
                        if k < KD:
                            x_split(k)
                for n, kind, h, v in head_visit(t):
                    if v == 0:
                        take_v(n, kind, h)
                if half == 0:
                    lo_half(u + AHEAD)
                if t == 5:
                    dve.wait_ge(sem("const_in"), 16)
                    copy(identb[:, :], K["ident"]).then_inc(sem("bf_consts"), 1)
                    copy(causalb[:, :], K["causal"]).then_inc(sem("bf_consts"), 1)
                    dve.wait_ge(sem("gate_w_hi"), 1)
                    tt(wg_lo.rearrange("p k c -> p (k c)"), A["gate_w"],
                       wg_hi.rearrange("p k c -> p (k c)").bitcast(F32), ALU.subtract).then_inc(sem("gate_w_split"), 1)
                    dve.wait_ge(sem("rm_ready"), 1)
                    for m in range(MT):
                        ts(mem_in[:, m, :], mem_in[:, m, :], rm[:, m:m + 1], None, ALU.mult).then_inc(sem("mem_normed"), 1)
                if VPG <= t < VPG + KD // 2:
                    mem_split(t - VPG)
                if t == VPG + 11:
                    dve.wait_ge(sem("gates_ready"), 1)
                    link(ts(gz, bank[3][0:NG, :], A["gate_bias"][0:NG], A["gate_sign"][0:NG], ALU.add, ALU.mult))
                    stt(gl, gz, -1.0, gz, ALU.mult, ALU.max).then_inc(sem("gate_abs"), 1)
                    dve.wait_ge(sem("rates"), 1)
                    link(ts(coef, coef, -1.0, None, ALU.mult))
                    dve.wait_ge(sem("gate_ln"), 1)
                    link(stt(gl, gz, 0.0, gl, ALU.max, ALU.add))
                    ts(gl, gl, coef[0:NG, :], None, ALU.mult).then_inc(sem("gate_logs"), 1)
                if t == VPG + 13:
                    dve.wait_ge(sem("gates_turned"), 1)
                    copy(ga.rearrange("p t c -> p (t c)"), bank[4][:, 0:TT * NG]).then_inc(sem("gates_by_token"), 1)
                if t == VPG + 15:
                    for i, (r, src) in enumerate(((GL, gl), (GC, bank[6][GC:GC + NG, :]), (NC, bank[7][NC:NC + NG, :]))):
                        dve.wait_ge(sem("rows_hi_done"), i + 1)
                        tt(rows_lo[r:r + NG, :], src, rows_hi[r:r + NG, :].bitcast(F32), ALU.subtract) \
                            .then_inc(sem("rows_lo_done"), 1)
                    dve.wait_ge(sem("gate_sums"), 1)
                    copy(gsum, bank[5][:, 0:4 * n4]).then_inc(sem("gate_sums_read"), 1)
                    dve.wait_ge(sem("gate_sums_read"), 1)
                    gc = gsum[:, 0:n4].rearrange("p (t h) -> p t h", t=TT)
                    tt(beg, gc, ga[:, :, N_FOX + N_GDN:], ALU.add).then_inc(sem("beg_arg"), 1)
                    ts(ngc, gc, -1.0, None, ALU.mult).then_inc(sem("ngc_ready"), 1)
                    nc.vector.memset(state, 0.0).then_inc(sem("state_clear"), 1)
                    dve.wait_ge(sem("ngc_ready"), 1)
                if t >= VPG * N_GROUPS and t % 2 == 0:
                    kk = (t - VPG * N_GROUPS) // 2
                    for j in range(2 * kk + 2 if kk else 0, min(2 * kk + 4, KD - 1)):
                        mix_split(j)
                for n, kind, h, v in head_visit(t):
                    {"mem": mem_side, "gdn": gdn_side, "fox": fox_side}[kind](n, h, v)
            mix_split(KD - 1)
            for u in range(LAST_VISIT // 2, FFN_UNIT0):
                lo_half(u + AHEAD)
                cg, kk = divmod(u - OUT_UNIT0, UPG)
                if kk == 0:
                    out_add(cg - 1)
            out_add_last()
            for t in range(TT):
                dve.wait_ge(sem("part_sq"), TT * (N_CG - 1) + t + 1)
                nc.vector.tensor_reduce(ss2s[:, t:t + 1], ss2[:, t, :], AX.X, ALU.add).then_inc(sem("ss2_sum"), 1)
            diagonals(r2, "r2_ready")

            def h_split(k):
                dve.wait_ge(sem("h_hi_done"), k + 1)
                stt(x_lo[:, k, :], bank[k if k < 4 else 4 + k % 4], A["norm_ffn"][:, k:k + 1], x_hi[:, k, :].bitcast(F32),
                    ALU.mult, ALU.subtract).then_inc(sem("h_split"), 1)

            def ffn_lo(u, jj):
                dve.wait_ge(hi_done, u + 1)
                sr, ss = 1024 * ffn_slot(jj, RAW), 1024 * ffn_slot(jj, SPL)
                tt(w_lo[:, ss:ss + 1024], w_raw[:, sr:sr + 1024], w_hi[:, ss:ss + 1024].bitcast(F32), ALU.subtract) \
                    .then_inc(lo_done, 1)

            def take_up(done, chunks):
                dve.wait_ge(unit_done, done)
                dve.wait_ge(sem("gate_taken"), chunks)
                tt(silu_gate[:, :], set_b, silu_gate[:, :], ALU.mult).then_inc(sem("up_taken"), 1)

            def act_lo_half(chunks):
                dve.wait_ge(sem("act_hi_done"), chunks)
                tt(act_lo.rearrange("p f t -> p (f t)"), silu_gate[:, :],
                   act_hi.rearrange("p f t -> p (f t)").bitcast(F32), ALU.subtract).then_inc(sem("act_ready"), 1)

            def down_add(done, before, cg, side):
                dve.wait_ge(unit_done, done)
                dve.wait_ge(resid_added, before)
                r = resid[:, :, 512 * cg:512 * cg + 512]
                tt(r, (set_a, set_b)[side].rearrange("p (t c) -> p t c", t=TT), r, ALU.add).then_inc(resid_added, 1)

            for k in range(4):
                h_split(k)
            for j in range(2 * UPG):
                for k in (2 * j + 4, 2 * j + 5):
                    if k < KD:
                        h_split(k)
                ffn_lo(FFN_UNIT0 + j + AHEAD, j + AHEAD)
            with dve.Fori(1, N_CHUNKS) as c:
                u0 = FFN_UNIT0 + c * UPC - UPG
                for j in range(UPC):
                    ffn_lo(u0 + j + AHEAD, LOOP_J + j + AHEAD)
                    if j == 0:
                        take_up(u0, c)
                    if j == 1:
                        act_lo_half(c)
                    if j in (10, 12, 14, 16):
                        cg = (j - 10) // 2
                        down_add(u0 + j, c * N_CG + cg, cg, 1 - cg % 2)
            u0 = FFN_UNIT0 + N_CHUNKS * UPC - UPG
            for j in range(UPG + 1):
                if j + AHEAD < UPG:
                    ffn_lo(u0 + j + AHEAD, LOOP_J + j + AHEAD)
                if j == 0:
                    dve.wait_ge(unit_done, u0)
                    dve.wait_ge(sem("gate_taken"), N_CHUNKS)
                    for f in range(5):
                        g, up = silu_gate[:, :], set_b
                        if f < 4:
                            cols = slice(f * SEQ, f * SEQ + SEQ)
                            tt(g[:, cols], up[:, cols], g[:, cols], ALU.mult).then_inc(sem("up_taken"), 1)
                        if f > 0:
                            dve.wait_ge(sem("act_hi_done"), N_CHUNKS + f - 1)
                            tt(act_lo[:, f - 1, :], g[:, (f - 1) * SEQ:f * SEQ], act_hi[:, f - 1, :].bitcast(F32),
                               ALU.subtract).then_inc(sem("act_ready"), 1)
                if 2 <= j < UPG and j % 2 == 0:
                    cg = j // 2 - 1
                    down_add(u0 + j, N_CHUNKS * N_CG + cg, cg, cg % 2)
            for t in range(TT):
                if t < TT - 1:
                    dve.wait_ge(sem("tail_sums"), t + 1)
                else:
                    dve.wait_ge(unit_done, u0 + UPG)
                r = resid[:, t, 512 * (N_CG - 1):]
                tt(r, bank[4 + t], r, ALU.add).then_inc(sem("tail_added"), 1)

        @block.gpsimd
        def _(pool):
            tt, copy = nc.gpsimd.tensor_tensor, nc.gpsimd.tensor_copy

            def norm_k(n, kind):
                pool.wait_ge(sem("rn_ready"), n + 1)
                w = MEM_LEN if kind == "mem" else SEQ
                tt(qkv[:, 1, 0:w], qkv[:, 1, 0:w], sq[:, 1, 0:w], ALU.mult).then_inc(sem("kn_ready"), 1)

            def mem_side(n, h, v):
                if v == 5:
                    norm_k(n, "mem")

            def fox_side(n, h, v):
                if v == 0:
                    pool.wait_ge(sem("gcb_rows"), N_GDN)
                    if h > 0:
                        pool.wait_ge(sem("negc_ready"), h)
                    copy(pick[:, 0, :], ident_col(NC + h)).then_inc(sem("picks_ready"), 1)
                if v == 5:
                    norm_k(n, "fox")

            def gdn_side(n, h, v):
                b = h % 2
                if v == 0:
                    pool.wait_ge(sem("qn_ready"), n)
                    pool.wait_ge(sem("kn_ready"), n)
                    nc.gpsimd.memset(cin[:, :, 0:TAPS - 1], 0.0).then_inc(sem("pads_zero"), 1)
                    if h > 0:
                        pool.wait_ge(sem("gcb_rows"), h)
                    copy(pick[:, 0, :], ident_col(GC + N_FOX + h)).then_inc(sem("picks_ready"), 1)
                    tt(pick[:, 1, :], ident_col(GC + N_FOX + h), ident_col(GL + N_FOX + N_GDN + h), ALU.add) \
                        .then_inc(sem("picks_ready"), 1)
                if v == 5:
                    norm_k(n, "gdn")
                if v == 6:
                    pool.wait_ge(sem("qn_ready"), n + 1)
                    pool.wait_ge(sem("qg_exp"), h + 1)
                    tt(sc_qg[b], sc_qg[b], qkv[:, 0, :], ALU.mult).then_inc(sem("qg_ready"), 1)
                if v == 7:
                    pool.wait_ge(sem("lt_ready"), h + 1)
                    if h > 0:
                        pool.wait_ge(sem("y_ready"), 5 * h)
                    for l in range(1, 6):
                        tt(coup[:, l - 1], lt, K[f"pair{l}"].unsqueeze(1).to_broadcast([P, TT, CHUNK]), ALU.mult) \
                            .then_inc(sem("coup_ready"), 1)

            def ident_col(r):
                return K["ident"][:, r:r + 1].to_broadcast([P, P])

            nc.gpsimd.memset(rows_hi[:, :].bitcast(F32), 0.0).then_inc(sem("rows_zero"), 1)
            nc.gpsimd.memset(rows_lo[:, :].bitcast(F32), 0.0).then_inc(sem("rows_zero"), 1)
            pool.wait_ge(sem("par_in"), 16)
            pool.wait_ge(sem("const_in"), 16)
            for t in range(LAST_VISIT):
                if t in (VPG, 2 * VPG):
                    i = t // VPG - 1
                    banks_taken(pool, i + 1)
                    z = zg[:, 3 * i:3 * i + 3, :]
                    nc.gpsimd.tensor_scalar(z, z, A["gdn_out"], 1.0, ALU.mult, ALU.mult).then_inc(sem("zg_ready"), 1)
                for n, kind, h, v in head_visit(t):
                    {"mem": mem_side, "gdn": gdn_side, "fox": fox_side}[kind](n, h, v)


_INS = ["x", "mem", "w_in", "w_mem_kv", "w_out", "w_gate_up", "w_down"]


def kernel(x, mem, norm_mix, w_in, fox_f_bias, fox_q_norm, fox_k_norm, gdn_conv, gdn_a_log, gdn_dt_bias,
           gdn_out_norm, mem_norm, w_mem_kv, mem_q_norm, mem_k_norm, w_out, norm_ffn, w_gate_up, w_down):
    import concourse.bacc as bacc
    from concourse.bass_utils import run_bass_kernel_spmd

    a = {n: np.ascontiguousarray(np.asarray(v)[0]) for n, v in
         dict(x=x, mem=mem, w_in=w_in, w_mem_kv=w_mem_kv, w_out=w_out, w_gate_up=w_gate_up, w_down=w_down).items()}
    tiles = lambda v: np.asarray(v)[0].reshape(-1, P).T
    rows = lambda *v: np.concatenate(v + (np.zeros(P - NG, np.float32),)).reshape(P, 1)
    zeros, ones = np.zeros(N_GDN, np.float32), np.ones(N_GDN, np.float32)
    gate_cols = np.concatenate([a["w_in"][:, C_FF:C_FF + N_FOX], a["w_in"][:, C_GA:C_GA + 2 * N_GDN]], 1)
    parts = dict(
        norm_mix=tiles(norm_mix), mem_norm=tiles(mem_norm), norm_ffn=tiles(norm_ffn),
        conv=np.asarray(gdn_conv)[0].reshape(TAPS, 3 * N_GDN, P).transpose(2, 1, 0).reshape(P, -1),
        fox_q=tiles(fox_q_norm), fox_k=tiles(fox_k_norm), mem_q=tiles(mem_q_norm), mem_k=tiles(mem_k_norm),
        gdn_out=tiles(gdn_out_norm),
        gate_bias=rows(np.asarray(fox_f_bias)[0], np.asarray(gdn_dt_bias)[0], zeros),
        gate_sign=rows(-ones, ones, -ones),
        a_log=rows(zeros, np.asarray(gdn_a_log)[0], zeros),
        gate_w=gate_cols.reshape(KD, P, NG).transpose(1, 0, 2).reshape(P, -1))
    a["const"] = CONST_ARRAY
    a["par"] = np.ascontiguousarray(np.concatenate([parts[n] for n in PAR], 1))
    nc = bacc.Bacc("TRN2", target_bir_lowering=False, num_devices=1)
    args = [nc.dram_tensor(f"in_{n}", v.shape, mybir.dt.from_np(v.dtype), kind="ExternalInput").ap()
            for n, v in a.items()]
    out = nc.dram_tensor("out", (SEQ, D_MODEL), F32, kind="ExternalOutput").ap()
    build(nc, *args, out)
    r = run_bass_kernel_spmd(nc, [{f"in_{n}": v for n, v in a.items()}], core_ids=[0])
    return r.results[0]["out"].reshape(1, SEQ, D_MODEL)
```

```python
from contextlib import ExitStack

import numpy as np

import concourse.bass as bass
from concourse import mybir

F32 = mybir.dt.float32
F32R = mybir.dt.float32r
BF16 = mybir.dt.bfloat16
ALU = mybir.AluOpType
ACT = mybir.ActivationFunctionType
AX = mybir.AxisListType

P = 128
D_MODEL = 2048
SEQ = 512
MEM_LEN = 256
HD = 128
CHUNK = 64
N_MEM, N_FOX, N_GDN = 4, 6, 6
FOX_W, GDN_W, MEM_W = N_FOX * HD, N_GDN * HD, N_MEM * HD
FF = 5632
TAPS = 4
EPS = 1e-6
SCALE = HD ** -0.5
KD = D_MODEL // P
TT = SEQ // P
MT = MEM_LEN // P
NCH = SEQ // CHUNK

C_FOX = 0
C_FF = 3 * FOX_W
C_GDN = C_FF + N_FOX
C_Z = C_GDN + 3 * GDN_W
C_GA = C_Z + GDN_W
C_MQ = C_GA + 2 * N_GDN
NG = N_FOX + 2 * N_GDN

MIX_FOX, MIX_GDN, MIX_MEM = 0, N_FOX, N_FOX + N_GDN

GROUPS = [("z", 0), ("z", 1)] + [("mem", h) for h in range(N_MEM)] + \
         [("gdn", h) for h in range(N_GDN)] + [("fox", h) for h in range(N_FOX)]
HEADS = GROUPS[2:]
N_GROUPS = len(GROUPS)
UPG = KD // 2
VPG = 2 * UPG
OUT_UNIT0 = N_GROUPS * UPG
N_CG = D_MODEL // 512
FFN_UNIT0 = OUT_UNIT0 + N_CG * UPG
N_CHUNKS = FF // 512
UPC = 3 * UPG
RAW = 3
SPL = 3
AHEAD = SPL - 1
assert UPC % RAW == 0 and UPC % SPL == 0

CONST = {}


def const_array():
    t = np.arange(P)
    half = t // CHUNK
    same = half[:, None] == half[None, :]
    le = t[:, None] <= t[None, :]
    r, c = t[:, None] % CHUNK, np.arange(CHUNK)[None, :]
    parts = {
        "eps": np.full((P, 1), EPS),
        "ident": np.eye(P),
        "ones": np.ones((P, P)),
        "cum": same & le,
        "suffix": same & ~le,
        "sel0": np.repeat(half[:, None] == 0, P, 1),
        "sel1": np.repeat(half[:, None] == 1, P, 1),
        "negcum": -(le.astype(float)),
        "negall": -np.ones((P, P)),
        "causal": np.where(t[None, :] <= t[:, None], 0.0, -1e30),
        "ident64": r == c,
        "neg64": np.where(r <= c, 0.0, -1e30),
    }
    for l in range(6):
        s = 1 << l
        parts[f"pair{l}"] = (r // (2 * s) == c // (2 * s)) & (r % (2 * s) < s) & (c % (2 * s) >= s)
    at = 0
    for name, a in parts.items():
        CONST[name] = (at, at + a.shape[1])
        at += a.shape[1]
    return np.concatenate([np.asarray(a, np.float32) for a in parts.values()], 1)


CONST_ARRAY = const_array()
PAR = {}
_at = 0
for _name, _n in (("norm_mix", KD), ("mem_norm", KD), ("norm_ffn", KD), ("conv", 3 * N_GDN * TAPS),
                  ("fox_q", 1), ("fox_k", 1), ("mem_q", 1), ("mem_k", 1), ("gdn_out", 1),
                  ("gate_bias", 1), ("gate_sign", 1), ("a_log", 1), ("gate_w", KD * NG)):
    PAR[_name] = (_at, _at + _n)
    _at += _n
N_PAR = _at


def build(nc, x, mem, w_in, w_mem_kv, w_out, w_gate_up, w_down, const, par, out):
    ctx = ExitStack()
    with ctx:
        at = [17 * 1024]

        def place(name, cols, dt=F32, offset=None):
            if offset is None:
                offset = at[0]
                at[0] += -(-4 * cols // 32) * 32
            return nc.alloc_sbuf_tensor_at(name, [P, cols], dt, offset=offset)

        x_hi = place("x_hi", KD * SEQ, F32R)[:, :].rearrange("p (k t) -> p k t", k=KD)
        x_lo = place("x_lo", KD * SEQ, F32R)[:, :].rearrange("p (k t) -> p k t", k=KD)
        w_raw = place("w_raw", RAW * 1024)
        w_hi = place("w_hi", SPL * 1024, F32R)
        w_lo = place("w_lo", SPL * 1024, F32R)
        mix_at = at[0]
        mix = place("mix", KD * SEQ)[:, :].rearrange("p (k t) -> p k t", k=KD)
        um_hi = place("um_hi", KD * MEM_LEN, F32R, mix_at)[:, :].rearrange("p (k t) -> p k t", k=KD)
        wg_hi = place("wg_hi", KD * NG, F32R, mix_at + 8 * 2048)[:, :].rearrange("p (k c) -> p k c", k=KD)
        wg_lo = place("wg_lo", KD * NG, F32R, mix_at + 9 * 2048)[:, :].rearrange("p (k c) -> p k c", k=KD)
        act_hi = place("act_hi", 4 * SEQ, F32R, mix_at)[:, :].rearrange("p (f t) -> p f t", f=4)
        act_lo = place("act_lo", 4 * SEQ, F32R, mix_at + 8192)[:, :].rearrange("p (f t) -> p f t", f=4)
        silu_gate = place("silu_gate", 4 * SEQ, F32, mix_at + 16384)
        res_at = at[0]
        res_t = place("residual", TT * D_MODEL)
        resid = res_t[:, :].rearrange("p (t c) -> p t c", t=TT)
        um_lo = place("um_lo", KD * MEM_LEN, F32R, res_at)[:, :].rearrange("p (k t) -> p k t", k=KD)
        SCAN = 4 * SEQ + 256
        scan_b = [res_t[:, b * SCAN:(b + 1) * SCAN] for b in range(2)]
        sc_u = [s[:, 0:512].rearrange("p (t d) -> p t d", t=TT) for s in scan_b]
        sc_nw = [s[:, 512:1024] for s in scan_b]
        sc_qg = [s[:, 1024:1536] for s in scan_b]
        sc_kd = [s[:, 1536:2048].rearrange("p (t d) -> p t d", t=TT) for s in scan_b]
        sc_at = [s[:, 2048:2304].rearrange("p (t c) -> p t c", t=TT) for s in scan_b]
        zg = res_t[:, 2 * SCAN:2 * SCAN + N_GDN * SEQ].rearrange("p (h t) -> p h t", h=N_GDN)
        state = res_t[:, 7680:7808]
        v_new = res_t[:, 7808:7936]
        WORK = 1548 + 1536 + 3840
        work = place("work", WORK)
        cin = work[:, 0:1545].rearrange("p (s c) -> p s c", s=3)
        sq = work[:, 0:1024].rearrange("p (s t) -> p s t", s=2)
        qkv = work[:, 1548:3084].rearrange("p (s t) -> p s t", s=3)
        tmp = work[:, 3084:6924]
        coup = tmp[:, 0:1280].rearrange("p (l t c) -> p l t c", l=5, t=TT)
        inv = tmp[:, 1280:1792].rearrange("p (w t c) -> p w t c", w=2, t=TT)
        yb = tmp[:, 1792:2048].rearrange("p (t c) -> p t c", t=TT)
        lt = tmp[:, 2048:2304].rearrange("p (t c) -> p t c", t=TT)
        dec = tmp[:, 2304:2816].rearrange("p (w t c) -> p w t c", w=2, t=TT)
        vb = tmp[:, 2816:3328].rearrange("p (t d) -> p t d", t=TT)
        kbg = tmp[:, 3328:3840].rearrange("p (t d) -> p t d", t=TT)
        pr = tmp[:, 0:1280]
        pt = tmp[:, 1280:2560]
        vtok = tmp[:, 2560:3072].rearrange("p (t d) -> p t d", t=TT)
        ncb = tmp[:, 3072:3584]
        mem_in = work[:, 1548:1548 + 2 * D_MODEL].rearrange("p (t c) -> p t c", t=MT)
        diag = work[:, 0:TT * P].rearrange("p (t c) -> p t c", t=TT)
        r_row = work[:, SEQ:2 * SEQ]
        scaled = work[:, 1548 + 2 * D_MODEL:1548 + 2 * D_MODEL + 2 * SEQ].rearrange("p (i t) -> p i t", i=2)

        def x_bank(k):
            return bank[3 + k % 4]

        def h_bank(k):
            return bank[k if k < 7 else 4 + (k - 4) % 3]

        gz = tmp[0:NG, 0:SEQ]
        gl = tmp[0:NG, SEQ:2 * SEQ]
        GL, GC, NC = 0, 32, 64
        N_ROWS = NC + NG
        rows_hi = place("rows_hi", SEQ, F32R)
        rows_lo = place("rows_lo", SEQ, F32R)
        pick = place("pick", 2 * P, F32R)[:, :].rearrange("p (w c) -> p w c", w=2)

        NC_ = CONST_ARRAY.shape[1]
        cst = place("cst", NC_)
        K = {n: cst[:, a:b] for n, (a, b) in CONST.items()}
        prm = place("prm", N_PAR)
        A = {n: prm[:, a:b] for n, (a, b) in PAR.items()}
        conv_w = A["conv"].rearrange("p (s h j) -> p s h j", s=3, h=N_GDN)
        identb = nc.alloc_sbuf_tensor_at("identb", [P, P], BF16, offset=at[0])
        causalb = nc.alloc_sbuf_tensor_at("causalb", [P, P], BF16, offset=at[0] + 256)
        at[0] += 512
        small_t = place("small", 464)
        small_at = [0]

        def small(n):
            small_at[0] += n
            assert small_at[0] <= 464
            return small_t[:, small_at[0] - n:small_at[0]]

        ga = small(TT * NG).rearrange("p (t c) -> p t c", t=TT)
        coef = small(1)
        gsum = small(4 * TT * N_GDN)
        n4 = TT * N_GDN
        ngc = small(n4).rearrange("p (t h) -> p t h", t=TT)
        kdf = small(n4).rearrange("p (t h) -> p t h", t=TT)
        beta = small(n4).rearrange("p (t h) -> p t h", t=TT)
        beg = small(n4).rearrange("p (t h) -> p t h", t=TT)
        egl = small(2 * n4).rearrange("p (j t h) -> p j t h", j=2, t=TT)
        ssx = small(4)
        rx = small(4)
        ssm = small(2)
        rm = small(2)
        mx = small(4)
        nmx = small(4)
        rsum = small(4)
        rrec = small(4)
        oss = small(4)
        orn = small(4)
        ss2 = small(TT * N_CG).rearrange("p (t g) -> p t g", t=TT)
        ss2s = small(4)
        r2 = small(4)
        r_work = small(4)
        q_root = small(len(HEADS) * TT).rearrange("p (n t) -> p n t", n=len(HEADS))
        comb = small(2)
        scratch = mix.rearrange("p k t -> p (k t)")[:, 10 * SEQ:10 * SEQ + D_MODEL]
        assert at[0] <= 224 * 1024
        psum = ctx.enter_context(nc.psum_tensor("psum", [P, 8 * 512], F32))
        bank = [psum[:, 512 * b:512 * b + 512] for b in range(8)]
        set_a, set_b = psum[:, 0:2048], psum[:, 2048:4096]
        S1, S2, T = bank[3], bank[7], bank[4:7]

        sems = {}

        def sem(name):
            if name not in sems:
                sems[name] = ctx.enter_context(nc.semaphore(name))
            return sems[name]

        raw_ready = [sem(f"raw_ready{i}") for i in range(RAW)]
        hi_done, lo_done, unit_done = sem("hi_done"), sem("lo_done"), sem("unit_done")
        group_sums = sem("group_sums")
        bank_taken = [sem(f"bank{s}_taken") for s in range(3)]

        w_in3 = {"gdn": w_in[:, C_GDN:C_GDN + 3 * GDN_W].rearrange("(k p) (s h c) -> p k s h c", p=P, s=3, h=N_GDN),
                 "fox": w_in[:, C_FOX:C_FOX + 3 * FOX_W].rearrange("(k p) (s h c) -> p k s h c", p=P, s=3, h=N_FOX)}
        w_in2 = w_in.rearrange("(k p) c -> p k c", p=P)
        w_kv = w_mem_kv.rearrange("(k p) (s h c) -> p k s h c", p=P, s=2, h=N_MEM)
        w_out_v = w_out.rearrange("(k p) c -> p k c", p=P)
        w_gu_v = w_gate_up.rearrange("(k p) c -> p k c", p=P)
        w_dn_v = w_down.rearrange("(f k p) c -> f p k c", p=P, k=2)
        MIX_ORDER = [6, 7, 8, 9, 10, 11, 12, 13, 14, 15, 0, 1, 2, 3, 4, 5]

        def raw_loads(u):
            s = w_raw[:, (u % RAW) * 1024:(u % RAW) * 1024 + 1024]
            if u >= OUT_UNIT0:
                cg, kk = divmod(u - OUT_UNIT0, UPG)
                k0 = MIX_ORDER[2 * kk]
                return [(s.rearrange("p (k c) -> p k c", k=2), w_out_v[:, k0:k0 + 2, 512 * cg:512 * cg + 512])]
            g, kk = divmod(u, UPG)
            kind, h = GROUPS[g]
            ks = slice(2 * kk, 2 * kk + 2)
            s = s[:, 0:768].rearrange("p (k s c) -> p k s c", k=2, s=3)
            if kind == "z":
                return [(s.rearrange("p k s c -> p k (s c)"), w_in2[:, ks, C_Z + 384 * h:C_Z + 384 * h + 384])]
            if kind == "mem":
                return [(s[:, :, 0, :], w_in2[:, ks, C_MQ + HD * h:C_MQ + HD * h + HD])] + \
                       [(s[:, k, 1:3, :], w_kv[:, 2 * kk + k, :, h, :]) for k in range(2)]
            return [(s[:, k, :, :], w_in3[kind][:, 2 * kk + k, :, h, :]) for k in range(2)]

        resid_added = sem("resid_added")
        LOOP_J = 2 * UPG

        def ffn_slot(jj, n):
            return (FFN_UNIT0 + jj) % n

        raw_count = [0] * RAW
        raw_at = []
        for u in range(FFN_UNIT0):
            raw_count[u % RAW] += 16 * len(raw_loads(u))
            raw_at.append(raw_count[u % RAW])

        def ffn_raw_at(jj):
            s = ffn_slot(jj, RAW)
            return raw_count[s] + 16 * sum(ffn_slot(i, RAW) == s for i in range(jj + 1))

        def unit_cols(u):
            return 768 if u < OUT_UNIT0 else 1024

        def head_visit(t):
            out_ = []
            for n, (kind, h) in enumerate(HEADS):
                v = t - VPG * (n + 3)
                last = {"mem": 16, "fox": 16, "gdn": 53}[kind]
                if 0 <= v < last:
                    out_.append((n, kind, h, v))
            return out_

        LAST_VISIT = VPG * N_GROUPS + 16

        def roots(n):
            return sum(kind != "gdn" for kind, _ in HEADS[:n])

        def late(n):
            kind, h = HEADS[n]
            return int(kind == "fox" and h <= 2)

        def norm_visit(n):
            return 4 + late(n)

        def turn_visit(n):
            return 13 + late(n) if n < len(HEADS) - 1 else 12

        def part(ap, l, second):
            d = " ".join(f"d{i}" for i in range(len(ap.shape) - 1))
            return ap.rearrange(f"{d} (g a c) -> {d} g a c", a=2, c=1 << l)[(slice(None),) * len(ap.shape) + (int(second),)]

        def mix_tiles(t):
            v = t - VPG * N_GROUPS
            if v in (-2, -1):
                return (2 * v + 4, 2 * v + 5)
            return [j for j in (v + 4, v + 5) if j < KD - 1] if v >= 0 and v % 2 == 0 else ()

        def banks_taken(eng, groups):
            for s in range(3):
                eng.wait_ge(bank_taken[s], groups)

        def qkv_free(eng, n):
            if n == 0:
                return
            kind, h = HEADS[n - 1]
            if kind == "gdn":
                eng.wait_ge(sem("tok_ready"), n)
                eng.wait_ge(sem("qg_ready"), h + 1)
            else:
                eng.wait_ge(sem(kind + "_scores"), (2 if kind == "mem" else 3) * (h + 1))

        def bcl(ap, n):
            return ap.unsqueeze(2).to_broadcast([ap.shape[0], ap.shape[1], n])

        block = ctx.enter_context(nc.Block())

        @block.sync
        def _(sp):
            x_v = x.rearrange("(t p) c -> p t c", p=P)
            for t in range(TT):
                sp.dma_start(resid[:, t, :], x_v[:, t, :]).then_inc(sem(f"x_in{t}"), 16)
            for u in range(FFN_UNIT0):
                if u >= RAW:
                    sp.wait_ge(lo_done, u - RAW + 1)
                for dst, src in raw_loads(u):
                    sp.dma_start(dst, src).then_inc(raw_ready[u % RAW], 16)

            def load(base, jj, src):
                slot = ffn_slot(jj, RAW)
                sp.wait_ge(lo_done, base - RAW + 1)
                s = w_raw[:, slot * 1024:slot * 1024 + 1024].rearrange("p (k c) -> p k c", k=2)
                sp.dma_start(s, src).then_inc(raw_ready[slot], 16)

            def gate_up(u0, jj, c, up):
                for kk in range(UPG):
                    load(u0 + kk, jj + kk, w_gu_v[:, 2 * kk:2 * kk + 2, bass.ds(c * 512 + (FF if up else 0), 512)])

            def down(u0, jj, c):
                for j in range(2 * N_CG):
                    cg, kk = divmod(j, 2)
                    load(u0 + j, jj + j, w_dn_v[bass.ds(c * 2 + kk, 1), :, :, 512 * cg:512 * cg + 512]
                         .rearrange("f p k c -> (f p) k c"))

            gate_up(FFN_UNIT0, 0, 0, False)
            gate_up(FFN_UNIT0 + UPG, UPG, 0, True)
            with sp.Fori(1, N_CHUNKS) as c:
                u0 = FFN_UNIT0 + c * UPC - UPG
                gate_up(u0, LOOP_J, c, False)
                down(u0 + UPG, LOOP_J + UPG, c - 1)
                gate_up(u0 + 2 * UPG, LOOP_J + 2 * UPG, c, True)
            down(FFN_UNIT0 + N_CHUNKS * UPC - UPG, LOOP_J, N_CHUNKS - 1)
            out_v = out.rearrange("(t p) c -> p t c", p=P)
            for cg in range(N_CG - 1):
                sp.wait_ge(resid_added, N_CG * N_CHUNKS + cg + 1)
                sp.dma_start(out_v[:, :, 512 * cg:512 * cg + 512],
                             resid[:, :, 512 * cg:512 * cg + 512]).then_inc(sem("out_done"), 16)
            for t in range(TT):
                sp.wait_ge(sem("tail_added"), t + 1)
                sp.dma_start(out_v[:, t, 512 * (N_CG - 1):], resid[:, t, 512 * (N_CG - 1):]) \
                    .then_inc(sem("out_done"), 16)
            sp.wait_ge(sem("out_done"), 16 * (N_CG - 1 + TT))

        @block.tensor
        def _(pe):
            mm = nc.tensor.matmul

            def mm3(dst, ahi, alo, bhi, blo, first, last):
                mm(dst, ahi, bhi, start=first, stop=False)
                mm(dst, ahi, blo, start=False, stop=False)
                return mm(dst, alo, bhi, start=False, stop=last)

            def w_tiles(slot, a, b):
                return w_hi[:, slot * 1024 + a:slot * 1024 + b], w_lo[:, slot * 1024 + a:slot * 1024 + b]

            def turn(dst, k, t):
                return nc.tensor.transpose(dst[:, t * P:t * P + P], resid[:, t, k * P:k * P + P], K["ident"])

            def spread_root(before):
                for t in range(TT):
                    pe.wait_ge(sem("diag_ready"), before + t + 1)
                    last = mm(bank[7][:, t * P:t * P + P], K["ones"], diag[:, t, :], start=True, stop=True)
                last.then_inc(sem("root_row"), 1)

            def x_transpose(k):
                pe.wait_ge(sem("x_scaled"), k - 3)
                for t in range(TT):
                    last = turn(x_bank(k), k, t)
                last.then_inc(sem("x_turned"), 1)

            def mem_transpose(j):
                if j < 5:
                    pe.wait_ge(sem("x_split"), KD)
                else:
                    pe.wait_ge(sem("mem_split"), 2 * (j - 4))
                for i in range(2):
                    for t in range(MT):
                        k = 2 * j + i
                        last = nc.tensor.transpose(bank[3 + j % 5][:, i * 256 + t * P:i * 256 + t * P + P],
                                                   mem_in[:, t, k * P:k * P + P], K["ident"])
                last.then_inc(sem("mem_turned"), 1)

            def gates():
                pe.wait_ge(sem("gate_w_split"), 1)
                pe.wait_ge(sem("mem_split"), KD)
                for k in range(KD):
                    last = mm3(bank[3][0:NG, :], wg_hi[:, k, :], wg_lo[:, k, :], x_hi[:, k, :], x_lo[:, k, :],
                               k == 0, k == KD - 1)
                last.then_inc(sem("gates_ready"), 1)

            def gates_turn():
                pe.wait_ge(sem("gate_logs"), 1)
                for t in range(TT):
                    last = nc.tensor.transpose(bank[4][:, t * NG:t * NG + NG], gl[:, t * P:t * P + P],
                                               K["ident"][0:NG, 0:NG])
                last.then_inc(sem("gates_turned"), 1)

            def gate_sums():
                pe.wait_ge(sem("gates_by_token"), 1)
                pe.wait_ge(sem("const_in"), 16)
                g = ga[:, :, N_FOX:N_FOX + N_GDN]
                for i, name in enumerate(("cum", "suffix", "sel0", "sel1")):
                    last = mm(bank[5][:, i * n4:i * n4 + n4].rearrange("p (t h) -> p t h", t=TT), K[name], g,
                              start=True, stop=True)
                last.then_inc(sem("gate_sums"), 1)
                for t in range(TT):
                    last = mm(bank[6][GC:GC + NG, t * P:t * P + P], ga[:, t, :], K["cum"], start=True, stop=True)
                for j in range(TT):
                    for t in range(j + 1):
                        last = mm(bank[7][NC:NC + NG, j * P:j * P + P], ga[:, t, :], K["negall" if t < j else "negcum"],
                                  start=(t == 0), stop=(t == j))
                last.then_inc(sem("gate_sum_rows"), 1)

            def spread(dst, w):
                mm(dst, pick[0:N_ROWS, w, :], rows_hi[0:N_ROWS, :], start=True, stop=False)
                return mm(dst, pick[0:N_ROWS, w, :], rows_lo[0:N_ROWS, :], start=False, stop=True)

            def unit_half(u, half):
                g, kk = divmod(u, UPG)
                slot = u % SPL
                k = 2 * kk + half
                if half == 0:
                    pe.wait_ge(lo_done, u + 1)
                if u >= OUT_UNIT0:
                    cg, kk = divmod(u - OUT_UNIT0, UPG)
                    k = MIX_ORDER[2 * kk + half]
                    pe.wait_ge(sem("mix_split"), 2 * kk + half + 1)
                    if kk == 0 and half == 0:
                        if cg == 0:
                            pe.wait_ge(sem("gdn_mixed"), N_GDN)
                        elif cg == 1:
                            pe.wait_ge(sem("fox_mixed"), N_FOX)
                        else:
                            pe.wait_ge(resid_added, cg - 1)
                    hi, lo = w_tiles(slot, half * 512, half * 512 + 512)
                    begin = kk == 0 and half == 0
                    for t in (3, 0, 1, 2) if begin and cg == 0 else range(TT):
                        if begin and cg == 0 and t < 3:
                            pe.wait_ge(bank_taken[t], N_GROUPS)
                        last = mm3(bank[4 * (cg % 2) + t], x_hi[:, k, t * P:t * P + P], x_lo[:, k, t * P:t * P + P],
                                   hi, lo, begin, kk == UPG - 1 and half == 1)
                        if u == FFN_UNIT0 - 1 and half == 1 and t < TT - 1:
                            last.then_inc(sem("last_out_sums"), 1)
                    if half == 1:
                        last.then_inc(unit_done, 1)
                    return
                kind, h = GROUPS[g]
                for s, i in ((0, 0), (0, 1), (1, 0)) if half == 0 else ((1, 1), (2, 0), (2, 1)):
                    k = 2 * kk + i
                    if kk == 0 and i == 0 and g > 0:
                        pe.wait_ge(bank_taken[s], g)
                    if g == 0 and s == 0:
                        pe.wait_ge(sem("x_split"), k + 1)
                    hi, lo = w_tiles(slot, i * 384 + s * P, i * 384 + s * P + P)
                    bhi, blo, dst = x_hi[:, k, :], x_lo[:, k, :], bank[s]
                    if kind == "mem" and s > 0:
                        bhi, blo, dst = um_hi[:, k, :], um_lo[:, k, :], bank[s][:, 0:MEM_LEN]
                    last = mm3(dst, hi, lo, bhi, blo, k == 0, k == KD - 1)
                    if k == KD - 1 and s < 2:
                        last.then_inc(group_sums, 1)
                if half == 1:
                    last.then_inc(unit_done, 1)

            def halves():
                for i in range(TT):
                    for a in range(2):
                        yield i, slice(64 * a, 64 * a + 64)

            def banks_free(n):
                if n == 0:
                    pe.wait_ge(sem("gate_sums_read"), 1)
                    pe.wait_ge(sem("rows_lo_done"), 3)
                elif HEADS[n - 1][0] == "gdn":
                    pe.wait_ge(sem("uw_taken"), 2 * (HEADS[n - 1][1] + 1))
                else:
                    pe.wait_ge(sem(HEADS[n - 1][0] + "_mixed"), HEADS[n - 1][1] + 1)

            def norms(n, kind):
                pe.wait_ge(sem("sq_ready"), n + 1)
                if kind == "fox":
                    mm(T[0], K["ones"], sq[:, 0, :], start=True, stop=True)
                else:
                    for t in range(TT):
                        mm(T[0][:, t:t + 1], sq[:, 0, t * P:t * P + P], K["ones"][:, 0:1], start=True, stop=True)
                nk = MEM_LEN if kind == "mem" else SEQ
                mm(T[1][:, 0:nk], K["ones"], sq[:, 1, 0:nk], start=True, stop=True).then_inc(sem("ssq_ready"), 1)

            def mem_side(n, h, v):
                if v == norm_visit(n):
                    banks_free(n)
                    norms(n, "mem")
                if v == 7:
                    for t in range(MT):
                        last = nc.tensor.transpose(T[2][:, t * P:t * P + P], qkv[:, 2, t * P:t * P + P], K["ident"])
                    last.then_inc(sem("tok_ready"), 1)
                if v in (8, 9):
                    if v == 8:
                        pe.wait_ge(sem("qn_ready"), n + 1)
                        pe.wait_ge(sem("kn_ready"), n + 1)
                    j0 = 2 * (v - 8)
                    for j in (j0, j0 + 1):
                        last = mm(T[v - 8][:, (j - j0) * 256:(j - j0) * 256 + 256], qkv[:, 0, j * P:j * P + P],
                                  qkv[:, 1, 0:MEM_LEN], start=True, stop=True)
                    last.then_inc(sem("mem_scores"), 1)
                if v == turn_visit(n):
                    pe.wait_ge(sem("mem_probs"), h + 1)
                    for i in range(MT):
                        for j in range(TT):
                            last = nc.tensor.transpose(T[i][:, j * P:j * P + P], pr[:, j * 256 + i * P:j * 256 + i * P + P],
                                                       K["ident"])
                        last.then_inc(sem("mem_turned_p"), 1)
                if v == turn_visit(n) + 1:
                    pe.wait_ge(sem("mem_pt0"), h + 1)
                    pe.wait_ge(sem("mem_pt1"), h + 1)
                    pe.wait_ge(sem("vtok_ready"), h + 1)
                    for i in range(MT):
                        last = mm(T[2], vtok[:, i, :], pt[:, i * 512:i * 512 + 512], start=(i == 0), stop=(i == MT - 1))
                    last.then_inc(sem("mem_pv"), 1)

            def fox_side(n, h, v):
                if v == norm_visit(n):
                    banks_free(n)
                    if h <= 2:
                        pe.wait_ge(sem("gdn_mixed"), h + 4)
                    pe.wait_ge(sem("picks_ready"), 2 * N_GDN + h + 1)
                    spread(T[2], 0).then_inc(sem("negc_ready"), 1)
                    norms(n, "fox")
                if v == 7:
                    pe.wait_ge(sem("ncb_ready"), h + 1)
                    for t in range(TT):
                        last = nc.tensor.transpose(T[2][:, t * P:t * P + P], qkv[:, 2, t * P:t * P + P], K["ident"])
                    last.then_inc(sem("tok_ready"), 1)
                vs = v - late(n)
                if vs in (8, 9, 10):
                    if vs == 8:
                        pe.wait_ge(sem("qn_ready"), n + 1)
                        pe.wait_ge(sem("kn_ready"), n + 1)
                        pe.wait_ge(sem("bf_consts"), 2)
                    if vs == 10:
                        pe.wait_ge(sem("vtok_ready"), N_MEM + h + 1)
                    for j, b, c0 in {8: ((0, 0, 0), (1, 0, 128)), 9: ((2, 1, 0),), 10: ((3, 2, 0),)}[vs]:
                        w = (j + 1) * P
                        mm(T[b][:, c0:c0 + w], qkv[:, 0, j * P:j * P + P], qkv[:, 1, 0:w], start=True, stop=False)
                        last = mm(T[b][:, c0 + j * P:c0 + w], identb[:, :], causalb[:, :], start=False, stop=True)
                    last.then_inc(sem("fox_scores"), 1)
                if v == turn_visit(n):
                    pe.wait_ge(sem("fox_probs"), h + 1)
                    off = [0, 128, 384, 768]
                    for b, blocks in ((0, ((0, 0),)), (1, ((1, 0),)), (2, ((2, 0), (3, 256)))):
                        for i, c0 in blocks:
                            for j in range(i, TT):
                                last = nc.tensor.transpose(T[b][:, c0 + (j - i) * P:c0 + (j - i + 1) * P],
                                                           pr[:, off[j] + i * P:off[j] + i * P + P], K["ident"])
                        last.then_inc(sem(f"fox_turned{b}"), 1)
                if v == turn_visit(n) + 1:
                    pe.wait_ge(sem("fox_pt0"), h + 1)
                    pe.wait_ge(sem("fox_pt1"), h + 1)
                    pe.wait_ge(sem("fox_pt2"), h + 1)
                    offp = [0, 512, 896, 1152]
                    for i in range(TT):
                        last = mm(T[2][:, i * P:], vtok[:, i, :], pt[:, offp[i]:offp[i] + SEQ - i * P],
                                  start=(i == 0), stop=(i == TT - 1))
                    last.then_inc(sem("fox_pv"), 1)

            def gdn_side(n, h, v):
                b = h % 2
                if v == 5:
                    banks_free(n)
                    if h >= 3:
                        pe.wait_ge(sem("gdn_mixed"), h - 2)
                    pe.wait_ge(sem("picks_ready"), 2 * h + 2)
                    spread(T[2], 0).then_inc(sem("gc_rows"), 1)
                    norms(n, "gdn")
                if v == 6:
                    pe.wait_ge(sem("gc_taken"), h + 1)
                    spread(T[2], 1).then_inc(sem("gcb_rows"), 1)
                if v == 7:
                    pe.wait_ge(sem("qn_ready"), n + 1)
                    pe.wait_ge(sem("kn_ready"), n + 1)
                    for i, s in halves():
                        c = i * P + s.start
                        mm(T[0][s, i * 64:i * 64 + 64], qkv[:, 1, c:c + 64], qkv[:, 1, c:c + 64], start=True, stop=True)
                        last = mm(T[0][s, 256 + i * 64:320 + i * 64], qkv[:, 1, c:c + 64], qkv[:, 0, c:c + 64],
                                  start=True, stop=True)
                    last.then_inc(sem("gram_ready"), 1)
                    for i in range(TT):
                        last = nc.tensor.transpose(T[1][:, i * P:i * P + P], qkv[:, 1, i * P:i * P + P], K["ident"])
                    last.then_inc(sem("ktok_ready"), 1)
                    pe.wait_ge(sem("dec_arg"), h + 1)
                    for i in range(TT):
                        last = nc.tensor.transpose(T[2][:, i * P:i * P + P], qkv[:, 2, i * P:i * P + P], K["ident"])
                    last.then_inc(sem("tok_ready"), 1)
                if v == 8:
                    pe.wait_ge(sem("inv0_ready"), h + 1)
                    for i, s in halves():
                        last = mm(T[0][s, i * 64:i * 64 + 64], inv[s, 1, i, :], K["ident64"][s, :], start=True, stop=True)
                    last.then_inc(sem("inv0_turned"), 1)
                for l in range(1, 6):
                    if v == 7 + 2 * l:
                        pe.wait_ge(sem("coup_ready"), 5 * h + l)
                        if l == 1:
                            pe.wait_ge(sem("inv0_copied"), h + 1)
                            pe.wait_ge(sem("k_scaled"), h + 1)
                        else:
                            pe.wait_ge(sem("inv_updated"), 5 * h + l - 1)
                        for i, s in halves():
                            last = mm(T[1][s, i * 64:i * 64 + 64], coup[s, l - 1, i, :], inv[s, 0, i, :],
                                      start=True, stop=True)
                        last.then_inc(sem("y_ready"), 1)
                    if v == 8 + 2 * l:
                        pe.wait_ge(sem("y_copied"), 5 * h + l)
                        for i, s in halves():
                            xy, xyt = (T[0][s, c + 32 * i:c + 32 * i + 32].rearrange("p (g c) -> p g c", c=1 << l)
                                       for c in (0, 256))
                            if l < 5:
                                mm(xy, inv[s, 1, i, :], part(yb[s, i, :], l, False), start=True, stop=True)
                            last = mm(xyt, yb[s, i, :], part(inv[s, 1, i, :], l, True), start=True, stop=True)
                        last.then_inc(sem("xy_ready"), 1)
                if v == 19:
                    pe.wait_ge(sem("inv_updated"), 5 * h + 5)
                    pe.wait_ge(sem("v_scaled"), h + 1)
                    for i, s in halves():
                        last = mm(T[1][s, i * P:i * P + P], inv[s, 1, i, :], vb[s, i, :], start=True, stop=True)
                    last.then_inc(sem("u_ready"), 1)
                    for i, s in halves():
                        last = mm(T[2 - s.start // 32][:, i * 64:i * 64 + 64], kbg[s, i, :], inv[s, 1, i, :],
                                  start=True, stop=True)
                    last.then_inc(sem("w_ready"), 1)
                if 21 <= v < 21 + 2 * NCH:
                    c, second = divmod(v - 21, 2)
                    i, s = c // 2, slice(64 * (c % 2), 64 * (c % 2) + 64)
                    cols = slice(64 * c, 64 * c + 64)
                    if not second:
                        if c == 0:
                            pe.wait_ge(sem("uw_taken"), 2 * h + 2)
                            pe.wait_ge(sem("state_clear"), h + 1)
                        else:
                            pe.wait_ge(sem("state_new"), (NCH - 1) * h + c)
                        mm(S1[s, 0:P], sc_nw[b][:, cols], state, start=True, stop=True).then_inc(sem("ws_ready"), 1)
                    else:
                        pe.wait_ge(sem("v_new"), NCH * h + c + 1)
                        if c == 0:
                            pe.wait_ge(sem("qg_ready"), h + 1)
                            if h > 0:
                                pe.wait_ge(sem("o_scaled"), h)
                        mm(S2[s, i * P:i * P + P], sc_qg[b][:, cols], state, start=True, stop=False)
                        mm(S2[s, i * P:i * P + P], sc_at[b][s, i, :], v_new[s, :], start=False, stop=True)
                        mm(S1[:, P:2 * P], sc_kd[b][s, i, :], v_new[s, :], start=True, stop=True) \
                            .then_inc(sem("ds_ready"), 1)
                if v == 52:
                    pe.wait_ge(sem("o_scaled"), h + 1)
                    if h + 2 < N_GDN:
                        pe.wait_ge(sem("uw_taken"), 2 * (h + 3))
                    k = MIX_GDN + h
                    for i in range(TT):
                        last = nc.tensor.transpose(T[0][:, i * P:i * P + P], mix[:, k, i * P:i * P + P], K["ident"])
                    last.then_inc(sem("o_turned"), 1)

            pe.wait_ge(sem("ident_in"), 16)
            for t in range(TT):
                pe.wait_ge(sem(f"x_in{t}"), 16)
                for k in range(4):
                    last = turn(x_bank(k), k, t)
                    if t == TT - 1:
                        last.then_inc(sem("x_turned"), 1)
            spread_root(0)
            x_transpose(4)
            for t in range(LAST_VISIT):
                u, half = divmod(t, 2)
                if u < UPG and half == 0:
                    for k in (2 * u + 5, 2 * u + 6):
                        if k < KD:
                            x_transpose(k)
                unit_half(u, half)
                if t == VPG:
                    pe.wait_ge(sem("mem_normed"), MT)
                if VPG <= t < VPG + KD // 2:
                    mem_transpose(t - VPG)
                if t == VPG + 10:
                    gates()
                if t == VPG + 12:
                    gates_turn()
                if t == VPG + 15:
                    gate_sums()
                for n, kind, h, v in head_visit(t):
                    {"mem": mem_side, "gdn": gdn_side, "fox": fox_side}[kind](n, h, v)
            for t in range(LAST_VISIT, 2 * FFN_UNIT0):
                unit_half(t // 2, t % 2)

            for t in range(TT):
                if t < TT - 1:
                    pe.wait_ge(sem("last_out_added"), t + 1)
                else:
                    pe.wait_ge(resid_added, N_CG)
                for k in range(4):
                    last = turn(h_bank(k), k, t)
                    if t == TT - 1:
                        last.then_inc(sem("h_turned"), 1)

            def h_transpose(k):
                if k >= 7:
                    pe.wait_ge(sem("h_scaled"), k - 2)
                for t in range(TT):
                    last = turn(h_bank(k), k, t)
                last.then_inc(sem("h_turned"), 1)

            for k in range(4, 7):
                h_transpose(k)
            spread_root(TT)

            def gate_up(u0, jj, side, peeled=False):
                for kk in range(UPG):
                    if peeled:
                        for k in (2 * kk + 5, 2 * kk + 6):
                            if 7 <= k < KD:
                                h_transpose(k)
                    pe.wait_ge(lo_done, u0 + kk + 1)
                    for half in range(2):
                        k = 2 * kk + half
                        if peeled:
                            pe.wait_ge(sem("h_split"), k + 1)
                        for s in range(4):
                            if peeled and k == 0:
                                pe.wait_ge(sem("h_scaled"), s + 1)
                            hi, lo = w_tiles(ffn_slot(jj + kk, SPL), half * 512 + s * P, half * 512 + s * P + P)
                            last = mm3(bank[4 * side + s], hi, lo, x_hi[:, k, :], x_lo[:, k, :], k == 0, k == KD - 1)
                    last.then_inc(unit_done, 1)

            def down(u0, jj, side, turned=False, tail=False):
                for kk in range(2):
                    pe.wait_ge(lo_done, u0 + kk + 1)
                    slot = ffn_slot(jj + kk, SPL)
                    steps = [(f, t) for f in (2 * kk, 2 * kk + 1) for t in range(TT)]
                    for f, t in sorted(steps, key=lambda ft: ft[1]) if tail and kk == 1 else steps:
                        if turned and t == 0:
                            pe.wait_ge(sem("act_ready"), N_CHUNKS + f)
                        hi, lo = w_tiles(slot, (f % 2) * 512, (f % 2) * 512 + 512)
                        last = mm3(bank[4 * side + t], act_hi[:, f, t * P:t * P + P], act_lo[:, f, t * P:t * P + P],
                                   hi, lo, f == 0, f == 3)
                        if tail and f == 3 and t < TT - 1:
                            last.then_inc(sem("tail_sums"), 1)
                    last.then_inc(unit_done, 1)

            gate_up(FFN_UNIT0, 0, 0, peeled=True)
            gate_up(FFN_UNIT0 + UPG, UPG, 1)
            with pe.Fori(1, N_CHUNKS) as c:
                u0 = FFN_UNIT0 + c * UPC - UPG
                added = c * N_CG
                pe.wait_ge(resid_added, added)
                pe.wait_ge(sem("gate_taken"), c)
                gate_up(u0, LOOP_J, 0)
                pe.wait_ge(sem("act_ready"), c)
                down(u0 + UPG, LOOP_J + UPG, 1)
                pe.wait_ge(sem("gate_taken"), c + 1)
                down(u0 + UPG + 2, LOOP_J + UPG + 2, 0)
                pe.wait_ge(resid_added, added + 1)
                down(u0 + UPG + 4, LOOP_J + UPG + 4, 1)
                pe.wait_ge(resid_added, added + 2)
                down(u0 + UPG + 6, LOOP_J + UPG + 6, 0)
                pe.wait_ge(resid_added, added + 3)
                gate_up(u0 + 2 * UPG, LOOP_J + 2 * UPG, 1)
            u0 = FFN_UNIT0 + N_CHUNKS * UPC - UPG
            added = N_CHUNKS * N_CG
            pe.wait_ge(resid_added, added)
            down(u0, LOOP_J, 0, turned=True)
            down(u0 + 2, LOOP_J + 2, 1)
            pe.wait_ge(resid_added, added + 1)
            down(u0 + 4, LOOP_J + 4, 0)
            pe.wait_ge(resid_added, added + 2)
            down(u0 + 6, LOOP_J + 6, 1, tail=True)

        @block.scalar
        def _(act):
            fn = nc.scalar.activation

            def roots_table():
                nc.scalar.preload_act_table_set("natural_log_exp_and_others")

            first = CONST["ones"][1]
            act.dma_start(cst[:, 0:first], const[:, 0:first]).then_inc(sem("ident_in"), 16)
            act.dma_start(prm[:, :], par).then_inc(sem("par_in"), 16)
            roots_table()

            def hi_half(u):
                if u >= SPL:
                    act.wait_ge(unit_done, u - SPL + 1)
                act.wait_ge(raw_ready[u % RAW], raw_at[u] if u < FFN_UNIT0 else ffn_raw_at(u - FFN_UNIT0))
                n = unit_cols(u)
                fn(w_hi[:, (u % SPL) * 1024:(u % SPL) * 1024 + n], w_raw[:, (u % RAW) * 1024:(u % RAW) * 1024 + n],
                   ACT.Copy).then_inc(hi_done, 1)

            def link(ins):
                chain[0] += 1
                ins.then_inc(sem("act_chain"), 1)
                act.wait_ge(sem("act_chain"), chain[0])

            def inv_root(dst, src, scale):
                link(fn(dst, src, ACT.Ln, scale=scale, bias=eps))
                return fn(dst, dst, ACT.Exp, scale=-0.5)

            chain = [0]
            eps = K["eps"]

            def copy_root(n):
                act.wait_ge(sem("root_row"), n)
                fn(r_row, bank[7], ACT.Copy).then_inc(sem("root_copied"), 1)

            act.wait_ge(sem("ident_in"), 16)
            act.wait_ge(sem("par_in"), 16)
            for t in range(TT):
                act.wait_ge(sem(f"x_in{t}"), 16)
                link(fn(scratch, resid[:, t, :], ACT.Square, accum_out=ssx[:, t:t + 1]))
                inv_root(rx[:, t:t + 1], ssx[:, t:t + 1], 1.0 / D_MODEL).then_inc(sem("rx_ready"), 1)
            hi_half(0)
            hi_half(1)
            copy_root(1)
            act.dma_start(cst[:, first:], const[:, first:]).then_inc(sem("const_in"), 16)
            act.dma_start(mem_in, mem.rearrange("(t p) c -> p t c", p=P)).then_inc(sem("mem_in"), 16)

            def x_split(k):
                act.wait_ge(sem("x_scaled"), k + 1)
                fn(x_hi[:, k, :], scaled[:, k % 2, :], ACT.Copy).then_inc(sem("x_hi_done"), 1)

            def mem_split(j):
                act.wait_ge(sem("mem_turned"), j + 1)
                for k in (2 * j, 2 * j + 1):
                    fn(um_hi[:, k, :], bank[3 + j % 5][:, (k % 2) * 256:(k % 2) * 256 + 256], ACT.Copy,
                       scale=A["mem_norm"][:, k:k + 1]).then_inc(sem("mem_hi_done"), 1)

            def main_copies(n, kind, h, g):
                if kind == "gdn":
                    act.wait_ge(sem("pads_zero"), h + 1)
                else:
                    qkv_free(act, n)
                for s in range(2):
                    act.wait_ge(group_sums, 2 * g + s + 1)
                    w = MEM_LEN if kind == "mem" and s == 1 else SEQ
                    dst = cin[:, s, 3:] if kind == "gdn" else qkv[:, s, 0:w]
                    fn(dst, bank[s][:, 0:w], ACT.Copy).then_inc(bank_taken[s], 1)

            def squares(n, kind, g):
                for s in range(2):
                    act.wait_ge(bank_taken[s], g + 1)
                if n > 0:
                    act.wait_ge(sem("qn_ready"), n)
                    act.wait_ge(sem("kn_ready"), n)
                if kind == "mem":
                    fn(sq[:, 0, :], qkv[:, 0, :], ACT.Square)
                    fn(sq[:, 1, 0:MEM_LEN], qkv[:, 1, 0:MEM_LEN], ACT.Square).then_inc(sem("sq_ready"), 1)
                else:
                    fn(sq, qkv[:, 0:2, :], ACT.Square).then_inc(sem("sq_ready"), 1)

            def factors(n, kind):
                act.wait_ge(sem("ssq_ready"), n + 1)
                scale = 1.0 if kind == "gdn" else 1.0 / HD
                if kind == "fox":
                    inv_root(sq.rearrange("p s t -> p (s t)"), psum[:, 2048:2048 + 2 * SEQ], scale) \
                        .then_inc(sem("rn_ready"), 1)
                    return
                nk = MEM_LEN if kind == "mem" else SEQ
                inv_root(sq[:, 1, 0:nk], T[1][:, 0:nk], scale)
                inv_root(q_root[:, n, :], T[0][:, 0:TT], scale).then_inc(sem("rn_ready"), 1)

            def mem_side(n, h, v):
                if v == 1:
                    squares(n, "mem", n + 2)
                if v == norm_visit(n):
                    factors(n, "mem")
                if v == 10:
                    act.wait_ge(sem("mem_max"), h + 1)
                    for j in range(TT):
                        last = fn(pr[:, j * 256:j * 256 + 256], T[j // 2][:, (j % 2) * 256:(j % 2) * 256 + 256], ACT.Exp,
                                  scale=q_root[:, n, j:j + 1], bias=nmx[:, j:j + 1], accum_out=rsum[:, j:j + 1])
                    last.then_inc(sem("mem_exp"), 1)
                if v == turn_visit(n):
                    act.wait_ge(sem("mem_turned_p"), 2 * h + 1)
                    fn(pt[:, 0:512], T[0], ACT.Copy).then_inc(sem("mem_pt0"), 1)

            def fox_side(n, h, v):
                if v == 1:
                    squares(n, "fox", n + 2)
                if v == norm_visit(n):
                    act.wait_ge(sem("negc_ready"), h + 1)
                    fn(ncb, T[2], ACT.Copy).then_inc(sem("ncb_ready"), 1)
                    factors(n, "fox")
                if v == 10 + late(n):
                    act.wait_ge(sem("fox_max"), h + 1)
                    off = [0, 128, 384, 768, 1280]
                    for j in range(TT):
                        last = fn(pr[:, off[j]:off[j + 1]], pr[:, off[j]:off[j + 1]], ACT.Exp,
                                  bias=nmx[:, j:j + 1], accum_out=rsum[:, j:j + 1])
                    last.then_inc(sem("fox_exp"), 1)
                if v == turn_visit(n):
                    act.wait_ge(sem("fox_turned0"), h + 1)
                    fn(pt[:, 0:512], T[0], ACT.Copy).then_inc(sem("fox_pt0"), 1)
                    act.wait_ge(sem("fox_turned2"), h + 1)
                    fn(pt[:, 896:1280], T[2][:, 0:384], ACT.Copy).then_inc(sem("fox_pt2"), 1)

            def gdn_side(n, h, v):
                b = h % 2
                if v == 3:
                    act.wait_ge(sem("conv_step"), 12 * h + 12)
                    fn(qkv, qkv, ACT.Silu).then_inc(sem("silu_done"), 1)
                    act.wait_ge(sem("silu_done"), h + 1)
                    squares(n, "gdn", n + 2)
                    roots_table()
                if v == 6:
                    act.wait_ge(sem("dec_arg"), h + 1)
                    fn(dec, dec, ACT.Exp).then_inc(sem("decay"), 1)
                if v == 5:
                    act.wait_ge(sem("gc_rows"), h + 1)
                    if h >= 2:
                        act.wait_ge(sem("ds_ready"), NCH * (h - 1))
                    fn(sc_qg[b], T[2], ACT.Exp).then_inc(sem("qg_exp"), 1)
                    factors(n, "gdn")
                if v == 8:
                    act.wait_ge(sem("inv0_turned"), h + 1)
                    fn(inv[:, 0, :, :].rearrange("p t c -> p (t c)"), T[0][:, 0:256], ACT.Copy) \
                        .then_inc(sem("inv0_copied"), 1)
                for l in range(1, 6):
                    if v == 7 + 2 * l:
                        act.wait_ge(sem("y_ready"), 5 * h + l)
                        fn(yb.rearrange("p t c -> p (t c)"), T[1][:, 0:256], ACT.Copy).then_inc(sem("y_copied"), 1)
                if v == 19:
                    act.wait_ge(sem("u_ready"), h + 1)
                    fn(sc_u[b].rearrange("p t d -> p (t d)"), T[1], ACT.Copy).then_inc(sem("uw_taken"), 1)
                    act.wait_ge(sem("w_ready"), h + 1)
                    for a in range(2):
                        last = fn(sc_nw[b].rearrange("p (t a c) -> p a t c", t=TT, a=2)[:, a],
                                  T[2 - 2 * a][:, 0:256].rearrange("p (t c) -> p t c", t=TT), ACT.Copy, scale=-1.0)
                    last.then_inc(sem("uw_taken"), 1)
                if v == 36:
                    act.wait_ge(sem("ds_ready"), NCH * (h + 1))
                    for i in range(TT):
                        last = fn(mix[:, MIX_GDN + h, i * P:i * P + P], S2[:, i * P:i * P + P], ACT.Square,
                                  scale=q_root[:, n, i:i + 1], accum_out=oss[:, i:i + 1])
                    link(last)
                    inv_root(orn, oss, 1.0 / HD).then_inc(sem("or_ready"), 1)

            def z_side(i):
                for s in range(3):
                    if s < 2:
                        act.wait_ge(group_sums, 2 * i + s + 1)
                    else:
                        act.wait_ge(unit_done, UPG * (i + 1))
                    fn(zg[:, 3 * i + s, :], bank[s], ACT.Silu).then_inc(bank_taken[s], 1)
                roots_table()

            def mix_split(j):
                k = MIX_ORDER[j]
                act.wait_ge(unit_done, OUT_UNIT0 - UPG + k // 2 + 1)
                if k >= MIX_MEM:
                    act.wait_ge(sem("mem_mixed"), N_MEM)
                elif k >= MIX_GDN:
                    act.wait_ge(sem("gdn_mixed"), k - MIX_GDN + 1)
                else:
                    act.wait_ge(sem("fox_mixed"), k + 1)
                fn(x_hi[:, k, :], mix[:, k, :], ACT.Copy).then_inc(sem("mix_hi_done"), 1)

            for k in range(4):
                x_split(k)
            for t in range(LAST_VISIT):
                u, half = divmod(t, 2)
                if half == 0 and u < UPG:
                    for k in (2 * u + 4, 2 * u + 5):
                        if k < KD:
                            x_split(k)
                if half == 0:
                    hi_half(u + AHEAD)
                if t == 4:
                    fn(wg_hi.rearrange("p k c -> p (k c)"), A["gate_w"], ACT.Copy).then_inc(sem("gate_w_hi"), 1)
                    act.wait_ge(sem("mem_in"), 16)
                    for m in range(MT):
                        link(fn(scratch, mem_in[:, m, :], ACT.Square, accum_out=ssm[:, m:m + 1]))
                    inv_root(rm, ssm, 1.0 / D_MODEL).then_inc(sem("rm_ready"), 1)
                if t in (VPG - 1, 2 * VPG - 1):
                    z_side(t // VPG)
                g = (t + 1) // VPG - 1
                if (t + 1) % VPG == 0 and 2 <= g < N_GROUPS:
                    main_copies(g - 2, *GROUPS[g], g)
                if VPG <= t < VPG + KD // 2:
                    mem_split(t - VPG)
                if t == VPG + 11:
                    fn(coef, A["a_log"], ACT.Exp).then_inc(sem("rates"), 1)
                    act.wait_ge(sem("gate_abs"), 1)
                    link(fn(gl, gl, ACT.Exp, scale=-1.0))
                    act.wait_ge(sem("const_in"), 16)
                    fn(gl, gl, ACT.Ln, bias=K["ones"][0:NG, 0:1]).then_inc(sem("gate_ln"), 1)
                if t == VPG + 15:
                    act.wait_ge(sem("rows_zero"), 2)
                    act.wait_ge(sem("gate_sum_rows"), 1)
                    for r, src in ((GL, gl), (GC, bank[6][GC:GC + NG, :]), (NC, bank[7][NC:NC + NG, :])):
                        fn(rows_hi[r:r + NG, :], src, ACT.Copy).then_inc(sem("rows_hi_done"), 1)
                    act.wait_ge(sem("gate_sums_read"), 1)
                    gs = gsum.rearrange("p (i t h) -> p i t h", i=4, t=TT)
                    fn(kdf, gs[:, 1], ACT.Exp)
                    fn(egl, gs[:, 2:4], ACT.Exp)
                    fn(beta, ga[:, :, N_FOX + N_GDN:], ACT.Exp)
                    act.wait_ge(sem("beg_arg"), 1)
                    fn(beg, beg, ACT.Exp).then_inc(sem("gate_exps"), 1)
                for j in mix_tiles(t):
                    mix_split(j)
                for n, kind, h, v in head_visit(t):
                    {"mem": mem_side, "gdn": gdn_side, "fox": fox_side}[kind](n, h, v)
                i = t - VPG * (N_GROUPS - 1)
                if 0 <= i < 2 * TT:
                    act.wait_ge(sem("gdn_mixed"), N_GDN)
                    cols = slice((i % 2) * (D_MODEL // 2), (i % 2 + 1) * (D_MODEL // 2))
                    act.dma_start(resid[:, i // 2, cols], x.rearrange("(t p) c -> p t c", p=P)[:, i // 2, cols]) \
                        .then_inc(sem("resid_in"), 16)
            mix_split(KD - 1)

            def part_squares(cg):
                act.wait_ge(sem("mix_split"), KD)
                if cg > 0:
                    act.wait_ge(sem("part_sq"), TT * cg)
                for t in range(TT):
                    if cg == N_CG - 1 and t < TT - 1:
                        act.wait_ge(sem("last_out_added"), t + 1)
                    elif t == 0 or cg == N_CG - 1:
                        act.wait_ge(resid_added, cg + 1)
                    fn(scratch[:, 512 * t:512 * t + 512], resid[:, t, 512 * cg:512 * cg + 512], ACT.Square,
                       accum_out=ss2[:, t, cg:cg + 1]).then_inc(sem("part_sq"), 1)

            for u in range(LAST_VISIT // 2, FFN_UNIT0):
                hi_half(u + AHEAD)
                cg, kk = divmod(u - OUT_UNIT0, UPG)
                if kk == 3 and cg > 0:
                    part_squares(cg - 1)
            part_squares(N_CG - 1)
            act.wait_ge(sem("ss2_sum"), 1)
            inv_root(r2, ss2s, 1.0 / D_MODEL).then_inc(sem("r2_ready"), TT)
            copy_root(2)

            def h_split(k):
                act.wait_ge(sem("h_scaled"), k + 1)
                fn(x_hi[:, k, :], scaled[:, k % 2, :], ACT.Copy).then_inc(sem("h_hi_done"), 1)

            def ffn_hi(u, jj, landed):
                act.wait_ge(unit_done, u - SPL + 1)
                act.wait_ge(raw_ready[ffn_slot(jj, RAW)], landed)
                sr, ss = 1024 * ffn_slot(jj, RAW), 1024 * ffn_slot(jj, SPL)
                fn(w_hi[:, ss:ss + 1024], w_raw[:, sr:sr + 1024], ACT.Copy).then_inc(hi_done, 1)

            def take_gate(done, taken):
                act.wait_ge(unit_done, done)
                if taken is not None:
                    act.wait_ge(sem("act_ready"), taken)
                fn(silu_gate[:, :], set_a, ACT.Silu).then_inc(sem("gate_taken"), 1)

            def act_hi_half(chunks):
                act.wait_ge(sem("up_taken"), chunks)
                fn(act_hi.rearrange("p f t -> p (f t)"), silu_gate[:, :], ACT.Copy).then_inc(sem("act_hi_done"), 1)

            for k in range(4):
                h_split(k)
            for j in range(2 * UPG):
                for k in (2 * j + 4, 2 * j + 5):
                    if k < KD:
                        h_split(k)
                ffn_hi(FFN_UNIT0 + j + AHEAD, j + AHEAD, ffn_raw_at(j + AHEAD))
                if j == UPG:
                    take_gate(FFN_UNIT0 + UPG, None)
            with act.Fori(1, N_CHUNKS) as c:
                u0 = FFN_UNIT0 + c * UPC - UPG
                for j in range(UPC):
                    jj = LOOP_J + j + AHEAD
                    ffn_hi(u0 + j + AHEAD, jj, c * (16 * UPC // RAW) + (ffn_raw_at(jj) - 16 * UPC // RAW))
                    if j == 0:
                        act_hi_half(c)
                    if j == UPG:
                        take_gate(u0 + UPG, c)
            u0 = FFN_UNIT0 + N_CHUNKS * UPC - UPG
            for j in range(UPG):
                if j == 0:
                    for f in range(4):
                        act.wait_ge(sem("up_taken"), N_CHUNKS + f)
                        fn(act_hi[:, f, :], silu_gate[:, f * SEQ:f * SEQ + SEQ], ACT.Copy).then_inc(sem("act_hi_done"), 1)
                if j + AHEAD < UPG:
                    jj = UPC * (N_CHUNKS - 1) + LOOP_J + j + AHEAD
                    ffn_hi(u0 + j + AHEAD, jj, ffn_raw_at(jj))

        @block.vector
        def _(dve):
            tt, ts, stt, copy = (nc.vector.tensor_tensor, nc.vector.tensor_scalar, nc.vector.scalar_tensor_tensor,
                                 nc.vector.tensor_copy)
            chain = [0]

            def link(ins):
                chain[0] += 1
                ins.then_inc(sem("dve_chain"), 1)
                dve.wait_ge(sem("dve_chain"), chain[0])

            def lo_half(u):
                dve.wait_ge(hi_done, u + 1)
                n, sr, ss = unit_cols(u), (u % RAW) * 1024, (u % SPL) * 1024
                tt(w_lo[:, ss:ss + n], w_raw[:, sr:sr + n], w_hi[:, ss:ss + n].bitcast(F32), ALU.subtract) \
                    .then_inc(lo_done, 1)

            def norm_step(k, name, bank_of, gain):
                if k + 1 < KD:
                    dve.wait_ge(sem(name + "_turned"), k + 2)
                    if k > 0:
                        dve.wait_ge(sem(name + "_split"), k)
                    stt(scaled[:, (k + 1) % 2, :], bank_of(k + 1), gain[:, k + 1:k + 2], r_row, ALU.mult, ALU.mult) \
                        .then_inc(sem(name + "_scaled"), 1)
                if k >= 0:
                    dve.wait_ge(sem(name + "_hi_done"), k + 1)
                    tt(x_lo[:, k, :], scaled[:, k % 2, :], x_hi[:, k, :].bitcast(F32), ALU.subtract) \
                        .then_inc(sem(name + "_split"), 1)

            def x_split(k):
                norm_step(k, "x", x_bank, A["norm_mix"])

            def mem_split(j):
                for k in (2 * j, 2 * j + 1):
                    dve.wait_ge(sem("mem_hi_done"), 2 * j + 2)
                    stt(um_lo[:, k, :], bank[3 + j % 5][:, (k % 2) * 256:(k % 2) * 256 + 256],
                        A["mem_norm"][:, k:k + 1], um_hi[:, k, :].bitcast(F32), ALU.mult, ALU.subtract) \
                        .then_inc(sem("mem_split"), 1)

            def take_v(n, kind, h):
                dve.wait_ge(unit_done, UPG * (n + 3))
                if kind == "gdn":
                    dve.wait_ge(sem("pads_zero"), h + 1)
                    copy(cin[:, 2, 3:], bank[2]).then_inc(bank_taken[2], 1)
                    return
                qkv_free(dve, n)
                w = MEM_LEN if kind == "mem" else SEQ
                copy(qkv[:, 2, 0:w], bank[2][:, 0:w]).then_inc(bank_taken[2], 1)

            def refine(y, w, a, addend, factor):
                link(stt(w, a, addend, y, ALU.add, ALU.mult))
                link(stt(w, w, -0.5 * factor, y, ALU.mult, ALU.mult))
                return stt(y, w, 1.5, y, ALU.add, ALU.mult)

            def refine_roots(n, kind):
                dve.wait_ge(sem("rn_ready"), n + 1)
                if kind == "fox":
                    last = refine(sq.rearrange("p s t -> p (s t)"), tmp[:, 0:2 * SEQ], psum[:, 2048:2048 + 2 * SEQ],
                                  EPS * HD, 1.0 / HD)
                else:
                    refine(q_root[:, n, :], r_work, T[0][:, 0:TT], EPS * HD, 1.0 / HD).then_inc(sem("qn_ready"), 1)
                    last = refine(sq[:, 1, 0:MEM_LEN], tmp[:, 0:MEM_LEN], T[1][:, 0:MEM_LEN], EPS * HD, 1.0 / HD)
                last.then_inc(sem("roots_refined"), 1)
                dve.wait_ge(sem("roots_refined"), roots(n) + 1)

            def scaled_k(n):
                stt(qkv[:, 1, 0:MEM_LEN], qkv[:, 1, 0:MEM_LEN], comb[:, 0:1], sq[:, 1, 0:MEM_LEN], ALU.mult, ALU.mult) \
                    .then_inc(sem("kn_ready"), 1)

            def scaled_q(n):
                stt(qkv[:, 0, :], qkv[:, 0, :], comb[:, 1:2], sq[:, 0, :], ALU.mult, ALU.mult).then_inc(sem("qn_ready"), 1)

            def scaled_q_root(n):
                dve.wait_ge(sem("rn_ready"), n + 1)
                ts(q_root[:, n, :], q_root[:, n, :], SCALE, None, ALU.mult).then_inc(sem("qn_ready"), 1)

            def scale_probs(kind, h, cuts):
                dve.wait_ge(sem(kind + "_exp"), h + 1)
                link(nc.vector.reciprocal(rrec, rsum))
                for j in range(TT):
                    last = ts(pr[:, cuts[j]:cuts[j + 1]], pr[:, cuts[j]:cuts[j + 1]], rrec[:, j:j + 1], None, ALU.mult)
                last.then_inc(sem(kind + "_probs"), 1)

            def mem_side(n, h, v):
                if v == norm_visit(n) + 1:
                    refine_roots(n, "mem")
                    scaled_k(n)
                if v == 7:
                    dve.wait_ge(sem("tok_ready"), n + 1)
                    copy(vtok[:, 0:MT, :].rearrange("p t d -> p (t d)"), T[2][:, 0:MEM_LEN]).then_inc(sem("vtok_ready"), 1)
                if v in (8, 9):
                    i = v - 8
                    dve.wait_ge(sem("mem_scores"), 2 * h + i + 1)
                    last = nc.vector.tensor_reduce(mx[:, 2 * i:2 * i + 2], T[i].rearrange("p (j c) -> p j c", j=2),
                                                   AX.X, ALU.max)
                    if v == 9:
                        link(last)
                        stt(nmx, mx, -1.0, q_root[:, n, :], ALU.mult, ALU.mult).then_inc(sem("mem_max"), 1)
                if v == 11:
                    scale_probs("mem", h, [256 * j for j in range(TT + 1)])
                if v == turn_visit(n):
                    dve.wait_ge(sem("mem_turned_p"), 2 * h + 2)
                    copy(pt[:, 512:1024], T[1]).then_inc(sem("mem_pt1"), 1)
                if v == turn_visit(n) + 1:
                    dve.wait_ge(sem("mem_pv"), h + 1)
                    copy(mix[:, MIX_MEM + h, :], T[2]).then_inc(sem("mem_mixed"), 1)

            def fox_side(n, h, v):
                if v == norm_visit(n) + 1:
                    refine_roots(n, "fox")
                    scaled_q(n)
                if v == 7:
                    dve.wait_ge(sem("tok_ready"), n + 1)
                    copy(vtok.rearrange("p t d -> p (t d)"), T[2]).then_inc(sem("vtok_ready"), 1)
                off = [0, 128, 384, 768, 1280]
                vs = v - late(n)
                if vs in (8, 9, 10):
                    if vs == 8:
                        dve.wait_ge(sem("ncb_ready"), h + 1)
                    dve.wait_ge(sem("fox_scores"), 3 * h + vs - 7)
                    for j, b, c0 in {8: ((0, 0, 0), (1, 0, 128)), 9: ((2, 1, 0),), 10: ((3, 2, 0),)}[vs]:
                        w = (j + 1) * P
                        last = nc.vector.tensor_tensor_reduce(pr[:, off[j]:off[j + 1]], T[b][:, c0:c0 + w], ncb[:, 0:w],
                                                              1.0, -3e38, ALU.add, ALU.max, mx[:, j:j + 1])
                    if vs == 10:
                        link(last)
                        ts(nmx, mx, -1.0, None, ALU.mult).then_inc(sem("fox_max"), 1)
                if vs == 11:
                    scale_probs("fox", h, off)
                if v == turn_visit(n):
                    dve.wait_ge(sem("fox_turned1"), h + 1)
                    copy(pt[:, 512:896], T[1][:, 0:384]).then_inc(sem("fox_pt1"), 1)
                if v == turn_visit(n) + 1:
                    dve.wait_ge(sem("fox_pv"), h + 1)
                    copy(mix[:, MIX_FOX + h, :], T[2]).then_inc(sem("fox_mixed"), 1)

            def conv(n, h, v):
                if v == 0:
                    banks_taken(dve, n + 3)
                    qkv_free(dve, n)
                for step in range(4 * v, 4 * v + 4):
                    j, s = divmod(step, 3)
                    w, src = conv_w[:, s, h, j:j + 1], cin[:, s, j:j + SEQ]
                    if j == 0:
                        ins = ts(qkv[:, s, :], src, w, None, ALU.mult)
                    else:
                        dve.wait_ge(sem("conv_step"), 12 * h + step - 2)
                        ins = stt(qkv[:, s, :], src, w, qkv[:, s, :], ALU.mult, ALU.add)
                    ins.then_inc(sem("conv_step"), 1)

            def decay_arg(w, h):
                rows_ = T[2].rearrange("p (t a c) -> p t a c", t=TT, a=2)
                for a in range(2):
                    s = slice(64 * a, 64 * a + 64)
                    last = tt(dec[s, w], rows_[s, :, a], bcl(ngc[s, :, h], CHUNK), ALU.add)
                return last

            def gdn_side(n, h, v):
                b = h % 2
                hc = slice(h, h + 1)
                if v in (0, 1, 2):
                    conv(n, h, v)
                if v == 5:
                    dve.wait_ge(sem("qg_exp"), h + 1)
                    if h == 0:
                        dve.wait_ge(sem("gate_exps"), 1)
                    decay_arg(0, h).then_inc(sem("gc_taken"), 1)
                    scaled_q_root(n)
                if v == 6:
                    dve.wait_ge(sem("gcb_rows"), h + 1)
                    link(decay_arg(1, h))
                    dve.wait_ge(sem("gc_taken"), h + 1)
                    d8 = dec.rearrange("p w t c -> p (w t) c")
                    tt(d8, d8, K["neg64"].unsqueeze(1).to_broadcast([P, 2 * TT, CHUNK]), ALU.add) \
                        .then_inc(sem("dec_arg"), 1)
                if v == 7:
                    i64 = K["ident64"].unsqueeze(1).to_broadcast([P, TT, CHUNK])
                    pair0 = K["pair0"].unsqueeze(1).to_broadcast([P, TT, CHUNK])
                    dve.wait_ge(sem("gram_ready"), h + 1)
                    dve.wait_ge(sem("decay"), h + 1)
                    if h > 0:
                        dve.wait_ge(sem("coup_ready"), 5 * h)
                    if h >= 2:
                        dve.wait_ge(sem("ds_ready"), NCH * (h - 1))
                    t0 = T[0].rearrange("p (w t c) -> p w t c", w=2, t=TT)
                    tt(lt, t0[:, 0], dec[:, 1], ALU.mult).then_inc(sem("lt_ready"), 1)
                    tt(sc_at[b], t0[:, 1], dec[:, 0], ALU.mult)
                    dve.wait_ge(sem("lt_ready"), h + 1)
                    link(tt(inv[:, 1], lt, pair0, ALU.mult))
                    tt(inv[:, 1], i64, inv[:, 1], ALU.subtract).then_inc(sem("inv0_ready"), 1)
                    dve.wait_ge(sem("ktok_ready"), h + 1)
                    k3 = T[1].rearrange("p (t d) -> p t d", t=TT)
                    tt(kbg, k3, bcl(beg[:, :, h], HD), ALU.mult)
                    tt(sc_kd[b], k3, bcl(kdf[:, :, h], HD), ALU.mult).then_inc(sem("k_scaled"), 1)
                    dve.wait_ge(sem("tok_ready"), n + 1)
                    tt(vb, T[2].rearrange("p (t d) -> p t d", t=TT), bcl(beta[:, :, h], HD), ALU.mult) \
                        .then_inc(sem("v_scaled"), 1)
                for l in range(1, 6):
                    if v == 8 + 2 * l:
                        dve.wait_ge(sem("xy_ready"), 5 * h + l)
                        if l == 1:
                            dve.wait_ge(sem("inv0_copied"), h + 1)
                        for w in (0, 1) if l < 5 else (1,):
                            x_w = part(inv[:, w], l, bool(w))
                            xy = T[0][:, 256 * w:256 * w + 128].rearrange("p (t g c) -> p t g c", t=TT, c=1 << l)
                            last = tt(x_w, x_w, xy, ALU.subtract)
                        last.then_inc(sem("inv_updated"), 1)
                if 21 <= v < 21 + 2 * NCH:
                    c, second = divmod(v - 21, 2)
                    i, s = c // 2, slice(64 * (c % 2), 64 * (c % 2) + 64)
                    if not second:
                        dve.wait_ge(sem("ws_ready"), NCH * h + c + 1)
                        tt(v_new[s, :], sc_u[b][s, i, :], S1[s, 0:P], ALU.add).then_inc(sem("v_new"), 1)
                    else:
                        dve.wait_ge(sem("ds_ready"), NCH * h + c + 1)
                        if c < NCH - 1:
                            stt(state, state, egl[:, c % 2, i, hc], S1[:, P:2 * P], ALU.mult, ALU.add) \
                                .then_inc(sem("state_new"), 1)
                        else:
                            nc.vector.memset(state, 0.0).then_inc(sem("state_clear"), 1)
                if v == 37:
                    dve.wait_ge(sem("or_ready"), h + 1)
                    link(tt(orn, orn, q_root[:, n, :], ALU.mult))
                    tt(mix[:, MIX_GDN + h, :].rearrange("p (t d) -> p t d", t=TT),
                       S2.rearrange("p (t d) -> p t d", t=TT), bcl(orn, HD), ALU.mult).then_inc(sem("o_scaled"), 1)
                if v == 52:
                    dve.wait_ge(sem("o_turned"), h + 1)
                    dve.wait_ge(sem("zg_ready"), 2)
                    tt(mix[:, MIX_GDN + h, :], T[0], zg[:, h, :], ALU.mult).then_inc(sem("gdn_mixed"), 1)

            def mix_split(j):
                k = MIX_ORDER[j]
                dve.wait_ge(sem("mix_hi_done"), j + 1)
                tt(x_lo[:, k, :], mix[:, k, :], x_hi[:, k, :].bitcast(F32), ALU.subtract).then_inc(sem("mix_split"), 1)

            def out_add(cg):
                dve.wait_ge(unit_done, OUT_UNIT0 + UPG * (cg + 1))
                dve.wait_ge(sem("resid_in"), 16 * 2 * TT)
                r = resid[:, :, 512 * cg:512 * cg + 512]
                tt(r, (set_a, set_b)[cg % 2].rearrange("p (t c) -> p t c", t=TT), r, ALU.add).then_inc(resid_added, 1)

            def out_add_last():
                for t in range(TT):
                    if t < TT - 1:
                        dve.wait_ge(sem("last_out_sums"), t + 1)
                    else:
                        dve.wait_ge(unit_done, FFN_UNIT0)
                    r = resid[:, t, 512 * (N_CG - 1):]
                    tt(r, bank[4 * ((N_CG - 1) % 2) + t], r, ALU.add) \
                        .then_inc(sem("last_out_added") if t < TT - 1 else resid_added, 1)

            def diagonals(r, ss, count, step):
                for t0 in range(0, TT, step):
                    ts_ = slice(t0, t0 + step)
                    dve.wait_ge(sem(count), t0 + step)
                    link(refine(r[:, ts_], r_work[:, ts_], ss[:, ts_], EPS * D_MODEL, 1.0 / D_MODEL))
                    for t in range(t0, t0 + step):
                        ts(diag[:, t, :], K["ident"], r[:, t:t + 1], None, ALU.mult).then_inc(sem("diag_ready"), 1)

            dve.wait_ge(sem("ident_in"), 16)
            dve.wait_ge(sem("par_in"), 16)
            stt(comb[:, 0:1], A["mem_q"], SCALE, A["mem_k"], ALU.mult, ALU.mult)
            stt(comb[:, 1:2], A["fox_q"], SCALE, A["fox_k"], ALU.mult, ALU.mult).then_inc(sem("comb_ready"), 1)
            dve.wait_ge(sem("comb_ready"), 1)
            diagonals(rx, ssx, "rx_ready", 1)
            lo_half(0)
            lo_half(1)
            dve.wait_ge(sem("root_copied"), 1)
            for k in range(-1, 4):
                x_split(k)
            for t in range(LAST_VISIT):
                u, half = divmod(t, 2)
                if half == 0 and u < UPG:
                    for k in (2 * u + 4, 2 * u + 5):
                        if k < KD:
                            x_split(k)
                for n, kind, h, v in head_visit(t):
                    if v == 0:
                        take_v(n, kind, h)
                if half == 1:
                    lo_half(u + AHEAD)
                if t == 5:
                    dve.wait_ge(sem("const_in"), 16)
                    copy(identb[:, :], K["ident"]).then_inc(sem("bf_consts"), 1)
                    copy(causalb[:, :], K["causal"]).then_inc(sem("bf_consts"), 1)
                    dve.wait_ge(sem("gate_w_hi"), 1)
                    tt(wg_lo.rearrange("p k c -> p (k c)"), A["gate_w"],
                       wg_hi.rearrange("p k c -> p (k c)").bitcast(F32), ALU.subtract).then_inc(sem("gate_w_split"), 1)
                    dve.wait_ge(sem("rm_ready"), 1)
                    for m in range(MT):
                        ts(mem_in[:, m, :], mem_in[:, m, :], rm[:, m:m + 1], None, ALU.mult).then_inc(sem("mem_normed"), 1)
                if VPG <= t < VPG + KD // 2:
                    mem_split(t - VPG)
                if t == VPG + 11:
                    dve.wait_ge(sem("gates_ready"), 1)
                    link(ts(gz, bank[3][0:NG, :], A["gate_bias"][0:NG], A["gate_sign"][0:NG], ALU.add, ALU.mult))
                    stt(gl, gz, -1.0, gz, ALU.mult, ALU.max).then_inc(sem("gate_abs"), 1)
                    dve.wait_ge(sem("rates"), 1)
                    link(ts(coef, coef, -1.0, None, ALU.mult))
                    dve.wait_ge(sem("gate_ln"), 1)
                    link(stt(gl, gz, 0.0, gl, ALU.max, ALU.add))
                    ts(gl, gl, coef[0:NG, :], None, ALU.mult).then_inc(sem("gate_logs"), 1)
                if t == VPG + 13:
                    dve.wait_ge(sem("gates_turned"), 1)
                    copy(ga.rearrange("p t c -> p (t c)"), bank[4][:, 0:TT * NG]).then_inc(sem("gates_by_token"), 1)
                if t == VPG + 15:
                    for i, (r, src) in enumerate(((GL, gl), (GC, bank[6][GC:GC + NG, :]), (NC, bank[7][NC:NC + NG, :]))):
                        dve.wait_ge(sem("rows_hi_done"), i + 1)
                        tt(rows_lo[r:r + NG, :], src, rows_hi[r:r + NG, :].bitcast(F32), ALU.subtract) \
                            .then_inc(sem("rows_lo_done"), 1)
                    dve.wait_ge(sem("gate_sums"), 1)
                    copy(gsum, bank[5][:, 0:4 * n4]).then_inc(sem("gate_sums_read"), 1)
                    dve.wait_ge(sem("gate_sums_read"), 1)
                    gc = gsum[:, 0:n4].rearrange("p (t h) -> p t h", t=TT)
                    tt(beg, gc, ga[:, :, N_FOX + N_GDN:], ALU.add).then_inc(sem("beg_arg"), 1)
                    ts(ngc, gc, -1.0, None, ALU.mult).then_inc(sem("ngc_ready"), 1)
                    nc.vector.memset(state, 0.0).then_inc(sem("state_clear"), 1)
                    dve.wait_ge(sem("ngc_ready"), 1)
                for j in mix_tiles(t):
                    mix_split(j)
                for n, kind, h, v in head_visit(t):
                    {"mem": mem_side, "gdn": gdn_side, "fox": fox_side}[kind](n, h, v)
            mix_split(KD - 1)
            for u in range(LAST_VISIT // 2, FFN_UNIT0):
                lo_half(u + AHEAD)
                cg, kk = divmod(u - OUT_UNIT0, UPG)
                if kk == 0:
                    out_add(cg - 1)
            out_add_last()
            dve.wait_ge(sem("part_sq"), TT * N_CG)
            nc.vector.tensor_reduce(ss2s, ss2, AX.X, ALU.add).then_inc(sem("ss2_sum"), 1)
            diagonals(r2, ss2s, "r2_ready", TT)

            def h_split(k):
                norm_step(k, "h", h_bank, A["norm_ffn"])

            def ffn_lo(u, jj):
                dve.wait_ge(hi_done, u + 1)
                sr, ss = 1024 * ffn_slot(jj, RAW), 1024 * ffn_slot(jj, SPL)
                tt(w_lo[:, ss:ss + 1024], w_raw[:, sr:sr + 1024], w_hi[:, ss:ss + 1024].bitcast(F32), ALU.subtract) \
                    .then_inc(lo_done, 1)

            def take_up(done, chunks):
                dve.wait_ge(unit_done, done)
                dve.wait_ge(sem("gate_taken"), chunks)
                tt(silu_gate[:, :], set_b, silu_gate[:, :], ALU.mult).then_inc(sem("up_taken"), 1)

            def act_lo_half(chunks):
                dve.wait_ge(sem("act_hi_done"), chunks)
                tt(act_lo.rearrange("p f t -> p (f t)"), silu_gate[:, :],
                   act_hi.rearrange("p f t -> p (f t)").bitcast(F32), ALU.subtract).then_inc(sem("act_ready"), 1)

            def down_add(done, before, cg, side):
                dve.wait_ge(unit_done, done)
                dve.wait_ge(resid_added, before)
                r = resid[:, :, 512 * cg:512 * cg + 512]
                tt(r, (set_a, set_b)[side].rearrange("p (t c) -> p t c", t=TT), r, ALU.add).then_inc(resid_added, 1)

            dve.wait_ge(sem("root_copied"), 2)
            for k in range(-1, 4):
                h_split(k)
            for j in range(2 * UPG):
                for k in (2 * j + 4, 2 * j + 5):
                    if k < KD:
                        h_split(k)
                ffn_lo(FFN_UNIT0 + j + AHEAD, j + AHEAD)
            with dve.Fori(1, N_CHUNKS) as c:
                u0 = FFN_UNIT0 + c * UPC - UPG
                for j in range(UPC):
                    ffn_lo(u0 + j + AHEAD, LOOP_J + j + AHEAD)
                    if j == 0:
                        take_up(u0, c)
                    if j == 1:
                        act_lo_half(c)
                    if j in (10, 12, 14, 16):
                        cg = (j - 10) // 2
                        down_add(u0 + j, c * N_CG + cg, cg, 1 - cg % 2)
            u0 = FFN_UNIT0 + N_CHUNKS * UPC - UPG
            for j in range(UPG + 1):
                if j == 0:
                    dve.wait_ge(unit_done, u0)
                    dve.wait_ge(sem("gate_taken"), N_CHUNKS)
                    for f in range(5):
                        g, up = silu_gate[:, :], set_b
                        if f < 4:
                            cols = slice(f * SEQ, f * SEQ + SEQ)
                            tt(g[:, cols], up[:, cols], g[:, cols], ALU.mult).then_inc(sem("up_taken"), 1)
                        if f > 0:
                            dve.wait_ge(sem("act_hi_done"), N_CHUNKS + f - 1)
                            tt(act_lo[:, f - 1, :], g[:, (f - 1) * SEQ:f * SEQ], act_hi[:, f - 1, :].bitcast(F32),
                               ALU.subtract).then_inc(sem("act_ready"), 1)
                if j + AHEAD < UPG:
                    ffn_lo(u0 + j + AHEAD, LOOP_J + j + AHEAD)
                if 2 <= j < UPG and j % 2 == 0:
                    cg = j // 2 - 1
                    down_add(u0 + j, N_CHUNKS * N_CG + cg, cg, cg % 2)
            for t in range(TT):
                if t < TT - 1:
                    dve.wait_ge(sem("tail_sums"), t + 1)
                else:
                    dve.wait_ge(unit_done, u0 + UPG)
                r = resid[:, t, 512 * (N_CG - 1):]
                tt(r, bank[4 + t], r, ALU.add).then_inc(sem("tail_added"), 1)

        @block.gpsimd
        def _(pool):
            tt, copy = nc.gpsimd.tensor_tensor, nc.gpsimd.tensor_copy

            def norm_k(n, kind):
                if kind == "gdn":
                    pool.wait_ge(sem("rn_ready"), n + 1)
                else:
                    pool.wait_ge(sem("roots_refined"), roots(n) + 1)
                tt(qkv[:, 1, :], qkv[:, 1, :], sq[:, 1, :], ALU.mult).then_inc(sem("kn_ready"), 1)

            def fox_side(n, h, v):
                if v == 0:
                    pool.wait_ge(sem("gcb_rows"), N_GDN)
                    if h > 0:
                        pool.wait_ge(sem("negc_ready"), h)
                    copy(pick[:, 0, :], ident_col(NC + h)).then_inc(sem("picks_ready"), 1)
                if v == norm_visit(n):
                    norm_k(n, "fox")

            def gdn_side(n, h, v):
                b = h % 2
                if v == 0:
                    pool.wait_ge(sem("qn_ready"), n)
                    pool.wait_ge(sem("kn_ready"), n)
                    nc.gpsimd.memset(cin[:, :, 0:TAPS - 1], 0.0).then_inc(sem("pads_zero"), 1)
                    if h > 0:
                        pool.wait_ge(sem("gcb_rows"), h)
                    copy(pick[:, 0, :], ident_col(GC + N_FOX + h)).then_inc(sem("picks_ready"), 1)
                    tt(pick[:, 1, :], ident_col(GC + N_FOX + h), ident_col(GL + N_FOX + N_GDN + h), ALU.add) \
                        .then_inc(sem("picks_ready"), 1)
                if v == 5:
                    norm_k(n, "gdn")
                if v == 6:
                    pool.wait_ge(sem("qn_ready"), n + 1)
                    pool.wait_ge(sem("qg_exp"), h + 1)
                    tt(sc_qg[b], sc_qg[b], qkv[:, 0, :], ALU.mult).then_inc(sem("qg_ready"), 1)
                if v == 7:
                    pool.wait_ge(sem("lt_ready"), h + 1)
                    if h > 0:
                        pool.wait_ge(sem("y_ready"), 5 * h)
                    for l in range(1, 6):
                        tt(coup[:, l - 1], lt, K[f"pair{l}"].unsqueeze(1).to_broadcast([P, TT, CHUNK]), ALU.mult) \
                            .then_inc(sem("coup_ready"), 1)

            def ident_col(r):
                return K["ident"][:, r:r + 1].to_broadcast([P, P])

            nc.gpsimd.memset(rows_hi[:, :].bitcast(F32), 0.0).then_inc(sem("rows_zero"), 1)
            nc.gpsimd.memset(rows_lo[:, :].bitcast(F32), 0.0).then_inc(sem("rows_zero"), 1)
            pool.wait_ge(sem("par_in"), 16)
            pool.wait_ge(sem("const_in"), 16)
            for t in range(LAST_VISIT):
                if t in (VPG, 2 * VPG):
                    i = t // VPG - 1
                    banks_taken(pool, i + 1)
                    z = zg[:, 3 * i:3 * i + 3, :]
                    nc.gpsimd.tensor_scalar(z, z, A["gdn_out"], 1.0, ALU.mult, ALU.mult).then_inc(sem("zg_ready"), 1)
                for n, kind, h, v in head_visit(t):
                    if kind != "mem":
                        {"gdn": gdn_side, "fox": fox_side}[kind](n, h, v)



def kernel(x, mem, norm_mix, w_in, fox_f_bias, fox_q_norm, fox_k_norm, gdn_conv, gdn_a_log, gdn_dt_bias,
           gdn_out_norm, mem_norm, w_mem_kv, mem_q_norm, mem_k_norm, w_out, norm_ffn, w_gate_up, w_down):
    import concourse.bacc as bacc
    from concourse.bass_utils import run_bass_kernel_spmd

    a = {n: np.ascontiguousarray(np.asarray(v)[0]) for n, v in
         dict(x=x, mem=mem, w_in=w_in, w_mem_kv=w_mem_kv, w_out=w_out, w_gate_up=w_gate_up, w_down=w_down).items()}
    tiles = lambda v: np.asarray(v)[0].reshape(-1, P).T
    rows = lambda *v: np.concatenate(v + (np.zeros(P - NG, np.float32),)).reshape(P, 1)
    zeros, ones = np.zeros(N_GDN, np.float32), np.ones(N_GDN, np.float32)
    gate_cols = np.concatenate([a["w_in"][:, C_FF:C_FF + N_FOX], a["w_in"][:, C_GA:C_GA + 2 * N_GDN]], 1)
    parts = dict(
        norm_mix=tiles(norm_mix), mem_norm=tiles(mem_norm), norm_ffn=tiles(norm_ffn),
        conv=np.asarray(gdn_conv)[0].reshape(TAPS, 3 * N_GDN, P).transpose(2, 1, 0).reshape(P, -1),
        fox_q=tiles(fox_q_norm), fox_k=tiles(fox_k_norm), mem_q=tiles(mem_q_norm), mem_k=tiles(mem_k_norm),
        gdn_out=tiles(gdn_out_norm),
        gate_bias=rows(np.asarray(fox_f_bias)[0], np.asarray(gdn_dt_bias)[0], zeros),
        gate_sign=rows(-ones, ones, -ones),
        a_log=rows(zeros, np.asarray(gdn_a_log)[0], zeros),
        gate_w=gate_cols.reshape(KD, P, NG).transpose(1, 0, 2).reshape(P, -1))
    a["const"] = CONST_ARRAY
    a["par"] = np.ascontiguousarray(np.concatenate([parts[n] for n in PAR], 1))
    nc = bacc.Bacc("TRN2", target_bir_lowering=False, num_devices=1)
    args = [nc.dram_tensor(f"in_{n}", v.shape, mybir.dt.from_np(v.dtype), kind="ExternalInput").ap()
            for n, v in a.items()]
    out = nc.dram_tensor("out", (SEQ, D_MODEL), F32, kind="ExternalOutput").ap()
    build(nc, *args, out)
    r = run_bass_kernel_spmd(nc, [{f"in_{n}": v for n, v in a.items()}], core_ids=[0])
    return r.results[0]["out"].reshape(1, SEQ, D_MODEL)
```
